# Optimizing a Trainium2 kernel written in Bass

```python
import math
import jax, jax.numpy as jnp
from jax import lax
import numpy as np
import jax
import jax.numpy as jnp

D_MODEL = 1024
BATCH = 1
SEQ = 1024
DEPTH = 1

N_META = 16
SSM_WIDTH = D_MODEL // 2
SSM_GROUP = 16
SSM_GROUPS = SSM_WIDTH // SSM_GROUP
SSM_STATE = 64
MLSTM_WIDTH = D_MODEL // 2
MLSTM_HEADS = 4
MLSTM_HEAD_DIM = MLSTM_WIDTH // MLSTM_HEADS
MLSTM_CHUNK = 64
QK_CONV = 4
FFN_DIM = 2816
FFN_CONV = 3
NORM_EPS = 1e-6
PAD_LOG_INPUT_GATE = -1e4
IN_WIDTHS = (SSM_WIDTH, MLSTM_WIDTH, MLSTM_WIDTH, MLSTM_WIDTH, MLSTM_WIDTH, MLSTM_HEADS, MLSTM_HEADS, D_MODEL, D_MODEL)
IN_SPLITS = tuple(int(s) for s in np.cumsum(IN_WIDTHS)[:-1])
N_IN = int(sum(IN_WIDTHS))


def rmsnorm(x, g):
    xf = x.astype(jnp.float32)
    y = xf * lax.rsqrt(jnp.mean(xf * xf, axis=-1, keepdims=True) + NORM_EPS)
    return (y * g.astype(jnp.float32)).astype(x.dtype)

def causal_dwconv(x, w, b):
    k = w.shape[0]
    y = lax.conv_general_dilated(x, w[:, None, :].astype(x.dtype), (1,), [(k - 1, 0)],
                                 dimension_numbers=('NWC', 'WIO', 'NWC'),
                                 feature_group_count=x.shape[-1])
    return y + b.astype(x.dtype)

def _complex_affine_combine(e1, e2):
    a1r, a1i, b1r, b1i = e1
    a2r, a2i, b2r, b2i = e2
    return (a2r * a1r - a2i * a1i,
            a2r * a1i + a2i * a1r,
            a2r * b1r - a2i * b1i + b2r,
            a2r * b1i + a2i * b1r + b2i)

def s5_ssm(u, lam_re, lam_im, b_re, b_im, c_re, c_im, d, log_dt):
    bsz, L, _ = u.shape
    u = u.astype(jnp.float32).reshape(bsz, L, SSM_GROUPS, SSM_GROUP)
    lam_re = lam_re.astype(jnp.float32)
    lam_im = lam_im.astype(jnp.float32)
    dt = jnp.exp(log_dt.astype(jnp.float32))[:, None]
    mag = jnp.exp(lam_re * dt)
    ab_re = mag * jnp.cos(lam_im * dt)
    ab_im = mag * jnp.sin(lam_im * dt)
    nr, ni = ab_re - 1.0, ab_im
    den = lam_re * lam_re + lam_im * lam_im
    z_re = (nr * lam_re + ni * lam_im) / den
    z_im = (ni * lam_re - nr * lam_im) / den
    b_re = b_re.astype(jnp.float32)
    b_im = b_im.astype(jnp.float32)
    bb_re = z_re[..., None] * b_re - z_im[..., None] * b_im
    bb_im = z_re[..., None] * b_im + z_im[..., None] * b_re
    bu_re = jnp.einsum('blgh,gph->blgp', u, bb_re)
    bu_im = jnp.einsum('blgh,gph->blgp', u, bb_im)
    a_re = jnp.broadcast_to(ab_re, bu_re.shape)
    a_im = jnp.broadcast_to(ab_im, bu_im.shape)
    _, _, x_re, x_im = lax.associative_scan(_complex_affine_combine, (a_re, a_im, bu_re, bu_im), axis=1)
    y = (jnp.einsum('blgp,ghp->blgh', x_re, c_re.astype(jnp.float32))
         - jnp.einsum('blgp,ghp->blgh', x_im, c_im.astype(jnp.float32))
         + d.astype(jnp.float32) * u)
    return y.reshape(bsz, L, SSM_WIDTH)

def mlstm_chunkwise(q, k, v, log_i, log_f):
    bsz, lp, nh, dh = q.shape
    nc = lp // MLSTM_CHUNK

    def to_chunks(t):
        return jnp.moveaxis(t.reshape(bsz, nc, MLSTM_CHUNK, nh, -1), 3, 1)

    q, k, v = to_chunks(q), to_chunks(k), to_chunks(v)
    log_i = to_chunks(log_i[..., None])[..., 0]
    log_f = to_chunks(log_f[..., None])[..., 0]
    b = jnp.cumsum(log_f, axis=-1)
    g = b[..., -1]
    causal = jnp.tril(jnp.ones((MLSTM_CHUNK, MLSTM_CHUNK), dtype=bool))
    log_d = jnp.where(causal, b[..., :, None] - b[..., None, :] + log_i[..., None, :], -jnp.inf)
    a = g[..., None] - b + log_i

    def step(carry, xs):
        c_st, n_st, m_st = carry
        k_c, v_c, a_c, g_c = xs
        m_new = jnp.maximum(g_c + m_st, jnp.max(a_c, axis=-1))
        decay = jnp.exp(g_c + m_st - m_new)
        w = jnp.exp(a_c - m_new[..., None])
        c_new = decay[..., None, None] * c_st + jnp.einsum('bhs,bhsd,bhse->bhde', w, v_c, k_c)
        n_new = decay[..., None] * n_st + jnp.einsum('bhs,bhse->bhe', w, k_c)
        return (c_new, n_new, m_new), (c_st, n_st, m_st)

    init = (jnp.zeros((bsz, nh, dh, dh), jnp.float32),
            jnp.zeros((bsz, nh, dh), jnp.float32),
            jnp.zeros((bsz, nh), jnp.float32))
    xs = (jnp.moveaxis(k, 2, 0), jnp.moveaxis(v, 2, 0), jnp.moveaxis(a, 2, 0), jnp.moveaxis(g, 2, 0))
    _, (c_prev, n_prev, m_prev) = lax.scan(step, init, xs)
    c_prev = jnp.moveaxis(c_prev, 0, 2)
    n_prev = jnp.moveaxis(n_prev, 0, 2)
    m_prev = jnp.moveaxis(m_prev, 0, 2)
    log_inter = b + m_prev[..., None]
    m_t = jnp.maximum(log_inter, jnp.max(log_d, axis=-1))
    s = jnp.einsum('bhnte,bhnse->bhnts', q, k) * jnp.exp(log_d - m_t[..., None])
    w_inter = jnp.exp(log_inter - m_t)
    num = (jnp.einsum('bhnts,bhnsd->bhntd', s, v)
           + w_inter[..., None] * jnp.einsum('bhnde,bhnte->bhntd', c_prev, q))
    den = jnp.sum(s, axis=-1) + w_inter * jnp.einsum('bhne,bhnte->bhnt', n_prev, q)
    h = num / jnp.maximum(jnp.abs(den), jnp.exp(-m_t))[..., None]
    return jnp.moveaxis(h, 1, 3).reshape(bsz, lp, nh, dh)

def token_mixer(x, g_pre, g_post, w_in, b_gates, lam_re, lam_im, b_re, b_im, c_re, c_im, d, log_dt,
                w_glu, w_qk, b_qk, g_head, w_a, w_b, w_out):
    bsz, L, _ = x.shape
    dtype = x.dtype
    h = rmsnorm(x, g_pre)
    proj = h @ w_in
    u, q, k, v, o, gi, gf, ga, gb = jnp.split(proj, IN_SPLITS, axis=-1)

    y_a = jax.nn.gelu(s5_ssm(u, lam_re, lam_im, b_re, b_im, c_re, c_im, d, log_dt))
    y_a = y_a * jax.nn.sigmoid(y_a @ w_glu.astype(jnp.float32))

    qk = jax.nn.silu(causal_dwconv(jnp.concatenate([q, k], axis=-1), w_qk, b_qk)).astype(jnp.float32)
    q, k = jnp.split(qk, 2, axis=-1)
    heads = lambda t: t.reshape(bsz, L, MLSTM_HEADS, MLSTM_HEAD_DIM)
    q = heads(q)
    k = heads(k) * (MLSTM_HEAD_DIM ** -0.5)
    v = heads(v.astype(jnp.float32))
    gates = (jnp.concatenate([gi, gf], axis=-1) + b_gates.astype(dtype)).astype(jnp.float32)
    log_i, f_pre = jnp.split(gates, 2, axis=-1)
    log_f = jax.nn.log_sigmoid(f_pre)
    pad = MLSTM_CHUNK - N_META
    padseq = lambda t, val: jnp.pad(t, [(0, 0), (pad, 0)] + [(0, 0)] * (t.ndim - 2), constant_values=val)
    hb = mlstm_chunkwise(padseq(q, 0.0), padseq(k, 0.0), padseq(v, 0.0),
                         padseq(log_i, PAD_LOG_INPUT_GATE), padseq(log_f, 0.0))[:, pad:]
    hb = hb * lax.rsqrt(jnp.mean(hb * hb, axis=-1, keepdims=True) + NORM_EPS)
    hb = hb * g_head.astype(jnp.float32).reshape(MLSTM_HEADS, MLSTM_HEAD_DIM)
    y_b = hb.reshape(bsz, L, MLSTM_WIDTH) * jax.nn.sigmoid(o.astype(jnp.float32))

    merged = (jax.nn.sigmoid(ga) * (y_a.astype(dtype) @ w_a)
              + jax.nn.sigmoid(gb) * (y_b.astype(dtype) @ w_b))
    return x + rmsnorm(merged @ w_out, g_post)

def channel_mixer(x, g_pre, g_post, w_gate, w_up, w_conv, b_conv, w_down):
    h = rmsnorm(x, g_pre)
    a = causal_dwconv(h @ w_gate, w_conv, b_conv)
    y = (jax.nn.gelu(a, approximate=True) * (h @ w_up)) @ w_down
    return x + rmsnorm(y, g_post)

def first_inputs(seed: int = 0) -> dict:
    key = jax.random.key(seed)
    ks = iter(jax.random.split(key, 40))
    f32 = jnp.float32
    nrm = lambda shape, scale: scale * jax.random.normal(next(ks), shape, f32)
    gain = lambda: 1.0 + nrm((DEPTH, D_MODEL), 0.02)
    G, P, GH, H = SSM_GROUPS, SSM_STATE, SSM_GROUP, MLSTM_HEADS
    x = nrm((BATCH, SEQ, D_MODEL), 1.0)
    meta_tokens = nrm((N_META, D_MODEL), 1.0)
    g_mix_pre = gain()
    g_mix_post = gain()
    w_in = nrm((DEPTH, D_MODEL, N_IN), D_MODEL ** -0.5)
    b_gates = jnp.concatenate([nrm((DEPTH, H), 0.1),
                               jnp.linspace(3.0, 6.0, H, dtype=f32)[None, :] + nrm((DEPTH, H), 0.1)], axis=-1)
    n_idx = jnp.arange(P, dtype=f32)
    ssm_lambda_re = -0.5 + nrm((DEPTH, G, P), 0.01)
    ssm_lambda_im = jnp.pi * n_idx[None, None, :] + nrm((DEPTH, G, P), 0.01)
    ssm_b_re = nrm((DEPTH, G, P, GH), (2 * GH) ** -0.5)
    ssm_b_im = nrm((DEPTH, G, P, GH), (2 * GH) ** -0.5)
    ssm_c_re = nrm((DEPTH, G, GH, P), P ** -0.5)
    ssm_c_im = nrm((DEPTH, G, GH, P), P ** -0.5)
    ssm_d = nrm((DEPTH, G, GH), 1.0)
    ssm_log_dt = jax.random.uniform(next(ks), (DEPTH, G), f32, math.log(1e-3), math.log(1e-1))
    w_ssm_glu = nrm((DEPTH, SSM_WIDTH, SSM_WIDTH), SSM_WIDTH ** -0.5)
    w_qk_conv = nrm((DEPTH, QK_CONV, 2 * MLSTM_WIDTH), QK_CONV ** -0.5)
    b_qk_conv = nrm((DEPTH, 2 * MLSTM_WIDTH), 0.02)
    g_head_norm = 1.0 + nrm((DEPTH, MLSTM_WIDTH), 0.02)
    w_branch_ssm = nrm((DEPTH, SSM_WIDTH, D_MODEL), SSM_WIDTH ** -0.5)
    w_branch_mlstm = nrm((DEPTH, MLSTM_WIDTH, D_MODEL), MLSTM_WIDTH ** -0.5)
    w_out = nrm((DEPTH, D_MODEL, D_MODEL), D_MODEL ** -0.5)
    g_ffn_pre = gain()
    g_ffn_post = gain()
    w_ffn_gate = nrm((DEPTH, D_MODEL, FFN_DIM), D_MODEL ** -0.5)
    w_ffn_up = nrm((DEPTH, D_MODEL, FFN_DIM), D_MODEL ** -0.5)
    w_ffn_conv = nrm((DEPTH, FFN_CONV, FFN_DIM), FFN_CONV ** -0.5)
    b_ffn_conv = nrm((DEPTH, FFN_DIM), 0.02)
    w_ffn_down = nrm((DEPTH, FFN_DIM, D_MODEL), FFN_DIM ** -0.5)
    return {'x': x, 'meta_tokens': meta_tokens, 'g_mix_pre': g_mix_pre, 'g_mix_post': g_mix_post,
            'w_in': w_in, 'b_gates': b_gates, 'ssm_lambda_re': ssm_lambda_re, 'ssm_lambda_im': ssm_lambda_im,
            'ssm_b_re': ssm_b_re, 'ssm_b_im': ssm_b_im, 'ssm_c_re': ssm_c_re, 'ssm_c_im': ssm_c_im,
            'ssm_d': ssm_d, 'ssm_log_dt': ssm_log_dt, 'w_ssm_glu': w_ssm_glu, 'w_qk_conv': w_qk_conv,
            'b_qk_conv': b_qk_conv, 'g_head_norm': g_head_norm, 'w_branch_ssm': w_branch_ssm,
            'w_branch_mlstm': w_branch_mlstm, 'w_out': w_out, 'g_ffn_pre': g_ffn_pre, 'g_ffn_post': g_ffn_post,
            'w_ffn_gate': w_ffn_gate, 'w_ffn_up': w_ffn_up, 'w_ffn_conv': w_ffn_conv, 'b_ffn_conv': b_ffn_conv,
            'w_ffn_down': w_ffn_down}

def first_block(x, meta_tokens, g_mix_pre, g_mix_post, w_in, b_gates, ssm_lambda_re, ssm_lambda_im,
              ssm_b_re, ssm_b_im, ssm_c_re, ssm_c_im, ssm_d, ssm_log_dt, w_ssm_glu, w_qk_conv,
              b_qk_conv, g_head_norm, w_branch_ssm, w_branch_mlstm, w_out, g_ffn_pre, g_ffn_post,
              w_ffn_gate, w_ffn_up, w_ffn_conv, b_ffn_conv, w_ffn_down):
    bsz = x.shape[0]
    meta = jnp.broadcast_to(meta_tokens.astype(x.dtype)[None], (bsz, N_META, D_MODEL))
    h = jnp.concatenate([meta, x], axis=1)
    for l in range(DEPTH):
        h = token_mixer(h, g_mix_pre[l], g_mix_post[l], w_in[l], b_gates[l],
                        ssm_lambda_re[l], ssm_lambda_im[l], ssm_b_re[l], ssm_b_im[l],
                        ssm_c_re[l], ssm_c_im[l], ssm_d[l], ssm_log_dt[l], w_ssm_glu[l],
                        w_qk_conv[l], b_qk_conv[l], g_head_norm[l],
                        w_branch_ssm[l], w_branch_mlstm[l], w_out[l])
        h = channel_mixer(h, g_ffn_pre[l], g_ffn_post[l], w_ffn_gate[l], w_ffn_up[l],
                          w_ffn_conv[l], b_ffn_conv[l], w_ffn_down[l])
    return h[:, N_META:]


HEAD_DIM = 64
D_MIX = D_MODEL
RWKV_WIDTH = D_MIX // 2
ATTN_WIDTH = D_MIX - RWKV_WIDTH
RWKV_HEADS = RWKV_WIDTH // HEAD_DIM
ATTN_HEADS = ATTN_WIDTH // HEAD_DIM
W_LORA = max(32, int(round(1.8 * RWKV_WIDTH ** 0.5 / 32)) * 32)
A_LORA = max(32, int(round(1.8 * RWKV_WIDTH ** 0.5 / 32)) * 32)
G_LORA = max(32, int(round(0.6 * RWKV_WIDTH ** 0.8 / 32)) * 32)
RWKV_COLS = 3 * RWKV_WIDTH + W_LORA + A_LORA + G_LORA
ATTN_COLS = 3 * ATTN_WIDTH
PROJ_COLS = RWKV_COLS + ATTN_COLS
D_FF = -(-8 * D_MODEL // (3 * 128)) * 128
CONV_WIDTH = 3
ROPE_THETA = 500000.0
ROT_DIM = HEAD_DIM // 4
DILATED_PATTERNS = ((128, 1), (512, 4), (2048, 16))
ATTN_BLOCK = 128
GN_EPS = 64e-5


def _rmsnorm(x, gain):
    xf = x.astype(jnp.float32)
    y = xf * lax.rsqrt(jnp.mean(xf * xf, axis=-1, keepdims=True) + NORM_EPS)
    return (y * gain.astype(jnp.float32)).astype(x.dtype)

def _token_shift(t):
    return jnp.pad(t, ((0, 0), (1, 0), (0, 0)))[:, :-1]

def _partial_rotary(x, positions):
    half = ROT_DIM // 2
    inv_freq = ROPE_THETA ** (-jnp.arange(half, dtype=jnp.float32) * 2.0 / ROT_DIM)
    ang = positions.astype(jnp.float32)[:, None] * inv_freq[None, :]
    cos = jnp.cos(ang)[None, :, None, :]
    sin = jnp.sin(ang)[None, :, None, :]
    xf = x[..., :ROT_DIM].astype(jnp.float32)
    x1, x2 = xf[..., :half], xf[..., half:]
    rot = jnp.concatenate([x1 * cos - x2 * sin, x2 * cos + x1 * sin], axis=-1)
    return jnp.concatenate([rot.astype(x.dtype), x[..., ROT_DIM:]], axis=-1)

def _banded_causal_attention(q, k, v, span):
    B, H, G, L, hd = q.shape
    n_blk = -(-L // ATTN_BLOCK)
    pad = n_blk * ATTN_BLOCK - L
    cfg = ((0, 0), (0, 0), (0, 0), (0, pad), (0, 0))
    q, k, v = (jnp.pad(t, cfg).reshape(B, H, G, n_blk, ATTN_BLOCK, hd) for t in (q, k, v))

    def with_prev(t):
        prev = jnp.pad(t, ((0, 0), (0, 0), (0, 0), (1, 0), (0, 0), (0, 0)))[:, :, :, :-1]
        return jnp.concatenate([prev, t], axis=4)

    kb, vb = with_prev(k), with_prev(v)
    s = jnp.einsum('bhgnqd,bhgnkd->bhgnqk', q, kb, preferred_element_type=jnp.float32) / math.sqrt(hd)
    blk = jnp.arange(n_blk)[:, None, None] * ATTN_BLOCK
    qpos = blk + jnp.arange(ATTN_BLOCK)[None, :, None]
    kpos = blk - ATTN_BLOCK + jnp.arange(2 * ATTN_BLOCK)[None, None, :]
    dist = qpos - kpos
    valid = (dist >= 0) & (dist <= span) & (kpos >= 0)
    s = jnp.where(valid, s, -jnp.inf)
    m = jnp.max(s, axis=-1, keepdims=True)
    p = jnp.exp(s - m)
    den = jnp.sum(p, axis=-1, keepdims=True)
    o = jnp.einsum('bhgnqk,bhgnkd->bhgnqd', p, vb.astype(jnp.float32)) / den
    lse = (m + jnp.log(den))[..., 0]
    o = o.reshape(B, H, G, n_blk * ATTN_BLOCK, hd)[:, :, :, :L]
    lse = lse.reshape(B, H, G, n_blk * ATTN_BLOCK)[..., :L]
    return o, lse

def _dilated_attention(q, k, v):
    B, S, H, hd = q.shape
    q, k, v = (t.transpose(0, 2, 1, 3) for t in (q, k, v))
    outs, lses = [], []
    for window, dil in DILATED_PATTERNS:
        L = S // dil

        def by_stride(t):
            return t.reshape(B, H, L, dil, hd).transpose(0, 1, 3, 2, 4)

        o, lse = _banded_causal_attention(by_stride(q), by_stride(k), by_stride(v), window // dil)
        outs.append(o.transpose(0, 1, 3, 2, 4).reshape(B, H, S, hd))
        lses.append(lse.transpose(0, 1, 3, 2).reshape(B, H, S))
    wts = jax.nn.softmax(jnp.stack(lses), axis=0)
    o = jnp.sum(wts[..., None] * jnp.stack(outs), axis=0)
    return o.transpose(0, 2, 1, 3)

def _rwkv7_scan(r, decay, k, v, kk, a):
    def step(state, inp):
        r_t, w_t, k_t, v_t, kk_t, a_t = inp
        sa = jnp.einsum('bhvk,bhk->bhv', state, -kk_t)
        state = (state * w_t[:, :, None, :]
                 + sa[..., None] * (kk_t * a_t)[:, :, None, :]
                 + v_t[..., None] * k_t[:, :, None, :])
        y = jnp.einsum('bhvk,bhk->bhv', state, r_t)
        return state, y

    B, S, H, N = r.shape
    xs = tuple(jnp.swapaxes(t, 0, 1) for t in (r, decay, k, v, kk, a))
    init = jnp.zeros((B, H, N, N), jnp.float32)
    _, ys = lax.scan(step, init, xs)
    return jnp.swapaxes(ys, 0, 1)

def _rwkv7_mixer(p, shift_mix, w0, w_lora_up, a0, a_lora_up, g_lora_up, k_k, k_a, r_k, ln_x_w, ln_x_b):
    B, S, _ = p.shape
    f32 = jnp.float32
    p = p + (_token_shift(p) - p) * shift_mix
    idx = [RWKV_WIDTH, 2 * RWKV_WIDTH, 3 * RWKV_WIDTH, 3 * RWKV_WIDTH + W_LORA, 3 * RWKV_WIDTH + W_LORA + A_LORA]
    r, k, v, wd, ad, gd = jnp.split(p, idx, axis=-1)
    w_log = -jax.nn.softplus(-(w0 + jnp.tanh(wd) @ w_lora_up)) - 0.5
    decay = jnp.exp(-jnp.exp(w_log.astype(f32)))
    a = jax.nn.sigmoid(a0 + ad @ a_lora_up)
    g = jax.nn.sigmoid(gd) @ g_lora_up

    def heads(t):
        return t.reshape(B, S, RWKV_HEADS, HEAD_DIM).astype(f32)

    kk = heads(k * k_k)
    kk = kk / jnp.maximum(jnp.sqrt(jnp.sum(kk * kk, axis=-1, keepdims=True)), 1e-12)
    k = k * (1.0 + (a - 1.0) * k_a)
    rh, kh, vh, ah, wh = heads(r), heads(k), heads(v), heads(a), heads(decay)
    y = _rwkv7_scan(rh, wh, kh, vh, kk, ah)
    mu = jnp.mean(y, axis=-1, keepdims=True)
    var = jnp.mean(jnp.square(y - mu), axis=-1, keepdims=True)
    y = ((y - mu) * lax.rsqrt(var + GN_EPS)).reshape(B, S, RWKV_WIDTH) * ln_x_w + ln_x_b
    bonus = jnp.sum(rh * kh * r_k.astype(f32), axis=-1, keepdims=True) * vh
    y = y + bonus.reshape(B, S, RWKV_WIDTH)
    return (y * g).astype(p.dtype)

def _causal_dwconv(t, w, b):
    out = lax.conv_general_dilated(t, w[:, None, :], window_strides=(1,), padding=[(CONV_WIDTH - 1, 0)],
                                   dimension_numbers=('NWC', 'WIO', 'NWC'), feature_group_count=t.shape[-1])
    return out + b

def second_inputs(seed: int = 0) -> dict:
    key = jax.random.key(seed)
    ks = jax.random.split(key, 24)
    f32 = jnp.float32
    L = DEPTH

    def normal(k, shape, scale):
        return jax.random.normal(k, shape, f32) * scale

    return {
        'x': normal(ks[0], (BATCH, SEQ, D_MODEL), 1.0),
        'mix_norm_gain': 1.0 + normal(ks[1], (L, D_MODEL), 0.02),
        'w_in': normal(ks[2], (L, D_MODEL, PROJ_COLS), D_MODEL ** -0.5),
        'rwkv_shift_mix': jax.random.uniform(ks[3], (L, RWKV_COLS), f32),
        'w0': jax.random.uniform(ks[4], (L, RWKV_WIDTH), f32, -4.0, 0.0),
        'w_lora_up': normal(ks[5], (L, W_LORA, RWKV_WIDTH), 0.1),
        'a0': normal(ks[6], (L, RWKV_WIDTH), 0.1),
        'a_lora_up': normal(ks[7], (L, A_LORA, RWKV_WIDTH), 0.1),
        'g_lora_up': normal(ks[8], (L, G_LORA, RWKV_WIDTH), G_LORA ** -0.5),
        'k_k': 0.85 + normal(ks[9], (L, RWKV_WIDTH), 0.02),
        'k_a': 1.0 + normal(ks[10], (L, RWKV_WIDTH), 0.02),
        'r_k': normal(ks[11], (L, RWKV_HEADS, HEAD_DIM), 0.1),
        'ln_x_w': 1.0 + normal(ks[12], (L, RWKV_WIDTH), 0.02),
        'ln_x_b': normal(ks[13], (L, RWKV_WIDTH), 0.02),
        'attn_norm_gain': 1.0 + normal(ks[14], (L, ATTN_WIDTH), 0.02),
        'w_out': normal(ks[15], (L, D_MIX, D_MODEL), D_MIX ** -0.5),
        'ffn_norm_gain': 1.0 + normal(ks[16], (L, D_MODEL), 0.02),
        'w_ffn_up': normal(ks[17], (L, D_MODEL, 2 * D_FF), D_MODEL ** -0.5),
        'ffn_conv_w': normal(ks[18], (L, CONV_WIDTH, D_FF), CONV_WIDTH ** -0.5),
        'ffn_conv_b': normal(ks[19], (L, D_FF), 0.02),
        'w_ffn_down': normal(ks[20], (L, D_FF, D_MODEL), D_FF ** -0.5),
        'final_norm_gain': 1.0 + normal(ks[21], (D_MODEL,), 0.02),
    }

def second_block(x, mix_norm_gain, w_in, rwkv_shift_mix, w0, w_lora_up, a0, a_lora_up, g_lora_up,
              k_k, k_a, r_k, ln_x_w, ln_x_b, attn_norm_gain, w_out, ffn_norm_gain, w_ffn_up,
              ffn_conv_w, ffn_conv_b, w_ffn_down, final_norm_gain):
    B, S, _ = x.shape
    positions = jnp.arange(S)
    for l in range(DEPTH):
        h = _rmsnorm(x, mix_norm_gain[l])
        proj = h @ w_in[l]
        p_rwkv, p_attn = proj[..., :RWKV_COLS], proj[..., RWKV_COLS:]
        y_rwkv = _rwkv7_mixer(p_rwkv, rwkv_shift_mix[l], w0[l], w_lora_up[l], a0[l], a_lora_up[l],
                              g_lora_up[l], k_k[l], k_a[l], r_k[l], ln_x_w[l], ln_x_b[l])
        q, k, v = (t.reshape(B, S, ATTN_HEADS, HEAD_DIM) for t in jnp.split(p_attn, 3, axis=-1))
        q = _partial_rotary(q, positions)
        k = _partial_rotary(k, positions)
        o = _dilated_attention(q, k, v)
        o = _rmsnorm(o, attn_norm_gain[l].reshape(ATTN_HEADS, HEAD_DIM)).astype(x.dtype)
        y_attn = o.reshape(B, S, ATTN_WIDTH)
        x = x + jnp.concatenate([y_rwkv, y_attn], axis=-1) @ w_out[l]
        h = _rmsnorm(x, ffn_norm_gain[l])
        gate, val = jnp.split(h @ w_ffn_up[l], 2, axis=-1)
        gate = _causal_dwconv(gate, ffn_conv_w[l], ffn_conv_b[l])
        x = x + (jax.nn.silu(gate) * val) @ w_ffn_down[l]
    return _rmsnorm(x, final_norm_gain)


_first_inputs = second_inputs


def second_inputs(seed=0):
    import zlib

    import numpy as np

    out = dict(_first_inputs(seed))
    spreads = {}
    factors = {'w_lora_up': 3.833,
     'a0': 3.667,
     'k_k': 8.0,
     'k_a': 7.763,
     'ln_x_w': 8.0,
     'ln_x_b': 8.0,
     'attn_norm_gain': 5.025,
     'ffn_norm_gain': 4.642,
     'ffn_conv_b': 6.946,
     'final_norm_gain': 2.75}
    for name, (base, spread) in spreads.items():
        noise = np.random.default_rng([zlib.crc32(name.encode()), seed]).standard_normal(out[name].shape)
        drawn = base * np.exp(spread * noise) if base else spread * noise
        out[name] = jnp.asarray(drawn.astype(out[name].dtype))
    for name, factor in factors.items():
        out[name] = (out[name] * factor).astype(out[name].dtype)
    return out


_narrow_inputs = second_inputs


def second_inputs(seed=0):

    out = dict(_narrow_inputs(seed))
    wider = {'k_k': 8.73,
     'ln_x_w': 3.67,
     'ln_x_b': 3.45,
     'attn_norm_gain': 3.31,
     'final_norm_gain': 3.09}
    for name, times in wider.items():
        mean = out[name].mean()
        out[name] = (mean + times * (out[name] - mean)).astype(out[name].dtype)
    return out


def setup_inputs(seed=0):
    out = dict(first_inputs(seed))
    for name, value in second_inputs(seed + 1).items():
        if name != "x":
            out[name + "_2"] = value
    return out


def reference(
    x, meta_tokens, g_mix_pre, g_mix_post, w_in, b_gates, ssm_lambda_re, ssm_lambda_im,
    ssm_b_re, ssm_b_im, ssm_c_re, ssm_c_im, ssm_d, ssm_log_dt, w_ssm_glu, w_qk_conv, b_qk_conv,
    g_head_norm, w_branch_ssm, w_branch_mlstm, w_out, g_ffn_pre, g_ffn_post, w_ffn_gate,
    w_ffn_up, w_ffn_conv, b_ffn_conv, w_ffn_down, mix_norm_gain_2, w_in_2, rwkv_shift_mix_2,
    w0_2, w_lora_up_2, a0_2, a_lora_up_2, g_lora_up_2, k_k_2, k_a_2, r_k_2, ln_x_w_2, ln_x_b_2,
    attn_norm_gain_2, w_out_2, ffn_norm_gain_2, w_ffn_up_2, ffn_conv_w_2, ffn_conv_b_2,
    w_ffn_down_2, final_norm_gain_2,
):
    x = first_block(
        x, meta_tokens, g_mix_pre, g_mix_post, w_in, b_gates, ssm_lambda_re, ssm_lambda_im,
        ssm_b_re, ssm_b_im, ssm_c_re, ssm_c_im, ssm_d, ssm_log_dt, w_ssm_glu, w_qk_conv,
        b_qk_conv, g_head_norm, w_branch_ssm, w_branch_mlstm, w_out, g_ffn_pre, g_ffn_post,
        w_ffn_gate, w_ffn_up, w_ffn_conv, b_ffn_conv, w_ffn_down,
    )
    return second_block(
        x, mix_norm_gain_2, w_in_2, rwkv_shift_mix_2, w0_2, w_lora_up_2, a0_2, a_lora_up_2,
        g_lora_up_2, k_k_2, k_a_2, r_k_2, ln_x_w_2, ln_x_b_2, attn_norm_gain_2, w_out_2,
        ffn_norm_gain_2, w_ffn_up_2, ffn_conv_w_2, ffn_conv_b_2, w_ffn_down_2,
        final_norm_gain_2,
    )


_drawn_inputs = setup_inputs


def setup_inputs(seed=0):
    import zlib

    import numpy as np

    out = dict(_drawn_inputs(seed))
    spreads = {}
    factors = {}
    for name, (base, spread) in spreads.items():
        noise = np.random.default_rng([zlib.crc32(name.encode()), seed]).standard_normal(out[name].shape)
        drawn = base * np.exp(spread * noise) if base else spread * noise
        out[name] = jnp.asarray(drawn.astype(out[name].dtype))
    for name, factor in factors.items():
        out[name] = (out[name] * factor).astype(out[name].dtype)
    return out
```

```python
from contextlib import ExitStack

import numpy as np
import concourse.bass as bass
from concourse import mybir

F = mybir.dt.float32
R = mybir.dt.float32r
ALU = mybir.AluOpType
ACT = mybir.ActivationFunctionType
AX_X = mybir.AxisListType.X
MUL, ADD, SUB, MAX, MIN = ALU.mult, ALU.add, ALU.subtract, ALU.max, ALU.min

T1 = 1040
CH1 = [(0, 352), (352, 344), (696, 344)]
T2 = 1024
CH2 = [(0, 512), (512, 512)]
TT1 = [(128 * i, min(128, T1 - 128 * i)) for i in range(9)]
NB = 130
FQ = [(0, 6), (6, 6), (12, 5), (17, 5)]
MAGIC = 12582912.0
TWO_PI_HI = 6.28125
TWO_PI_LO = 0.0019353071795864769

VCOLS = {}


def _vec_layout():
    at = 0
    for name, n in (("g_mix_pre", 8), ("g_mix_post", 8), ("wqk", 32), ("bqk", 8), ("bgate", 1), ("g_head", 4),
                    ("ssm_d", 4), ("g_ffn_pre", 8), ("g_ffn_post", 8), ("fconv", 66), ("fcb", 22),
                    ("mix_norm", 8), ("smix", 14), ("w0", 4), ("a0", 4), ("k_k", 4), ("k_a", 4), ("r_k", 4),
                    ("ln_w", 4), ("ln_b", 4), ("attn_g", 4), ("ffn_norm", 8), ("fconv2", 66), ("fcb2", 22),
                    ("final", 8)):
        VCOLS[name] = (at, n)
        at += n
    return at


NV = _vec_layout()


class Queue:

    def __init__(self, sem):
        self.sem, self.n, self.ops, self.seen, self.last = sem, 0, [], {}, None

    def wait(self, *toks):
        for t in toks:
            if t is None:
                continue
            if isinstance(t, list):
                self.wait(*t)
                continue
            key, sem, v = t
            if self.seen.get(key, 0) < v:
                self.seen[key] = v
                self.ops.append((0, sem, v))

    def do(self, fn, *toks, inc=True):
        self.wait(*toks)
        if not inc:
            self.ops.append((1, fn, None))
            return None
        self.n += 1
        self.ops.append((1, fn, self.sem))
        self.last = (self.sem[0], self.sem[1], self.n)
        return self.last

    def play(self, eng):
        for kind, a, b in self.ops:
            if kind == 0:
                eng.wait_ge(a, b)
            elif kind == 2:
                a(eng).then_inc(b, 16)
            elif b is None:
                a(eng)
            else:
                a(eng).then_inc(b[1], 1)


class Buf:

    def __init__(self, t):
        self.t, self.free = t, []


class Ring:
    def __init__(self, bufs):
        self.bufs, self.i = bufs, 0

    def get(self):
        b = self.bufs[self.i % len(self.bufs)]
        self.i += 1
        return b


class Banks:

    def __init__(self, tensors):
        self.idle = [Buf(t) for t in tensors]

    def get(self):
        assert self.idle
        return self.idle.pop(0)

    def put(self, b, *toks):
        b.free = [t for t in toks if t is not None]
        self.idle.append(b)


class Prog:
    pass


def dma(q, out, src, sem, count, *toks):
    q.wait(*toks)
    q.ops.append((2, lambda e: e.dma_start(out, src), sem[1]))
    return (sem[0], sem[1], count)


def mm(P, out, a, b, start, stop, *toks, inc=False, skip=False):
    if skip:
        return P.pe.do(lambda e: e.matmul(out, a, b, start=start, stop=stop, skip_group_check=True), *toks, inc=inc)
    return P.pe.do(lambda e: e.matmul(out, a, b, start=start, stop=stop), *toks, inc=inc)


def tp(P, out, src, ident, *toks, inc=False):
    return P.pe.do(lambda e: e.transpose(out, src, ident), *toks, inc=inc)


def act(P, out, src, func, *toks, bias=None, scale=None, acc=None):
    kw = {}
    if bias is not None:
        kw["bias"] = bias
    if scale is not None:
        kw["scale"] = scale
    if acc is not None:
        kw["accum_out"] = acc
    return P.act.do(lambda e: e.activation(out, src, func, **kw), *toks)


def cp(P, out, src, *toks):
    return act(P, out, src, ACT.Copy, *toks)


def tt(q, out, a, b, op, *toks):
    return q.do(lambda e: e.tensor_tensor(out, a, b, op), *toks)


def ts(q, out, a, s1, s2, op0, op1, *toks):
    if op1 is None:
        return q.do(lambda e: e.tensor_scalar(out, a, s1, None, op0), *toks)
    return q.do(lambda e: e.tensor_scalar(out, a, s1, s2, op0, op1), *toks)


def stt(q, out, a, s, b, op0, op1, *toks):
    return q.do(lambda e: e.scalar_tensor_tensor(out=out, in0=a, scalar=s, in1=b, op0=op0, op1=op1), *toks)


def recip(P, out, src, *toks):
    return P.dve.do(lambda e: e.reciprocal(out, src), *toks)


def vcopy(q, out, src, *toks):
    return q.do(lambda e: e.tensor_copy(out, src), *toks)


def reduce(P, out, src, op, *toks):
    return P.dve.do(lambda e: e.tensor_reduce(out, src, AX_X, op), *toks)


def mset(q, out, v, *toks):
    return q.do(lambda e: e.memset(out, v), *toks)


def split(P, src, hi, lo, *toks):
    t = cp(P, hi, src, *toks)
    return tt(P.dve, lo, src, hi.bitcast(F), SUB, t, *toks)


def everyone(P):
    return [q.last for q in (P.pe, P.act, P.dve, P.pool)]


class Weights:

    def __init__(self, P, plan, raws, his, los, sems):
        self.P, self.plan, self.raws, self.his, self.los, self.sems = P, plan, raws, his, los, sems
        self.loads = self.splits = self.used = 0
        self.raw_tok, self.split_tok, self.done_tok = {}, {}, {}

    def load(self):
        i = self.loads
        if i >= len(self.plan):
            return
        self.loads += 1
        name, src, kt = self.plan[i]
        s = i % len(self.raws)
        free = self.split_tok[i - len(self.raws)] if i >= len(self.raws) else None
        self.raw_tok[i] = dma(self.P.sp, self.raws[s][:, 0:kt * 128], src, self.sems[s],
                              16 * (i // len(self.raws) + 1), free)

    def split(self):
        i = self.splits
        if i >= len(self.plan):
            return
        self.splits += 1
        kt = self.plan[i][2]
        raw = self.raws[i % len(self.raws)][:, 0:kt * 128]
        s = i % len(self.his)
        free = self.done_tok[i - len(self.his)] if i >= len(self.his) else None
        self.split_tok[i] = split(self.P, raw, self.his[s][:, 0:kt * 128], self.los[s][:, 0:kt * 128],
                                  self.raw_tok[i], free)
        self.load()

    def use(self, name):
        i = self.used
        assert self.plan[i][0] == name, (self.plan[i][0], name)
        self.used += 1
        while self.splits < min(i + len(self.his), len(self.plan)):
            self.split()
        kt = self.plan[i][2]
        s = i % len(self.his)
        shape = lambda t: t[:, 0:kt * 128].rearrange("p (k n) -> p k n", k=kt)
        return i, shape(self.his[s]), shape(self.los[s]), self.split_tok[i]

    def done(self, i, tok):
        self.done_tok[i] = tok


def tick(P, n=1):
    for _ in range(n):
        if P.bg:
            if next(P.bg[0], "end") == "end":
                P.bg.pop(0)


def drain(P):
    while P.bg:
        tick(P)


def dense(P, name, kt, xh, xl, xtok, chunks, evac):
    i, wh, wl, wt = P.w.use(name)
    for c, (c0, cn) in enumerate(chunks):
        b = P.ps.get()
        t = None
        for k in range(kt):
            xs = (xh[:, k, c0:c0 + cn], xl[:, k, c0:c0 + cn])
            for n, (a, x) in enumerate(((wh, xs[0]), (wh, xs[1]), (wl, xs[0]))):
                last = k == kt - 1 and n == 2
                t = mm(P, b.t[:, 0:cn], a[:, k, :], x, k == 0 and n == 0, last, wt, xtok[k], b.free, inc=last)
        if c == len(chunks) - 1:
            P.w.done(i, t)
        P.ps.put(b, *evac(c, c0, cn, b.t[:, 0:cn], t))
        tick(P, P.rate)


class Stats:

    def __init__(self, P, acc, sq, T, chunks, free):
        self.P, self.acc, self.sq, self.T, self.chunks = P, acc[:, 0:T], sq, T, chunks
        self.n, self.tok, self.free = 0, None, free

    def add(self, x, *toks):
        P = self.P
        if self.n == 0:
            self.tok = tt(P.dve, self.acc, x, x, MUL, self.free, *toks)
        else:
            b = self.sq.get()
            t = act(P, b.t[:, 0:self.T], x, ACT.Square, b.free, *toks)
            self.tok = tt(P.dve, self.acc, self.acc, b.t[:, 0:self.T], ADD, t, self.tok)
            b.free = [self.tok]
        self.n += 1

    def finish(self, rstd, count, eps):
        P = self.P
        toks = []
        for c0, cn in self.chunks:
            b = P.ps.get()
            t = mm(P, b.t[:, 0:cn], P.ones, self.acc[:, c0:c0 + cn], True, True, self.tok, P.ctok, b.free, inc=True)
            t = act(P, rstd[:, c0:c0 + cn], b.t[:, 0:cn], ACT.Sqrt, t, bias=eps, scale=1.0 / count)
            P.ps.put(b, t)
            toks.append(recip(P, rstd[:, c0:c0 + cn], rstd[:, c0:c0 + cn], t))
        return toks[-1]


def ffn(P, kind, T, chunks, xtok, H, tag, vconv, vcb, after):
    htok = [None] * 8
    wname = "ffn" + tag
    with ExitStack() as cx:
        PH = cx.enter_context(P.nc.sbuf_tensor("PH" + tag, [128, 6, T], R))
        PL = cx.enter_context(P.nc.sbuf_tensor("PL" + tag, [128, 6, T], R))
        gs = Ring([Buf(cx.enter_context(P.nc.sbuf_tensor(f"G{tag}{i}", [128, T + 2], F))) for i in range(2)])
        cs = Ring([Buf(cx.enter_context(P.nc.sbuf_tensor(f"C{tag}{i}", [128, T], F))) for i in range(2)])
        for b in gs.bufs:
            b.free = [mset(P.pool, b.t[:, 0:2], 0.0, after)]
        for b in cs.bufs:
            b.free = [after]
        pfree = [after] * 6
        for f0, nf in FQ:
            ptok = [None] * nf
            for f in range(f0, f0 + nf):
                g, cbuf = gs.get(), cs.get()
                gt = []

                def ev_gate(c, c0, cn, ps, t):
                    gt.append(cp(P, g.t[:, 2 + c0:2 + c0 + cn], ps, t, g.free))
                    return [gt[-1]]

                dense(P, wname + "g", 8, P.XH, P.XL, xtok, chunks, ev_gate)
                w = lambda j: P.vec(vconv, 3 * f + j)
                t = ts(P.dve, cbuf.t[:, :], g.t[:, 2:2 + T], w(2), P.vec(vcb, f), MUL, ADD, gt, cbuf.free)
                t = stt(P.dve, cbuf.t[:, :], g.t[:, 1:1 + T], w(1), cbuf.t[:, :], MUL, ADD, t)
                t = stt(P.dve, cbuf.t[:, :], g.t[:, 0:T], w(0), cbuf.t[:, :], MUL, ADD, t)
                g.free = [t]
                ta = act(P, cbuf.t[:, :], cbuf.t[:, :], kind, t)
                ut = []

                def ev_up(c, c0, cn, ps, t):
                    ut.append(tt(P.dve, cbuf.t[:, c0:c0 + cn], cbuf.t[:, c0:c0 + cn], ps, MUL, t, ta))
                    return [ut[-1]]

                dense(P, wname + "u", 8, P.XH, P.XL, xtok, chunks, ev_up)
                k = f - f0
                ptok[k] = split(P, cbuf.t[:, :], PH[:, k, :], PL[:, k, :], ut, pfree[k])
                cbuf.free = [ptok[k]]
            last = None
            for m in range(8):
                def ev_down(c, c0, cn, ps, t):
                    if f0 == 0:
                        htok[m] = cp(P, H[:, m, c0:c0 + cn], ps, t, P.hfree)
                    else:
                        htok[m] = tt(P.dve, H[:, m, c0:c0 + cn], H[:, m, c0:c0 + cn], ps, ADD, t, htok[m])
                    return [htok[m]]

                dense(P, wname + "d", nf, PH, PL, ptok, chunks, ev_down)
            last = P.pe.last
            pfree = [last] * 6
        P.xfree = P.pe.last
    return htok


def cmul(q, outr, outi, ar, ai, br, bi, t1, t2, *toks):
    a = tt(q, t1, ar, br, MUL, *toks)
    b = tt(q, t2, ai, bi, MUL)
    c = tt(q, outr, t1, t2, SUB, a, b)
    a = tt(q, t1, ar, bi, MUL, c)
    b = tt(q, t2, ai, br, MUL)
    return tt(q, outi, t1, t2, ADD, a, b)


def discretise(P, lr, li, ldt, s, *toks):
    d = P.dve
    dt, mag, kc, cs, sn, ar, ai, den, zr, zi = s
    t0 = act(P, dt, ldt, ACT.Exp, *toks)
    t = tt(d, den, lr, dt, MUL, t0)
    tm = act(P, mag, den, ACT.Exp, t)
    t = tt(d, ar, li, dt, MUL, t0)
    for out, shift, back in ((sn, 0.0, 0.0), (cs, 0.25, 1.5707963267948966)):
        k = ts(d, kc, ar, 1.0 / (2.0 * np.pi), shift, MUL, ADD, t)
        k = ts(d, kc, kc, MAGIC, None, ADD, None, k)
        k = ts(d, kc, kc, -MAGIC, None, ADD, None, k)
        k2 = stt(d, out, kc, -TWO_PI_HI, ar, MUL, ADD, k)
        k2 = stt(d, out, kc, -TWO_PI_LO, out, MUL, ADD, k2)
        k2 = ts(d, out, out, back, None, ADD, None, k2)
        k2 = ts(d, out, out, 3.1415925, -3.1415925, MIN, MAX, k2)
        t = act(P, out, out, ACT.Sin, k2)
    t = tt(d, ar, mag, cs, MUL, t, tm)
    t = tt(d, ai, mag, sn, MUL, t)
    a = tt(d, den, lr, lr, MUL, t)
    b = tt(d, kc, li, li, MUL, t)
    a = tt(d, den, den, kc, ADD, a, b)
    rd = recip(P, den, den, a)
    n = ts(d, dt, ar, -1.0, None, ADD, None, t, t0)
    a = tt(d, zr, dt, lr, MUL, n)
    b = tt(d, kc, ai, li, MUL, n)
    a = tt(d, zr, zr, kc, ADD, a, b)
    a = tt(d, zr, zr, den, MUL, a, rd)
    b = tt(d, zi, ai, lr, MUL, a)
    c = tt(d, kc, dt, li, MUL, b)
    b = tt(d, zi, zi, kc, SUB, b, c)
    b = tt(d, zi, zi, den, MUL, b)
    return mag, cs, sn, ar, ai, zr, zi, b


def ssm(P, U, utok, free, after):
    nc, d = P.nc, P.dve
    ytok = [None] * 4
    with ExitStack() as cx:
        sb = lambda name, shape: cx.enter_context(nc.sbuf_tensor(name, shape, F))
        p1 = sb("ssm_p1", [128, 3, 16])
        s1 = sb("ssm_s1", [128, 10, 16])
        bc1 = sb("ssm_bc1", [128, 4, 16, 16])
        bb1 = sb("ssm_bb1", [128, 2, 256])
        q1 = sb("ssm_q1", [128, 2, 256])
        Bn = sb("ssm_Bn", [128, 2, 16, 2, 16])
        a2 = sb("ssm_a2", [128, 2, 256])
        bb2 = sb("ssm_bb2", [128, 2, 256])
        E = free.rearrange("p (r q c) -> p r q c", r=2, q=16)
        e8 = sb("ssm_e8", [128, 4, 16])
        r8 = sb("ssm_r8", [128, 16])
        Bop = sb("ssm_Bop", [128, 16, 2, 64])
        W = sb("ssm_W", [128, 9, 2, 64])
        Cop = sb("ssm_Cop", [128, 72, 2, 16])
        Dop = sb("ssm_Dop", [128, 8, 128])
        bt_ = sb("ssm_BT", [128, 4 * 4 * NB])
        BU = bt_[:, 0:8 * NB].rearrange("p (r c) -> p r c", r=2)
        tq = bt_[:, 8 * NB:16 * NB].rearrange("p (r c) -> p r c", r=2)
        p2 = bt_[:, 0:1280].rearrange("p (a c) -> p a c", a=5)
        q2 = Bop[:, :, :, :].rearrange("p a b c -> p (a b c)").rearrange("p (r c) -> p r c", r=2)
        pw = W[:, 0:8, :, :]
        s2 = Cop[:, :, :, :].rearrange("p a b c -> p (a b c)").rearrange("p (r c) -> p r c", r=9)
        V = sb("ssm_V", [128, 2, 4 * NB])
        Rk = sb("ssm_R", [128, 4 * NB])
        X = sb("ssm_X", [128, 2, 4, NB + 1])
        sem = P.newsem("ssm")
        dma(P.sp, p1[:, :, :], P.I["ssm_p1"], sem, 16, after)
        dma(P.sp, bc1[:, :, :, :], P.I["ssm_bc1"], sem, 32)
        ld = dma(P.sp, p2, P.I["ssm_p2"], sem, 48)
        s = [s1[:, i, :] for i in range(10)]
        mag1, c1, n1, ar1, ai1, zr1, zi1, t1 = discretise(P, p1[:, 0, :], p1[:, 1, :], p1[:, 2, :], s, ld, after)
        s = [s2[:, i, :] for i in range(5)] + [a2[:, 0, :], a2[:, 1, :]] + [s2[:, i, :] for i in range(5, 8)]
        _, _, _, ar2, ai2, zr2, zi2, t2 = discretise(P, p2[:, 0, :], p2[:, 1, :], p2[:, 2, :], s, ld, after)
        t2 = cmul(d, bb2[:, 0, :], bb2[:, 1, :], zr2, zi2, p2[:, 3, :], p2[:, 4, :], q1[:, 0, :], q1[:, 1, :], t2)
        b16 = lambda a: a.unsqueeze(2).broadcast_to([128, 16, 16])
        sq = lambda a: a.rearrange("p (q h) -> p q h", h=16)
        t1 = cmul(d, sq(bb1[:, 0, :]), sq(bb1[:, 1, :]), b16(zr1), b16(zi1), bc1[:, 0], bc1[:, 1],
                  sq(q1[:, 0, :]), sq(q1[:, 1, :]), t1, t2)
        for ri in range(2):
            for gg in range(2):
                t1 = ts(d, Bn[:, ri, :, gg, :], sq(bb1[:, ri, :]), P.mask64[:, gg:gg + 1], None, MUL, None, t1, P.ctok)
        t = t1
        cur = (c1, n1)
        for i in range(3):
            nxt = (e8[:, 2 * (i % 2), :], e8[:, 2 * (i % 2) + 1, :])
            t = cmul(d, nxt[0], nxt[1], cur[0], cur[1], cur[0], cur[1], q2[:, 0, 0:16], q2[:, 1, 0:16], t)
            cur = nxt
        m = tt(d, r8[:, :], mag1, mag1, MUL, t)
        m = tt(d, r8[:, :], r8[:, :], r8[:, :], MUL, m)
        m = tt(d, r8[:, :], r8[:, :], r8[:, :], MUL, m)
        ta = mset(d, E[:, 0, :, 0:1], 1.0, after)
        tb = mset(d, E[:, 1, :, 0:1], 0.0, after)
        t = tb
        n, which = 1, 0
        while n < NB:
            k = min(n, NB - n)
            bc = lambda a: a.unsqueeze(2).broadcast_to([128, 16, k])
            qa = q2[:, 0, 0:16 * k].rearrange("p (q c) -> p q c", c=k)
            qb = q2[:, 1, 0:16 * k].rearrange("p (q c) -> p q c", c=k)
            t = cmul(d, E[:, 0, :, n:n + k], E[:, 1, :, n:n + k], E[:, 0, :, 0:k], E[:, 1, :, 0:k],
                     bc(cur[0]), bc(cur[1]), qa, qb, t, ta, m)
            n += k
            if n < NB:
                i = 1 if which else 0
                nxt = (e8[:, 2 * (1 - i), :], e8[:, 2 * (1 - i) + 1, :])
                t = cmul(d, nxt[0], nxt[1], cur[0], cur[1], cur[0], cur[1], q2[:, 0, 0:16], q2[:, 1, 0:16], t)
                cur, which = nxt, not which
        setup = t
        dz = mset(P.pool, Dop[:, :, :], 0.0, after)
        peB, peC, peX = setup, setup, after
        xz = mset(P.pool, X[:, :, :, 0:1], 0.0, after)
        for j in range(4):
            a64r, a64i = ar2[:, 64 * j:64 * j + 64], ai2[:, 64 * j:64 * j + 64]
            t = vcopy(d, pw[:, 7, :, :], bb2[:, :, 64 * j:64 * j + 64], t2, setup)
            for tau in range(6, -1, -1):
                t = cmul(d, pw[:, tau, 0, :], pw[:, tau, 1, :], pw[:, tau + 1, 0, :], pw[:, tau + 1, 1, :],
                         a64r, a64i, q1[:, 0, 0:64], q1[:, 1, 0:64], t)
            pv = pw.rearrange("p a b c -> p (a b) c")
            for gg in range(2):
                bt = ts(P.pool, Bop[:, :, gg, :], pv, P.mask16[:, gg:gg + 1], None, MUL, None, t, peB, P.ctok)
            but = []
            for k in range(4):
                b = P.ps.get()
                for ri in range(2):
                    for tau in range(8):
                        tk = mm(P, b.t[:, ri * NB:(ri + 1) * NB],
                                Bop[32 * k:32 * k + 32, 2 * tau + ri, :, :].rearrange("p a b -> p (a b)"),
                                U[32 * k:32 * k + 32, j, tau:T1:8], tau == 0, tau == 7, bt, utok[j], b.free,
                                inc=(tau == 7 and ri == 1))
                t = cp(P, BU[:, :, NB * k:NB * k + NB], b.t[:, 0:2 * NB].rearrange("p (r c) -> p r c", r=2), tk, peX)
                P.ps.put(b, t)
                but.append(t)
                tick(P)
            peB = tk
            fl = lambda a: a.rearrange("p q c -> p (q c)")
            Er, Ei = fl(E[:, 0, 4 * j:4 * j + 4, :]), fl(E[:, 1, 4 * j:4 * j + 4, :])
            br, bi = BU[:, 0, :], BU[:, 1, :]
            a = tt(d, tq[:, 0, :], br, Er, MUL, but, peX, setup)
            b_ = tt(d, tq[:, 1, :], bi, Ei, MUL)
            v1 = tt(d, V[:, 0, :], tq[:, 0, :], tq[:, 1, :], ADD, a, b_)
            a = tt(d, tq[:, 0, :], bi, Er, MUL, v1)
            b_ = tt(d, tq[:, 1, :], br, Ei, MUL, v1)
            v2 = tt(d, V[:, 1, :], tq[:, 0, :], tq[:, 1, :], SUB, a, b_)
            rv = Rk[:, :].rearrange("p (q c) -> p q c", c=NB)
            t = vcopy(d, rv, r8[:, 4 * j:4 * j + 4].unsqueeze(2).broadcast_to([128, 4, NB]), v2, setup)
            t = mset(d, rv[:, :, 0:1], 0.0, t)
            yr, yi = BU[:, 0, :], BU[:, 1, :]

            def scan(o, v):
                return d.do(lambda e: e.tensor_tensor_scan(o, Rk[:, :], v, 0.0, MUL, ADD), t, v2)

            t = scan(yr, V[:, 0, :])
            t = scan(yi, V[:, 1, :])
            q = lambda a: a.rearrange("p (q c) -> p q c", c=NB)
            xt = cmul(d, X[:, 0, :, 1:NB + 1], X[:, 1, :, 1:NB + 1], q(yr), q(yi), E[:, 0, 4 * j:4 * j + 4, :],
                      E[:, 1, 4 * j:4 * j + 4, :], q(tq[:, 0, :]), q(tq[:, 1, :]), t, xz, peX)
            w4 = lambda tau, ri: W[:, tau, ri, :].rearrange("p (k h) -> p k h", h=16)
            t = vcopy(d, w4(0, 0), bc1[:, 2, 4 * j:4 * j + 4, :], ld, xt)
            t = ts(d, w4(0, 1), bc1[:, 3, 4 * j:4 * j + 4, :], -1.0, None, MUL, None, ld)
            a4 = lambda a: a[:, 4 * j:4 * j + 4].unsqueeze(2).broadcast_to([128, 4, 16])
            A, AI = a4(ar1), a4(ai1)
            h4 = lambda a: a[:, 0:64].rearrange("p (k h) -> p k h", h=16)
            ua, ub = h4(q1[:, 0, :]), h4(q1[:, 1, :])
            for tau in range(8):
                a = tt(d, ua, w4(tau, 0), A, MUL, t, t1)
                b_ = tt(d, ub, w4(tau, 1), AI, MUL, t)
                c = tt(d, w4(tau + 1, 0), ua, ub, ADD, a, b_)
                a = tt(d, ua, w4(tau, 1), A, MUL, c)
                b_ = tt(d, ub, w4(tau, 0), AI, MUL, c)
                t = tt(d, w4(tau + 1, 1), ua, ub, SUB, a, b_)
            wv = W[:, :, :, :].rearrange("p a b (k h) -> p (a b k) h", h=16)
            for gg in range(2):
                ct = ts(P.pool, Cop[:, :, gg, :], wv, P.mask64[:, gg:gg + 1], None, MUL, None, t, peC)
            cop = Cop[:, :, :, :].rearrange("p (a b k) g h -> p a b k (g h)", a=9, b=2)
            b = P.ps.get()
            for k in range(4):
                for ri in range(2):
                    tk = mm(P, b.t[32 * k:32 * k + 32, 0:256], Bn[:, ri, 4 * j + k, :, :].rearrange("p g h -> p (g h)"),
                            cop[:, 0:8, ri, k, :], ri == 0, ri == 1, ct, t1, b.free, inc=(k == 3 and ri == 1))
            dt = []
            for k in range(4):
                dt.append(vcopy(d, Dop[32 * k:32 * k + 32, :, 32 * k:32 * k + 32],
                                b.t[32 * k:32 * k + 32, 0:256].rearrange("p (a c) -> p a c", a=8), tk, dz, peC))
            P.ps.put(b, dt[-1])
            dt = stt(d, Dop[:, 0, :], P.ident, P.vec("ssm_d", j), Dop[:, 0, :], MUL, ADD, dt)
            gt = []
            for half in (3, 2, 1, 0):
                b = P.ps.get()
                for tau in (2 * half, 2 * half + 1):
                    o = b.t[:, (tau % 2) * NB:(tau % 2 + 1) * NB]
                    for sg in range(tau + 1):
                        mm(P, o, Dop[:, tau - sg, :], U[:, j, sg:T1:8], sg == 0, False, dt, utok[j], b.free, skip=True)
                    for k in range(4):
                        for ri in range(2):
                            tk = mm(P, b.t[32 * k:32 * k + 32, (tau % 2) * NB:(tau % 2 + 1) * NB],
                                    cop[:, tau + 1, ri, k, :], X[:, ri, k, 0:NB], False, ri == 1, xt, ct,
                                    inc=(tau % 2 == 1 and k == 3 and ri == 1), skip=True)
                yv = U[:, j, 0:T1].rearrange("p (c a) -> p a c", a=8)
                t = act(P, yv[:, 2 * half:2 * half + 2, :], b.t[:, 0:2 * NB].rearrange("p (a c) -> p a c", a=2),
                        ACT.Gelu_apprx_tanh, tk, after)
                P.ps.put(b, t)
                gt.append(t)
                tick(P)
            peC = peX = tk
            ytok[j] = gt[-1]
    return ytok


def mlstm_head(P, h, q, k, V1, M, free):
    d = P.dve
    sc = float(128 ** -0.5)
    nt = []
    for c0, cn in CH1:
        b = P.ps.get()
        t = mm(P, b.t[:, 0:cn], P.sel4[0:4, h, :], M.negM[0:4, c0:c0 + cn], True, True, M.tok, P.ctok, b.free, inc=True)
        t = cp(P, M.NMB[:, c0:c0 + cn], b.t[:, 0:cn], t, M.nmbfree)
        P.ps.put(b, t)
        nt.append(t)
    offs, off = [], 0
    stoks = []
    for i in range(9):
        s0 = 128 * i
        L = T1 - s0
        dn = min(128, L)
        D = M.D.get()
        u = M.UC[:, i, h:h + 1]
        t = ts(d, D.t[:, 0:dn], M.NMB[:, s0:s0 + dn], u, 0.0, ADD, MIN, nt, M.uctok, D.free)
        t = tt(d, D.t[:, 0:dn], D.t[:, 0:dn], P.triu_neg[:, 0:dn], ADD, t)
        dt = [act(P, D.t[:, 0:dn], D.t[:, 0:dn], ACT.Exp, t)]
        if L > 128:
            dt.append(act(P, D.t[:, 128:L], M.NMB[:, s0 + 128:T1], ACT.Exp, nt, M.uctok, D.free, bias=u))
        for c0 in range(0, L, 512):
            cn = min(512, L - c0)
            b = P.ps.get()
            t = mm(P, b.t[:, 0:cn], k.t[:, s0:s0 + 128], q.t[:, s0 + c0:s0 + c0 + cn], True, True, q.tok, k.tok,
                   b.free, inc=True)
            t = stt(d, M.SS[:, off + c0:off + c0 + cn], b.t[:, 0:cn], sc, D.t[:, c0:c0 + cn], MUL, MUL, t, dt, M.ssfree)
            P.ps.put(b, t)
            yield
        D.free = [t]
        stoks.append(t)
        offs.append(off)
        off += L
    M.nmbfree = P.everyone()
    q.buf.free = [P.pe.last]
    k.buf.free = [P.pe.last]
    ct = []
    for j in range(9):
        t0, tn = TT1[j]
        b = P.ps.get()
        for i in range(j + 1):
            o = offs[i] + t0 - 128 * i
            t = mm(P, b.t[0:tn, 0:129], M.SS[:, o:o + tn], V1.t[:, i, 0:129], i == 0, i == j, stoks[i], V1.tok,
                   b.free, inc=(i == j))
        ct.append(cp(P, M.NUM[0:tn, j, :], b.t[0:tn, 0:129], t, M.numfree))
        P.ps.put(b, ct[-1])
        yield
    M.ssfree = P.pe.last
    V1.buf.free = [P.pe.last]
    g = M.small
    N3 = M.NUM[:, :, 0:128]
    den = g[:, 0, :]
    t = stt(d, den, M.NUM[:, :, 128], -1.0, M.NUM[:, :, 128], MUL, MAX, ct)
    t = tt(d, den, den, M.EC[:, :, h], MAX, t, M.uctok)
    t = recip(P, den, den, t)
    bc = lambda a: a.unsqueeze(2).broadcast_to([128, 9, 128])
    t = tt(d, N3, N3, bc(den), MUL, t)
    D = M.D.get()
    HQ = D.t[:, :].rearrange("p (a c) -> p a c", a=9)
    t = tt(d, HQ, N3, N3, MUL, t, D.free)
    t = P.dve.do(lambda e: e.tensor_reduce(g[:, 1, :], HQ, AX_X, ADD), t)
    D.free = [t]
    t = act(P, g[:, 1, :], g[:, 1, :], ACT.Sqrt, t, bias=P.eps6, scale=1.0 / 128)
    t = recip(P, g[:, 1, :], g[:, 1, :], t)
    t = tt(d, N3, N3, bc(g[:, 1, :]), MUL, t)
    yield
    for j0 in (0, 4, 8):
        b = P.ps.get()
        js = range(j0, min(j0 + 4, 9))
        for j in js:
            t0, tn = TT1[j]
            tk = tp(P, b.t[:, 128 * (j - j0):128 * (j - j0) + tn], M.NUM[0:tn, j, 0:128], P.ident[0:tn, 0:tn], t,
                    b.free, inc=(j == js[-1]))
        w = T1 - 128 * j0 if j0 == 8 else 512
        M.ytok[h] = ts(d, M.Y[:, h, 128 * j0:128 * j0 + w], b.t[:, 0:w], P.vec("g_head", h), None, MUL, None, tk)
        P.ps.put(b, M.ytok[h])
        yield
    M.numfree = P.pe.last


class Tiled:
    def __init__(self, buf, tok):
        self.buf, self.t, self.tok = buf, buf.t, tok


def project(P, name, G, T, chunks, xtok, pad):
    toks = []

    def ev(c, c0, cn, ps, t):
        toks.append(cp(P, G.t[:, pad + c0:pad + c0 + cn], ps, t, G.free))
        return [toks[-1]]

    dense(P, name, 8, P.XH, P.XL, xtok, chunks, ev)
    return toks


def block1(P):
    nc, d = P.nc, P.dve
    I = P.I
    P.rate = 1
    HB = P.HB
    toks = []
    for k in range(8):
        toks.append(dma(P.pool, HB[:, k, 0:T1], I["x1"][:, k, :], P.xsem[k], 16))
    with ExitStack() as cx:
        sb = lambda name, shape: cx.enter_context(nc.sbuf_tensor(name, shape, F))
        acc = sb("n1_acc", [128, T1])
        rst = sb("n1_rs", [128, T1])
        sqr = Ring([Buf(sb(f"n1_sq{i}", [128, T1])) for i in range(2)])
        xtok = prenorm(P, HB, toks, T1, CH1, "g_mix_pre", acc, rst, sqr, None)
    after = P.everyone()
    with ExitStack() as cx:
        sb = lambda name, shape: cx.enter_context(nc.sbuf_tensor(name, shape, F))
        gi, gw = HB[0:64, 3, :], HB[0:64, 0:3, :]
        M = Prog()
        M.negM = gi[0:4, :]
        M.UC = sb("UC", [128, 9, 4])
        M.EC = sb("EC", [128, 9, 4])
        utok = [[] for _ in range(4)]
        for m in range(4):
            def ev_u(c, c0, cn, ps, t):
                utok[m].append(cp(P, HB[:, 4 + m, c0:c0 + cn], ps, t, after))
                return [utok[m][-1]]

            dense(P, "u", 8, P.XH, P.XL, xtok, CH1, ev_u)
        P.dbg("u", HB[:, 4:8, 0:T1], utok)
        ytok = ssm(P, HB[:, 4:8, :], utok, HB[:, 0:4, :].rearrange("p a t -> p (a t)"), P.everyone())
        P.dbg("ya0", HB[:, 4:8, 0:T1], ytok)
        after = P.everyone()
        with ExitStack() as cy:
            AH = cy.enter_context(nc.sbuf_tensor("glu_h", [128, 4, T1], R))
            AL = cy.enter_context(nc.sbuf_tensor("glu_l", [128, 4, T1], R))
            sg = Ring([Buf(cy.enter_context(nc.sbuf_tensor(f"glu_s{i}", [128, 352], F))) for i in range(2)])
            for b in sg.bufs:
                b.free = [after]
            at = [split(P, HB[:, 4 + m, 0:T1], AH[:, m, :], AL[:, m, :], ytok[m], after) for m in range(4)]
            for m in range(4):
                def ev_glu(c, c0, cn, ps, t):
                    s = sg.get()
                    t = act(P, s.t[:, 0:cn], ps, ACT.Sigmoid, t, s.free)
                    ytok[m] = tt(d, HB[:, 4 + m, c0:c0 + cn], HB[:, 4 + m, c0:c0 + cn], s.t[:, 0:cn], MUL, t, at)
                    s.free = [ytok[m]]
                    return [t]

                dense(P, "glu", 4, AH, AL, at, CH1, ev_glu)
        after = P.everyone()
        P.dbg("ya", HB[:, 4:8, 0:T1], ytok)
        gt = []

        def ev_g(c, c0, cn, ps, t):
            gt.append(ts(d, gi[0:64, c0:c0 + cn], ps[0:64, :], P.vec("bgate", 0)[0:64, :], None, ADD, None, t, after,
                         P.vtok))
            return [gt[-1]]

        dense(P, "gates", 8, P.XH, P.XL, xtok, CH1, ev_g)
        mlstm_gates(P, gi, gw, M, gt, after)
        with ExitStack() as cy:
            sb = lambda name, shape: cy.enter_context(nc.sbuf_tensor(name, shape, F))
            G = Ring([Buf(sb("m_G0", [128, T1 + 3]))])
            qs = Ring([Buf(sb(f"m_q{i}", [128, T1])) for i in range(2)])
            ks = Ring([Buf(sb(f"m_k{i}", [128, 1152])) for i in range(2)])
            vs = Ring([Buf(sb("m_V0", [128, 9, 130]))])
            M.SS = sb("m_SS", [128, 4752])
            M.D = Ring([Buf(sb(f"m_D{i}", [128, 1152])) for i in range(2)])
            M.NMB = sb("m_NMB", [128, T1])
            M.NUM = sb("m_NUM", [128, 9, 129])
            M.small = sb("m_small", [128, 2, 9])
            M.Y, M.ytok = HB, [None] * 4
            M.ssfree = M.nmbfree = after
            for b in G.bufs:
                b.free = [mset(P.pool, b.t[:, 0:3], 0.0, after), after]
            for b in qs.bufs + M.D.bufs:
                b.free = [after]
            for b in ks.bufs:
                b.free = [mset(P.pool, b.t[:, T1:1152], 0.0, after), after]
            for b in vs.bufs:
                t = mset(P.pool, b.t[:, 8, :], 0.0, after)
                b.free = [mset(P.pool, b.t[:, 0:8, 128:130], 1.0, after), mset(P.pool, b.t[0:16, 8, 128:130], 1.0, t),
                          after]
            M.numfree = mset(P.pool, M.NUM[:, 8, :], 0.0, after)

            def conv_silu(name, out, w0):
                g = G.get()
                t = project(P, name, g, T1, CH1, xtok, 3)
                w = lambda j: P.vec("wqk", 4 * w0 + j)
                o = out.t[:, 0:T1]
                t = ts(d, o, g.t[:, 3:3 + T1], w(3), P.vec("bqk", w0), MUL, ADD, t, out.free, P.vtok)
                for j in (2, 1, 0):
                    t = stt(d, o, g.t[:, j:j + T1], w(j), o, MUL, ADD, t)
                g.free = [t]
                return Tiled(out, act(P, o, o, ACT.Silu, t))

            for h in range(4):
                q = conv_silu("q", qs.get(), h)
                k = conv_silu("k", ks.get(), 4 + h)
                g = G.get()
                t = project(P, "v", g, T1, CH1, xtok, 3)
                V = vs.get()
                vt = []
                drain(P)
                for j0 in (0, 4, 8):
                    b = P.ps.get()
                    js = range(j0, min(j0 + 4, 9))
                    for j in js:
                        t0, tn = TT1[j]
                        tk = tp(P, b.t[0:tn, 128 * (j - j0):128 * (j - j0) + 128], g.t[:, 3 + t0:3 + t0 + tn], P.ident,
                                t, P.ctok, b.free, inc=(j == js[-1]))
                    n = len(js)
                    tn = TT1[js[-1]][1]
                    vt.append(cp(P, V.t[0:tn, j0:j0 + n, 0:128],
                                 b.t[0:tn, 0:128 * n].rearrange("p (a c) -> p a c", a=n), tk, V.free))
                    P.ps.put(b, vt[-1])
                g.free = [tk]
                drain(P)
                P.bg.append(mlstm_head(P, h, q, k, Tiled(V, vt), M, None))
            drain(P)
        ytok[0:4] = [ytok[3]] * 4
        after = P.everyone()
        P.dbg("hb", HB[:, 0:4, 0:T1], M.ytok)
    with ExitStack() as cx:
        sb = lambda name, shape, t=F: cx.enter_context(nc.sbuf_tensor(name, shape, t))
        AH, AL = sb("ya_h", [128, 4, T1], R), sb("ya_l", [128, 4, T1], R)
        BH, BL = sb("yb_h", [128, 4, T1], R), sb("yb_l", [128, 4, T1], R)
        tmp = Ring([Buf(sb(f"mg{i}", [128, 352])) for i in range(3)])
        for b in tmp.bufs:
            b.free = [after]
        at = [split(P, HB[:, 4 + m, 0:T1], AH[:, m, :], AL[:, m, :], ytok[m], after) for m in range(4)]
        bt = []
        for m in range(4):
            yt = []

            def ev_o(c, c0, cn, ps, t):
                s = tmp.get()
                t = act(P, s.t[:, 0:cn], ps, ACT.Sigmoid, t, s.free)
                yt.append(tt(d, HB[:, m, c0:c0 + cn], HB[:, m, c0:c0 + cn], s.t[:, 0:cn], MUL, t, M.ytok[m]))
                s.free = [yt[-1]]
                return [t]

            dense(P, "o", 8, P.XH, P.XL, xtok, CH1, ev_o)
            bt.append(split(P, HB[:, m, 0:T1], BH[:, m, :], BL[:, m, :], yt, after))
        mt = []
        for m in range(8):
            ga, gb = [], []

            def ev_ga(c, c0, cn, ps, t):
                ga.append(act(P, HB[:, m, c0:c0 + cn], ps, ACT.Sigmoid, t, at, bt))
                return [ga[-1]]

            def ev_a(c, c0, cn, ps, t):
                ga[c] = tt(d, HB[:, m, c0:c0 + cn], HB[:, m, c0:c0 + cn], ps, MUL, t, ga[c])
                return [ga[c]]

            def ev_gb(c, c0, cn, ps, t):
                s = tmp.get()
                s.tok = act(P, s.t[:, 0:cn], ps, ACT.Sigmoid, t, s.free)
                gb.append(s)
                return [s.tok]

            def ev_b(c, c0, cn, ps, t):
                s = gb[c]
                r = tt(d, s.t[:, 0:cn], s.t[:, 0:cn], ps, MUL, t, s.tok)
                mt.append(tt(d, HB[:, m, c0:c0 + cn], HB[:, m, c0:c0 + cn], s.t[:, 0:cn], ADD, r, ga[c]))
                s.free = [mt[-1]]
                return [r]

            dense(P, "ga", 8, P.XH, P.XL, xtok, CH1, ev_ga)
            dense(P, "wa", 4, AH, AL, at, CH1, ev_a)
            dense(P, "gb", 8, P.XH, P.XL, xtok, CH1, ev_gb)
            dense(P, "wb", 4, BH, BL, bt, CH1, ev_b)
        xfree = P.pe.last
        P.dbg("merged", HB[:, :, 0:T1], mt)
        xtok = [split(P, HB[:, m, 0:T1], P.XH[:, m, 0:T1], P.XL[:, m, 0:T1], mt[3 * m + 2], xfree) for m in range(8)]
    after = P.everyone()
    with ExitStack() as cx:
        sb = lambda name, shape, t=F: cx.enter_context(nc.sbuf_tensor(name, shape, t))
        acc, rs = sb("n2_acc", [128, T1]), sb("n2_rs", [128, T1])
        sq = Ring([Buf(sb(f"n2_sq{i}", [128, T1])) for i in range(2)])
        xr = Ring([Buf(sb(f"n2_x{i}", [128, T1])) for i in range(3)])
        for b in sq.bufs + xr.bufs:
            b.free = [after]
        st = Stats(P, acc, sq, T1, CH1, after)
        ht = [None] * 8
        for m in range(8):
            t8 = []

            def ev_w(c, c0, cn, ps, t):
                t8.append(cp(P, HB[:, m, c0:c0 + cn], ps, t, xtok[m]))
                return [t8[-1]]

            dense(P, "wout", 8, P.XH, P.XL, xtok, CH1, ev_w)
            st.add(HB[:, m, 0:T1], t8)
        t = st.finish(rs, 1024, P.eps6)
        after2 = P.pe.last
        ht = residual(P, HB, rs, t, "g_mix_post", xr, T1, I["x1"])
        P.dbg("h1", HB[:, :, 0:T1], ht)
        P.h1store = [dma(P.pool, P.h1[:, k, :], HB[:, k, 0:T1], P.hsem[k], 16, ht[k]) for k in range(8)]
        xtok = prenorm(P, HB, ht, T1, CH1, "g_ffn_pre", acc, rs, sq, after2)
    after = P.everyone()
    P.hfree = [after, P.h1store]
    htok = ffn(P, ACT.Gelu_apprx_tanh, T1, CH1, xtok, HB, "1", "fconv", "fcb", after)
    P.dbg("ffn1", HB[:, :, 0:T1], htok)
    after = P.everyone()
    with ExitStack() as cx:
        sb = lambda name, shape, t=F: cx.enter_context(nc.sbuf_tensor(name, shape, t))
        acc, rs = sb("n3_acc", [128, T1]), sb("n3_rs", [128, T1])
        sq = Ring([Buf(sb(f"n3_sq{i}", [128, T1])) for i in range(2)])
        xr = Ring([Buf(sb(f"n3_x{i}", [128, T1])) for i in range(3)])
        for b in sq.bufs + xr.bufs:
            b.free = [after]
        st = Stats(P, acc, sq, T1, CH1, after)
        for m in range(8):
            st.add(HB[:, m, 0:T1], htok[m])
        t = st.finish(rs, 1024, P.eps6)
        ht = residual(P, HB, rs, t, "g_ffn_post", xr, T1, P.h1, P.h1store)
        P.dbg("b1", HB[:, :, 0:T1], ht)
        P.h2store = [dma(P.pool, P.h2[:, k, :], HB[:, k, 16:T1], P.hsem[k], 32, ht[k]) for k in range(8)]
        xtok = prenorm(P, HB[:, :, 16:T1], ht, T2, CH2, "mix_norm", acc, rs, sq, None)
    return xtok


def residual(P, H, rs, t, gname, xr, T, src, *ready):
    ht = []
    for m in range(8):
        x, lt = reload(P, xr, m, T, src, list(ready))
        a = stt(P.dve, H[:, m, 0:T], H[:, m, 0:T], P.vec(gname, m), rs[:, 0:T], MUL, MUL, t)
        ht.append(tt(P.dve, H[:, m, 0:T], H[:, m, 0:T], x.t[:, 0:T], ADD, a, lt))
        x.free = [ht[-1]]
    return ht


def prenorm(P, H, toks, T, chunks, gname, acc, rs, sq, free):
    st = Stats(P, acc, sq, T, chunks, free)
    for k in range(8):
        st.add(H[:, k, 0:T], toks[k])
    t = st.finish(rs, 1024, P.eps6)
    out = []
    for k in range(8):
        b = sq.get()
        a = stt(P.dve, b.t[:, 0:T], H[:, k, 0:T], P.vec(gname, k), rs[:, 0:T], MUL, MUL, t, b.free, P.vtok)
        out.append(split(P, b.t[:, 0:T], P.XH[:, k, 0:T], P.XL[:, k, 0:T], a, P.xfree))
        b.free = [out[-1]]
    return out


def mlstm_gates(P, gi, gw, M, gt, after):
    d = P.dve
    f = gi[32:36, :]
    a, b = gw[32:36, 0, :], gw[32:36, 1, :]
    t = act(P, a, f, ACT.Abs, gt, after)
    t = act(P, a, a, ACT.Exp, t, scale=-1.0)
    t = act(P, a, a, ACT.Ln, t, bias=P.one[32:36, :])
    t = stt(d, b, f, 0.0, a, MIN, SUB, t)
    o = mset(d, gw[32:36, 2, :], 1.0, after)
    t = d.do(lambda e: e.tensor_tensor_scan(a, gw[32:36, 2, :], b, 0.0, MUL, ADD), t, o)
    B, u, m = gw[0:4, 0, :], gw[0:4, 1, :], gw[0:4, 2, :]
    t = vcopy(d, B, a, t)
    t = tt(d, u, gi[0:4, :], B, SUB, t)
    z = mset(d, M.negM[0:4, :], 0.0, t)
    t = d.do(lambda e: e.tensor_tensor_scan(m, M.negM[0:4, :], u, 0.0, ADD, MAX), t, z)
    n = ts(d, M.negM[0:4, :], m, -1.0, None, MUL, None, t)
    t = tt(d, B, B, m, ADD, t)
    e = act(P, B, B, ACT.Exp, t, scale=-1.0)
    z = mset(P.pool, M.UC[:, 8, :], -1e30, after)
    z2 = mset(P.pool, M.EC[:, 8, :], 1.0, after)
    bk = P.ps.get()
    for j, (t0, tn) in enumerate(TT1):
        tp(P, bk.t[0:tn, 8 * j:8 * j + 4], gw[0:4, 1, t0:t0 + tn], P.ident[0:4, 0:4], e, n, P.ctok, bk.free)
        tk = tp(P, bk.t[0:tn, 8 * j + 4:8 * j + 8], gw[0:4, 0, t0:t0 + tn], P.ident[0:4, 0:4], inc=(j == 8))
    v = bk.t[:, 0:72].rearrange("p (a c) -> p a c", c=8)
    t1 = cp(P, M.UC[:, 0:8, :], v[:, 0:8, 0:4], tk, after)
    t2 = cp(P, M.EC[:, 0:8, :], v[:, 0:8, 4:8], tk)
    t3 = cp(P, M.UC[0:16, 8, :], v[0:16, 8, 0:4], tk, z)
    t4 = cp(P, M.EC[0:16, 8, :], v[0:16, 8, 4:8], tk, z2)
    P.ps.put(bk, t4)
    M.uctok = [t1, t2, t3, t4, z, z2]
    M.tok = n


def vtrans(P, out, src, *toks):
    t = None
    for h in range(2):
        for a in range(2):
            for b in range(2):
                r, w = 64 * h + 32 * a, 64 * h + 32 * b
                o = out[w:w + 32, :].rearrange("p (c x) -> p c x", x=64)[:, :, 32 * a:32 * a + 32]
                s = src[r:r + 32, :].rearrange("p (c x) -> p c x", x=64)[:, :, 32 * b:32 * b + 32]
                t = P.dve.do(lambda e, o=o, s=s: e.transpose(o, s), *toks)
    return t


def pieces(P, n, outs, emit, evac):
    per = 512 // n
    for c0 in range(0, 8, per):
        b = P.ps.get()
        for c in range(c0, c0 + per):
            for h in range(2):
                last = c == c0 + per - 1 and h == 1
                t = emit(h, c, b.t[64 * h:64 * h + 64, (c - c0) * n:(c - c0 + 1) * n], b.free, last)
        P.ps.put(b, evac(c0, per, b.t[:, 0:512], t))
        yield


def rwkv_half(P, j, hf, D):
    d = P.dve
    g0 = 512 * hf
    r, k, v = D.r.t[:, g0:g0 + 512], D.k.t[:, g0:g0 + 512], D.v.t[:, g0:g0 + 512]
    r_t, k_t, v_t = D.r.tok, D.k.tok, D.v.tok
    S = D.S
    full = lambda n: S[n][:, :]
    c3 = lambda a: a.rearrange("p (c x) -> p c x", x=64)
    lw, a_, kk = full("t0"), full("t1"), full("t2")
    tk = []
    for c0, cn in ((0, 512),):
        b = P.ps.get()
        t = mm(P, b.t[:, 0:cn], D.wl[0:32, 128 * j:128 * j + 128], D.WA[0:32, g0:g0 + cn], True, True, D.wat, b.free,
               inc=True)
        t = act(P, lw[:, c0:c0 + cn], b.t[:, 0:cn], ACT.Sigmoid, t, D.free, bias=P.vec("w0", j))
        P.ps.put(b, t)
        b = P.ps.get()
        t = mm(P, b.t[:, 0:cn], D.wl[32:64, 128 * j:128 * j + 128], D.WA[32:64, g0:g0 + cn], True, True, D.wat, b.free,
               inc=True)
        t = act(P, a_[:, c0:c0 + cn], b.t[:, 0:cn], ACT.Sigmoid, t, D.free, bias=P.vec("a0", j))
        P.ps.put(b, t)
        yield
    lt = ts(d, lw, lw, -0.6065306597126334, None, MUL, None, t)
    t2 = ts(d, kk, k, P.vec("k_k", j), None, MUL, None, k_t, t)
    t3 = tt(d, full("t3"), kk, kk, MUL, t2)
    for c0, cn in ((0, 512),):
        b = P.ps.get()
        t = mm(P, b.t[:, 0:cn], P.ones64, full("t3")[:, c0:c0 + cn], True, True, t3, P.ctok, b.free, inc=True)
        t = act(P, full("t4")[:, c0:c0 + cn], b.t[:, 0:cn], ACT.Sqrt, t, D.free)
        P.ps.put(b, t)
    t = ts(d, full("t4"), full("t4"), 1e-12, None, MAX, None, t)
    t = recip(P, full("t4"), full("t4"), t)
    t = tt(d, kk, kk, full("t4"), MUL, t)
    tb = stt(d, full("t3"), kk, -1.0, a_, MUL, MUL, t)
    yield
    t = ts(d, a_, a_, -1.0, P.vec("k_a", j), ADD, MUL, tb)
    tk2 = stt(d, a_, a_, 1.0, k, ADD, MUL, t, k_t)
    k2, bn = a_, full("t3")
    t = stt(d, full("bon"), r, P.vec("r_k", j), k2, MUL, MUL, tk2, r_t, D.free)
    bt = []
    for c0, cn in ((0, 512),):
        b = P.ps.get()
        t1 = mm(P, b.t[:, 0:cn], P.ones64, full("bon")[:, c0:c0 + cn], True, True, t, b.free, inc=True)
        t1 = tt(d, full("bon")[:, c0:c0 + cn], b.t[:, 0:cn], v[:, c0:c0 + cn], MUL, t1, v_t)
        P.ps.put(b, t1)
        bt.append(t1)
    yield
    cum = full("t4")
    t = d.do(lambda e: e.tensor_tensor_scan(cum, D.reset[:, :], lw, 0.0, MUL, ADD), lt, tk2, D.rtok)
    AR = S["AR"][:, :].rearrange("p (c a x) -> p c a x", a=2, x=64)
    e1 = act(P, AR[:, :, 1, :], c3(cum), ACT.Exp, t, D.free)
    trho = tt(d, AR[:, :, 1, :], AR[:, :, 1, :], c3(r), MUL, e1, r_t)
    tl = tt(d, lw, cum, lw, SUB, t)
    e2 = act(P, AR[:, :, 0, :], c3(lw), ACT.Exp, tl)
    tal = tt(d, AR[:, :, 0, :], AR[:, :, 0, :], c3(kk), MUL, e2)
    e3 = act(P, lw, cum, ACT.Exp, tl, e2, scale=-1.0)
    be, ka = S["BK"][:, 0:512], S["BK"][:, 512:1024]
    tbe = tt(d, be, bn, lw, MUL, e3, D.free)
    tka = tt(d, ka, k2, lw, MUL, e3)
    last = c3(cum)[:, :, 63:64].broadcast_to([128, 8, 64])
    t = tt(d, c3(kk), last, c3(cum), SUB, tal)
    e4 = act(P, kk, kk, ACT.Exp, t)
    e5 = act(P, D.pc[:, :], c3(cum)[:, :, 63], ACT.Exp, t, D.free)
    tb2 = tt(d, bn, bn, kk, MUL, e4, tbe)
    tk2b = tt(d, k2, k2, kk, MUL, e4, tka)
    yield
    AM = S["AM"][:, :].rearrange("p (c a x) -> p c a x", a=2, x=64)
    tcp = vcopy(d, c3(lw), AR[:, :, 0, :], tal, tbe, tka)
    Vt, Bt, Kt, At = full("Vt"), kk, full("t4"), full("Xa")
    x1 = vtrans(P, Vt, v, v_t, D.free)
    x2 = vtrans(P, Bt, bn, tb2, tk2b)
    x3 = vtrans(P, Kt, k2, tk2b, e5)
    x4 = vtrans(P, At, lw, tcp, D.free)
    x5 = vcopy(d, AM[:, :, 0, :], c3(At), x4)
    if hf == 1:
        D.r.buf.free = D.k.buf.free = D.v.buf.free = P.everyone()
        D.released = True
    yield
    GB = S["GB"][:, :].rearrange("p (c a x) -> p c a x", a=2, x=64)
    GK = S["GK"][:, :].rearrange("p (c a x) -> p c a x", a=2, x=64)
    hs = lambda h: slice(64 * h, 64 * h + 64)
    cs = lambda c: slice(64 * c, 64 * c + 64)
    st = {}

    def keep(key, t):
        st.setdefault(key, []).append(t)
        return t

    for key, out, lhs in (("GB", GB, be), ("GK", GK, ka)):
        def emit(h, c, o, fr, lastone):
            return mm(P, o, lhs[hs(h), cs(c)], AR[hs(h), c, :, :].rearrange("p a x -> p (a x)"), True, True, tbe, tka,
                      trho, tal, fr, inc=lastone)

        def evac(c0, n, ps, t):
            return keep(key, tt(d, out[:, c0:c0 + n, :, :].rearrange("p c a x -> p c (a x)"),
                                ps.rearrange("p (c x) -> p c x", x=128),
                                P.mtri[:, :].unsqueeze(1).broadcast_to([128, n, 128]), MUL, t, P.ctok, D.free))

        yield from pieces(P, 128, out, emit, evac)
    X, Xt, Y = full("Xa"), full("Xt"), full("t0")
    Ln = full("t1")

    def emit(h, c, o, fr, lastone):
        return mm(P, o, AR[hs(h), c, 0, :], be[hs(h), cs(c)], True, True, fr, inc=lastone)

    def evac(c0, n, ps, t):
        return keep("L", tt(d, c3(Ln)[:, c0:c0 + n, :], ps.rearrange("p (c x) -> p c x", x=64),
                            P.levels[:, 0, :].unsqueeze(1).broadcast_to([128, n, 64]), MUL, t, x3, P.ctok))

    yield from pieces(P, 64, Ln, emit, evac)
    id3 = P.ident2[:, :].unsqueeze(1).broadcast_to([128, 8, 64])
    t = tt(d, c3(X), c3(Ln), id3, ADD, st["L"], x5)
    tx = t
    t = tt(d, c3(Xt), GB[:, :, 0, :], P.levels[:, 1, :].unsqueeze(1).broadcast_to([128, 8, 64]), MUL, st["GB"], D.free)
    txt = tt(d, c3(Xt), c3(Xt), id3, ADD, t)
    ty = [tcp]
    for lv in range(5):
        st["Y"] = []

        def emit(h, c, o, fr, lastone):
            return mm(P, o, GB[hs(h), c, 0, :], X[hs(h), cs(c)], True, True, tx, txt, st["GB"], fr, inc=lastone)

        def evac(c0, n, ps, t):
            return keep("Y", tt(d, c3(Y)[:, c0:c0 + n, :], ps.rearrange("p (c x) -> p c x", x=64),
                                P.levels[:, 2 + lv, :].unsqueeze(1).broadcast_to([128, n, 64]), MUL, t, ty))

        yield from pieces(P, 64, Y, emit, evac)
        st["X"], st["Xt"] = [], []
        outs = []
        for c0 in (0,):
            bx, by = P.ps.get(), P.ps.get()
            for c in range(c0, c0 + 8):
                for h in range(2):
                    end = c == c0 + 7 and h == 1
                    o = slice(64 * (c - c0), 64 * (c - c0) + 64)
                    if lv < 4:
                        tz = mm(P, bx.t[hs(h), o], Xt[hs(h), cs(c)], Y[hs(h), cs(c)], True, True, st["Y"], txt, bx.free,
                                inc=end)
                    tzt = mm(P, by.t[hs(h), o], Y[hs(h), cs(c)], Xt[hs(h), cs(c)], True, True, st["Y"], txt, by.free,
                             inc=end)
            outs.append((bx, by, tz if lv < 4 else None, tzt))
            yield
        for c0, (bx, by, tz, tzt) in zip((0,), outs):
            w = slice(64 * c0, 64 * c0 + 512)
            if lv < 4:
                tx = tt(d, X[:, w], X[:, w], bx.t[:, 0:512], ADD, tz)
                P.ps.put(bx, tx)
            else:
                P.ps.put(bx, bx.free)
            txt = tt(d, Xt[:, w], Xt[:, w], by.t[:, 0:512], ADD, outs[0][3])
            P.ps.put(by, txt)
        ty = [outs[0][3]]
        yield

    def emit(h, c, o, fr, lastone):
        return mm(P, o, GK[hs(h), c, 0, :], Vt[hs(h), cs(c)], True, True, st["GK"], x1, fr, inc=lastone)

    def evac(c0, n, ps, t):
        return keep("MV", cp(P, AM[:, c0:c0 + n, 1, :], ps.rearrange("p (c x) -> p c x", x=64), t, D.free))

    yield from pieces(P, 64, None, emit, evac)
    WU = S["BK"][:, :].rearrange("p (c a x) -> p c a x", a=2, x=64)

    def emit(h, c, o, fr, lastone):
        return mm(P, o, Xt[hs(h), cs(c)], AM[hs(h), c, :, :].rearrange("p a x -> p (a x)"), True, True, st["MV"], x5,
                  txt, fr, inc=lastone)

    def evac(c0, n, ps, t):
        return keep("WU", cp(P, WU[:, c0:c0 + n, :, :].rearrange("p c a x -> p c (a x)"),
                             ps.rearrange("p (c x) -> p c x", x=128), t, st["L"]))

    yield from pieces(P, 128, None, emit, evac)
    FT, O, Rh, S0 = full("Xa"), full("t1"), full("t0"), full("S0")
    tdp = tt(d, c3(FT), id3, D.pc[:, :].unsqueeze(2).broadcast_to([128, 8, 64]), MUL, e5, tx, ty)

    def emit(h, c, o, fr, lastone):
        return mm(P, o, WU[hs(h), c, 0, :], Bt[hs(h), cs(c)], True, True, st["WU"], x2, fr, inc=lastone)

    def evac(c0, n, ps, t):
        w = slice(64 * c0, 64 * (c0 + n))
        return keep("F", tt(d, FT[:, w], FT[:, w], ps, ADD, t, tdp))

    yield from pieces(P, 64, None, emit, evac)

    def emit(h, c, o, fr, lastone):
        mm(P, o, Kt[hs(h), cs(c)], Vt[hs(h), cs(c)], True, False, st["WU"], x3, x1, fr)
        return mm(P, o, Bt[hs(h), cs(c)], WU[hs(h), c, 1, :], False, True, inc=lastone)

    def evac(c0, n, ps, t):
        return keep("O", cp(P, O[:, 64 * c0:64 * (c0 + n)], ps, t, tx))

    yield from pieces(P, 64, None, emit, evac)

    def emit(h, c, o, fr, lastone):
        return mm(P, o, WU[hs(h), c, 0, :], GB[hs(h), c, 1, :], True, True, fr, inc=lastone)

    def evac(c0, n, ps, t):
        return keep("R", tt(d, c3(Rh)[:, c0:c0 + n, :], ps.rearrange("p (c x) -> p c x", x=64), AR[:, c0:c0 + n, 1, :],
                            ADD, t))

    yield from pieces(P, 64, None, emit, evac)
    if hf == 0:
        t = mset(d, S0[:, 0:64], 0.0, D.free)
    else:
        t = vcopy(d, S0[:, 0:64], S0[:, 512:576], D.free)
    sk = [t]
    for c in range(8 if hf == 0 else 7):
        b = P.ps.get()
        for h in range(2):
            t = mm(P, b.t[hs(h), 0:64], FT[hs(h), cs(c)], S0[hs(h), cs(c)], True, True, sk[-1], st["F"], b.free,
                   inc=h == 1)
        t = tt(d, S0[:, 64 * (c + 1):64 * (c + 2)], b.t[:, 0:64], O[:, cs(c)], ADD, t, st["O"])
        P.ps.put(b, t)
        sk.append(t)
        yield

    def emit(h, c, o, fr, lastone):
        mm(P, o, Vt[hs(h), cs(c)], GK[hs(h), c, 1, :], True, False, fr)
        mm(P, o, WU[hs(h), c, 1, :], GB[hs(h), c, 1, :], False, False)
        return mm(P, o, S0[hs(h), cs(c)], Rh[hs(h), cs(c)], False, True, sk, st["R"], inc=lastone)

    yc = full("t2")

    def evac(c0, n, ps, t):
        return keep("YY", cp(P, yc[:, 64 * c0:64 * (c0 + n)], ps, t))

    yield from pieces(P, 64, None, emit, evac)
    sq, rs = full("t3"), full("t4")
    yt = []
    for c0, cn in ((0, 512),):
        b = P.ps.get()
        t = mm(P, b.t[:, 0:cn], P.ones64, yc[:, c0:c0 + cn], True, True, st["YY"], b.free, inc=True)
        t = stt(d, yc[:, c0:c0 + cn], b.t[:, 0:cn], -1.0 / 64, yc[:, c0:c0 + cn], MUL, ADD, t)
        P.ps.put(b, t)
    t = tt(d, sq, yc, yc, MUL, t)
    yield
    for c0, cn in ((0, 512),):
        b = P.ps.get()
        tq = mm(P, b.t[:, 0:cn], P.ones64, sq[:, c0:c0 + cn], True, True, t, b.free, inc=True)
        tq = act(P, rs[:, c0:c0 + cn], b.t[:, 0:cn], ACT.Sqrt, tq, t, bias=P.eps64, scale=1.0 / 64)
        P.ps.put(b, tq)
    t = recip(P, rs, rs, tq)
    t = tt(d, yc, yc, rs, MUL, t)
    t = ts(d, yc, yc, P.vec("ln_w", j), P.vec("ln_b", j), MUL, ADD, t)
    t = tt(d, yc, yc, full("bon"), ADD, t, bt)
    yield
    for c0, cn in ((0, 512),):
        b = P.ps.get()
        tg = mm(P, b.t[:, 0:cn], D.gl[0:96, 128 * j:128 * j + 128], D.GD[0:96, g0:g0 + cn], True, True, D.gdt, b.free,
                inc=True)
        tg = tt(d, P.HB[:, j, g0:g0 + cn], yc[:, c0:c0 + cn], b.t[:, 0:cn], MUL, tg, t, D.hfree)
        P.ps.put(b, tg)
        yt.append(tg)
    P.ytok[j] = yt[-1]
    D.free = P.everyone()


def rwkv_pair(P, j, D):
    for hf in range(2):
        yield from rwkv_half(P, j, hf, D)


def attention_pair(P, j, D):
    d = P.dve
    q, k, v = D.q, D.k, D.v
    VT = D.VT.get()
    vt = []
    for c in range(0, 8, 4):
        b = P.ps.get()
        for n in range(4):
            t = tp(P, b.t[:, 128 * n:128 * n + 128], v.t[:, 128 * (c + n):128 * (c + n) + 128], P.ident, v.tok,
                   P.ctok, b.free, inc=n == 3)
        vt.append(cp(P, VT.t[:, 512 * (c // 4):512 * (c // 4) + 512], b.t[:, :], t, VT.free))
        P.ps.put(b, vt[-1])
    v.buf.free = [P.pe.last]
    yield
    ot = []
    for i in range(8):
        n = 128 * (i + 1)
        for h in range(2):
            hs = slice(64 * h, 64 * h + 64)
            A = D.A.get()
            at = []
            for c0 in range(0, n, 512):
                cn = min(512, n - c0)
                b = P.ps.get()
                t = mm(P, b.t[:, 0:cn], q.t[hs, 128 * i:128 * i + 128], k.t[hs, c0:c0 + cn], True, True, q.tok, k.tok,
                       b.free, inc=True)
                t = tt(d, A.t[:, c0:c0 + cn], b.t[:, 0:cn], D.mask[:, (7 - i) * 128 + c0:(7 - i) * 128 + c0 + cn], ADD,
                       t, A.free, D.mtok)
                P.ps.put(b, t)
                at.append(t)
            mx = D.mx[:, 2 * i + h:2 * i + h + 1]
            t = reduce(P, mx, A.t[:, 0:n], MAX, at, D.ofree)
            t = ts(d, mx, mx, -1.0, None, MUL, None, t)
            t = act(P, A.t[:, 0:n], A.t[:, 0:n], ACT.Exp, t, bias=mx, acc=D.den[:, 2 * i + h:2 * i + h + 1])
            yield
            PT = D.PT.get()
            ptt = []
            for c0 in range(0, i + 1, 4):
                cn = min(4, i + 1 - c0)
                b = P.ps.get()
                for c in range(cn):
                    tk = tp(P, b.t[:, 128 * c:128 * c + 128], A.t[:, 128 * (c0 + c):128 * (c0 + c) + 128], P.ident, t,
                            b.free, inc=c == cn - 1)
                ptt.append(cp(P, PT.t[:, 128 * c0:128 * (c0 + cn)], b.t[:, 0:128 * cn], tk, PT.free))
                P.ps.put(b, ptt[-1])
            A.free = [tk]
            yield
            b = P.ps.get()
            for c in range(i + 1):
                tk = mm(P, b.t[:, 0:64], PT.t[:, 128 * c:128 * c + 128], VT.t[:, 128 * c + 64 * h:128 * c + 64 * h + 64],
                        c == 0, c == i, ptt, vt, b.free, inc=c == i)
            PT.free = [tk]
            ot.append(cp(P, D.O[:, i, h, :], b.t[:, 0:64], tk, D.ofree))
            P.ps.put(b, ot[-1])
            yield
    q.buf.free = k.buf.free = [P.pe.last]
    VT.free = [P.pe.last]
    O = D.O[:, :, :, :].rearrange("p a h x -> p (a h) x")
    bc = lambda a: a.unsqueeze(2).broadcast_to([128, 16, 64])
    t = recip(P, D.den[:, :], D.den[:, :], ot)
    t = tt(d, O, O, bc(D.den[:, :]), MUL, t)
    t = tt(d, D.OQ[:, :, :], O, O, MUL, t)
    t = d.do(lambda e: e.tensor_reduce(D.mx[:, :], D.OQ[:, :, :], AX_X, ADD), t)
    t = act(P, D.mx[:, :], D.mx[:, :], ACT.Sqrt, t, bias=P.eps6, scale=1.0 / 64)
    t = recip(P, D.mx[:, :], D.mx[:, :], t)
    t = tt(d, O, O, bc(D.mx[:, :]), MUL, t)
    yield
    for c in range(0, 8, 4):
        b = P.ps.get()
        for n in range(4):
            tk = tp(P, b.t[:, 128 * n:128 * n + 128], D.O[:, c + n, :, :].rearrange("p h x -> p (h x)"), P.ident, t,
                    b.free, inc=n == 3)
        P.ytok[4 + j] = ts(d, P.HB[:, 4 + j, 128 * c:128 * c + 512], b.t[:, :], P.vec("attn_g", j), None, MUL, None, tk,
                           D.hfree)
        P.ps.put(b, P.ytok[4 + j])
    D.ofree = [P.pe.last, P.dve.last]


def shift_mix(P, dst, G, rows, mix, *toks):
    t = tt(P.dve, dst, G.t[0:rows, 0:1024], G.t[0:rows, 1:1025], SUB, *toks)
    return stt(P.dve, dst, dst, mix, G.t[0:rows, 1:1025], MUL, ADD, t)


def block2(P, xtok):
    nc, d = P.nc, P.dve
    I, HB = P.I, P.HB
    P.rate = 2
    P.ytok = [None] * 8
    after = P.everyone()
    with ExitStack() as cx:
        sb = lambda name, shape, t=F: cx.enter_context(nc.sbuf_tensor(name, shape, t))
        D = Prog()
        D.WA, D.GD = sb("r_WA", [64, 1024]), sb("r_GD", [96, 1024])
        D.wl, D.gl = sb("r_wl", [64, 512]), sb("r_gl", [96, 512])
        D.reset, D.pc = sb("r_reset", [128, 512]), sb("r_pc", [128, 8])
        D.S = {}
        for n, w in (("t0", 1), ("t1", 1), ("t2", 1), ("t3", 1), ("t4", 1), ("bon", 1), ("AR", 2), ("BK", 2),
                     ("GB", 2), ("GK", 2), ("AM", 2), ("Xa", 1), ("Xt", 1), ("Vt", 1)):
            D.S[n] = sb("r_" + n, [128, 512 * w])
        D.S["S0"] = sb("r_S0", [128, 576])
        bufs = [Buf(sb(f"r_in{i}", [128, 1024])) for i in range(3)]
        G = Ring([Buf(HB[:, 6, 0:1025]), Buf(HB[:, 7, 0:1025])])
        for b in bufs:
            b.free = [after]
        for b in G.bufs:
            b.free = [mset(P.pool, b.t[:, 0:1], 0.0, after, P.h2store), after]
        D.free, D.hfree = after, [after, P.h2store]
        sem = P.newsem("r_ld")
        dma(P.sp, D.wl[:, :], I["lora_wa"], sem, 16, after)
        lt = dma(P.sp, D.gl[:, :], I["lora_g"], sem, 32, after)
        t = mset(P.pool, D.reset[:, :], 1.0, after)
        D.rtok = mset(P.pool, D.reset[:, :].rearrange("p (c x) -> p c x", x=64)[:, :, 0:1], 0.0, t)
        g = G.get()
        t = project(P, "wa", g, T2, CH2, xtok, 1)
        t = shift_mix(P, D.WA[:, :], g, 64, P.vec("smix", 12)[0:64, :], t, after)
        g.free = [t]
        D.wat = [act(P, D.WA[0:32, :], D.WA[0:32, :], ACT.Tanh, t), lt, t]
        g = G.get()
        t = project(P, "gd", g, T2, CH2, xtok, 1)
        t = shift_mix(P, D.GD[:, :], g, 96, P.vec("smix", 13)[0:96, :], t, after)
        g.free = [t]
        D.gdt = [act(P, D.GD[:, :], D.GD[:, :], ACT.Sigmoid, t), lt]
        D.released = True
        for j in range(4):
            tiles = []
            while not D.released:
                tick(P)
            for n, b in enumerate(bufs):
                g = G.get()
                t = project(P, "rkv", g, T2, CH2, xtok, 1)
                t = shift_mix(P, b.t[:, :], g, 128, P.vec("smix", 4 * n + j), t, b.free)
                g.free = [t]
                tiles.append(Tiled(b, t))
            drain(P)
            D.r, D.k, D.v = tiles
            D.released = False
            P.bg.append(rwkv_pair(P, j, D))
        drain(P)
        P.dbg("rwkv", HB[:, 0:4, 0:1024], P.ytok[0:4])
    after = P.everyone()
    with ExitStack() as cx:
        sb = lambda name, shape, t=F: cx.enter_context(nc.sbuf_tensor(name, shape, t))
        D = Prog()
        D.mask = sb("a_mask", [128, 1024])
        rot = sb("a_rot", [128, 2, 1024])
        D.mx, D.den = sb("a_mx", [128, 16]), sb("a_den", [128, 16])
        D.O, D.OQ = sb("a_O", [128, 8, 2, 64]), sb("a_OQ", [128, 16, 64])
        D.A = Ring([Buf(sb(f"a_A{i}", [128, 1024])) for i in range(2)])
        D.PT = Ring([Buf(sb(f"a_PT{i}", [128, 1024])) for i in range(2)])
        D.VT = Ring([Buf(sb("a_VT", [128, 1024]))])
        ins = [Ring([Buf(sb(f"a_in{i}{n}", [128, 1024])) for n in range(2)]) for i in range(3)]
        rt = Ring([Buf(sb("a_rt", [128, 1024]))])
        for r in ins + [D.A, D.PT, D.VT, rt]:
            for b in r.bufs:
                b.free = [after]
        D.ofree, D.hfree = after, [after, P.h2store]
        sem = P.newsem("a_ld")
        dma(P.sp, D.mask[:, :], I["a_mask"], sem, 16, after)
        rl = dma(P.sp, rot[:, :, :], I["a_rot"], sem, 32, after)
        D.mtok = rl
        for j in range(4):
            tiles = []
            for n in range(3):
                b = ins[n].get()
                pt = []

                def ev(c, c0, cn, ps, t):
                    if n == 0:
                        pt.append(act(P, b.t[:, c0:c0 + cn], ps, ACT.Copy, t, b.free, scale=0.125))
                    else:
                        pt.append(cp(P, b.t[:, c0:c0 + cn], ps, t, b.free))
                    return [pt[-1]]

                dense(P, "aqkv", 8, P.XH, P.XL, xtok, CH2, ev)
                t = pt[-1]
                if n < 2:
                    r = rt.get()
                    for c0, cn in CH2:
                        bk = P.ps.get()
                        t = mm(P, bk.t[:, 0:cn], P.perm, b.t[:, c0:c0 + cn], True, True, pt, P.ctok, bk.free, inc=True)
                        a = tt(d, r.t[:, c0:c0 + cn], bk.t[:, 0:cn], rot[:, 1, c0:c0 + cn], MUL, t, rl, r.free)
                        P.ps.put(bk, a)
                        t = tt(d, b.t[:, c0:c0 + cn], b.t[:, c0:c0 + cn], rot[:, 0, c0:c0 + cn], MUL, a)
                        t = tt(d, b.t[:, c0:c0 + cn], b.t[:, c0:c0 + cn], r.t[:, c0:c0 + cn], ADD, t)
                    r.free = [t]
                tiles.append(Tiled(b, t))
            drain(P)
            D.q, D.k, D.v = tiles
            P.bg.append(attention_pair(P, j, D))
        drain(P)
        P.dbg("attn", HB[:, 4:8, 0:1024], P.ytok[4:8])
    after = P.everyone()
    xfree = P.pe.last
    xtok = [split(P, HB[:, m, 0:T2], P.XH[:, m, 0:T2], P.XL[:, m, 0:T2], P.ytok[m], xfree) for m in range(8)]
    with ExitStack() as cx:
        sb = lambda name, shape, t=F: cx.enter_context(nc.sbuf_tensor(name, shape, t))
        acc, rs = sb("n4_acc", [128, T2]), sb("n4_rs", [128, T2])
        sq = Ring([Buf(sb(f"n4_sq{i}", [128, T2])) for i in range(2)])
        xr = Ring([Buf(sb(f"n4_x{i}", [128, T2])) for i in range(3)])
        for b in sq.bufs + xr.bufs:
            b.free = [after]
        ht = []
        for m in range(8):
            t2 = []
            x, lt = reload(P, xr, m, T2, P.h2, P.h2store)

            def ev(c, c0, cn, ps, t):
                t2.append(tt(d, HB[:, m, c0:c0 + cn], x.t[:, c0:c0 + cn], ps, ADD, t, lt, xtok[m]))
                return [t2[-1]]

            dense(P, "wout2", 8, P.XH, P.XL, xtok, CH2, ev)
            x.free = [t2[-1]]
            ht.append(t2[-1])
        P.xfree = P.pe.last
        P.h3store = [dma(P.pool, P.h3[:, k, :], HB[:, k, 0:T2], P.hsem[k], 48, ht[k]) for k in range(8)]
        P.dbg("h3", HB[:, :, 0:T2], ht)
        xtok = prenorm(P, HB, ht, T2, CH2, "ffn_norm", acc, rs, sq, after)
    after = P.everyone()
    P.hfree = [after, P.h3store]
    htok = ffn(P, ACT.Silu, T2, CH2, xtok, HB, "2", "fconv2", "fcb2", after)
    after = P.everyone()
    with ExitStack() as cx:
        sb = lambda name, shape, t=F: cx.enter_context(nc.sbuf_tensor(name, shape, t))
        acc, rs = sb("n5_acc", [128, T2]), sb("n5_rs", [128, T2])
        sq = Ring([Buf(sb(f"n5_sq{i}", [128, T2])) for i in range(2)])
        xr = Ring([Buf(sb(f"n5_x{i}", [128, T2])) for i in range(3)])
        for b in sq.bufs + xr.bufs:
            b.free = [after]
        st = Stats(P, acc, sq, T2, CH2, after)
        for m in range(8):
            x, lt = reload(P, xr, m, T2, P.h3, P.h3store)
            htok[m] = tt(d, HB[:, m, 0:T2], HB[:, m, 0:T2], x.t[:, 0:T2], ADD, htok[m], lt)
            x.free = [htok[m]]
            st.add(HB[:, m, 0:T2], htok[m])
        t = st.finish(rs, 1024, P.eps6)
        for m in range(8):
            t = stt(d, HB[:, m, 0:T2], HB[:, m, 0:T2], P.vec("final", m), rs[:, 0:T2], MUL, MUL, t)
            P.outs.append(dma(P.sp, P.out[:, m, :], HB[:, m, 0:T2], P.osem, 16 * (m + 1), t))


def reload(P, xr, m, T, src, ready):
    x = xr.get()
    P.xrcount[m % 3] += 16
    return x, dma(P.pool, x.t[:, 0:T], src[:, m, :], P.xrsem[m % 3], P.xrcount[m % 3], x.free, ready)


def build(nc, I, out, dbg=None):
    with ExitStack() as cx:
        sem_count = [0]

        def newsem(name):
            sem_count[0] += 1
            return (name, cx.enter_context(nc.semaphore(name)))

        sb = lambda name, shape, t=F: cx.enter_context(nc.sbuf_tensor(name, shape, t))
        P = Prog()
        P.nc, P.I, P.out, P.newsem = nc, I, out, newsem
        P.pe, P.act, P.dve, P.pool, P.sp = [Queue(newsem(n)) for n in ("s_pe", "s_act", "s_dve", "s_pool", "s_sp")]
        P.everyone = lambda: everyone(P)
        P.bg, P.rate, P.xfree = [], 1, None
        P.xsem = [newsem(f"s_x{i}") for i in range(8)]
        P.hsem = [newsem(f"s_h{i}") for i in range(8)]
        P.xrsem, P.xrcount = [newsem(f"s_xr{i}") for i in range(3)], [0, 0, 0]
        P.osem, P.outs = newsem("s_out"), []
        P.h1 = nc.dram_tensor("h1", [128, 8, T1], F).ap()
        P.h2 = nc.dram_tensor("h2", [128, 8, T2], F).ap()
        P.h3 = nc.dram_tensor("h3", [128, 8, T2], F).ap()
        P.XH, P.XL = sb("XH", [128, 8, T1], R), sb("XL", [128, 8, T1], R)
        P.HB = sb("HB", [128, 8, T1])
        vecs = sb("vecs", [128, NV])
        cst = sb("cst", [128, 1224])
        small = sb("small", [128, 4])
        P.ps = Banks([cx.enter_context(nc.psum_tensor(f"ps{i}", [128, 512], F)) for i in range(8)])
        P.vec = lambda name, i: vecs[:, VCOLS[name][0] + i:VCOLS[name][0] + i + 1]
        csem, vsem = newsem("s_c"), newsem("s_v")
        ct = dma(P.act, cst[:, :], I["cst"], csem, 16)
        P.vtok = dma(P.act, vecs[:, :], I["vecs"], vsem, 16)
        P.ident, P.ones, P.ones64 = cst[:, 0:128], cst[:, 128:256], cst[:, 256:384]
        P.triu_neg, P.perm, P.mtri = cst[:, 384:512], cst[:, 512:640], cst[:, 640:768]
        P.levels = cst[:, 768:1216].rearrange("p (a x) -> p a x", x=64)
        P.mask64, P.mask16 = cst[:, 1216:1218], cst[:, 1218:1220]
        P.sel4 = cst[:, 1220:1224]
        id2 = sb("ident2", [128, 64])
        s4 = sb("sel4", [4, 4, 128])
        P.ident2 = id2
        t = mset(P.pool, small[:, 0:1], 1e-6)
        t2 = mset(P.pool, small[:, 1:2], 64e-5)
        t3 = mset(P.pool, small[:, 2:3], 1.0)
        P.eps6, P.eps64, P.one = small[:, 0:1], small[:, 1:2], small[:, 2:3]
        t4 = vcopy(P.dve, s4[:, :, :], cst[0:4, 1220:1224].unsqueeze(2).broadcast_to([4, 4, 128]), ct)
        P.sel4 = s4
        t5 = tt(P.dve, id2[:, :], P.ident[:, 0:64], P.ident[:, 64:128], ADD, ct)
        P.ctok = [ct, t, t2, t3, t4, t5]
        P.ctok = [ct, t3, t5]
        plan = []
        for name, src, kt in weight_plan(I):
            if dbg is not None and dbg["_stop"] == 1 and plan and plan[-1][0] == "ffn1d" and name == "wa":
                break
            plan.append((name, src, kt))
        raws = [sb(f"w_raw{i}", [128, 1024]) for i in range(2)]
        his = [sb(f"w_hi{i}", [128, 1024], R) for i in range(3)]
        los = [sb(f"w_lo{i}", [128, 1024], R) for i in range(3)]
        P.w = Weights(P, plan, raws, his, los, [newsem(f"s_w{i}") for i in range(2)])
        for _ in range(2):
            P.w.load()
        dsem = []

        def dbg_store(name, ap, toks):
            if dbg is not None and name in dbg:
                s = newsem("s_dbg_" + name)
                dma(P.pool, dbg[name], ap, s, 16, *[t for t in toks])
                for q in (P.pool, P.act, P.dve, P.pe):
                    q.wait((s[0], s[1], 16))
                P.pool.do(lambda e: e.memset(small[:, 3:4], 0.0))

        P.dbg = dbg_store
        stop = dbg.get("_stop") if dbg is not None else None
        xtok = block1(P)
        if stop != 1:
            block2(P, xtok)
        for t in P.outs + P.h1store + P.h2store + (P.h3store if stop != 1 else []):
            P.sp.wait(t)
        block = cx.enter_context(nc.Block())

        @block.sync
        def _(eng):
            P.sp.play(eng)

        @block.gpsimd
        def _(eng):
            P.pool.play(eng)

        @block.scalar
        def _(eng):
            P.act.play(eng)

        @block.vector
        def _(eng):
            P.dve.play(eng)

        @block.tensor
        def _(eng):
            P.pe.play(eng)


def weight_plan(I):
    for m in range(4):
        yield "u", I["w_u"][m], 8
    for m in range(4):
        yield "glu", I["w_glu"][m], 4
    yield "gates", I["w_gates"][0], 8
    for h in range(4):
        for n, name in enumerate("qkv"):
            yield name, I["w_qkvo"][4 * n + h], 8
    for m in range(4):
        yield "o", I["w_qkvo"][12 + m], 8
    for m in range(8):
        yield "ga", I["w_g"][m], 8
        yield "wa", I["w_a"][m], 4
        yield "gb", I["w_g"][8 + m], 8
        yield "wb", I["w_b"][m], 4
    for m in range(8):
        yield "wout", I["w_out"][m], 8
    yield from ffn_plan(I, "1")
    yield "wa", I["w2_wa"][0], 8
    yield "gd", I["w2_gd"][0], 8
    for j in range(4):
        for n in range(3):
            yield "rkv", I["w2_rkv"][4 * n + j], 8
    for j in range(4):
        for n in range(3):
            yield "aqkv", I["w2_attn"][4 * n + j], 8
    for m in range(8):
        yield "wout2", I["w2_out"][m], 8
    yield from ffn_plan(I, "2")


def ffn_plan(I, tag):
    for f0, nf in FQ:
        for f in range(f0, f0 + nf):
            yield "ffn" + tag + "g", I["f_gate" + tag][f], 8
            yield "ffn" + tag + "u", I["f_up" + tag][f], 8
        for m in range(8):
            yield "ffn" + tag + "d", I["f_down" + tag][m][:, f0 * 128:(f0 + nf) * 128], nf


def constants():
    p = np.arange(128)
    c = np.zeros((128, 1224), np.float32)
    c[:, 0:128] = np.eye(128)
    c[:, 128:256] = 1.0
    c[:, 256:384] = (p[:, None] // 64) == (p[None, :] // 64)
    c[:, 384:512] = np.where(p[:, None] <= p[None, :], 0.0, -1e30)
    perm = np.zeros((128, 128), np.float32)
    for i in range(128):
        r = i % 64
        if r < 8:
            perm[i + 8, i] = -1.0
        elif r < 16:
            perm[i - 8, i] = 1.0
    c[:, 512:640] = perm
    s, t = (p % 64)[:, None], np.arange(64)[None, :]
    c[:, 640:704] = s < t
    c[:, 704:768] = s <= t
    level = lambda b, r, q: ((r // b) % 2 == 1) & ((q // b) == (r // b) - 1)
    c[:, 768:832] = level(1, s, t)
    c[:, 832:896] = level(1, t, s)
    for n, b in enumerate((2, 4, 8, 16, 32)):
        c[:, 896 + 64 * n:960 + 64 * n] = level(b, s, t)
    c[:, 1216], c[:, 1217] = p < 64, p >= 64
    c[:, 1218], c[:, 1219] = (p // 16) % 2 == 0, (p // 16) % 2 == 1
    c[0:4, 1220:1224] = np.eye(4)
    half = 8
    inv = (np.float32(500000.0) ** (-np.arange(half, dtype=np.float32) * np.float32(2.0) / np.float32(16))).astype(np.float32)
    ang = np.arange(1024, dtype=np.float32)[:, None] * inv[None, :]
    rot = np.zeros((128, 2, 1024), np.float32)
    rot[:, 0, :] = 1.0
    for i in range(128):
        if i % 64 < 16:
            rot[i, 0], rot[i, 1] = np.cos(ang[:, i % 8]), np.sin(ang[:, i % 8])
    mask = np.zeros((128, 8, 128), np.float32)
    for b in range(8):
        dist = 128 * (7 - b) + p[:, None] - p[None, :]
        n = ((dist >= 0) & (dist <= 128)).astype(int) + ((dist >= 0) & (dist <= 512) & (dist % 4 == 0)) \
            + ((dist >= 0) & (dist % 16 == 0))
        mask[:, b] = np.where(n > 0, np.log(np.maximum(n, 1)), -1e30)
    return c, rot, mask.reshape(128, 1024)


def layout(i):
    g = {n: np.asarray(a)[0] if np.asarray(a).ndim > 1 and n not in ("meta_tokens",) else np.asarray(a)
         for n, a in i.items()}
    o = {}
    x = np.concatenate([g["meta_tokens"], g["x"]], axis=0)
    cm = lambda a: np.ascontiguousarray(a.T.reshape(8, 128, -1).transpose(1, 0, 2))
    o["x1"] = cm(x)

    def wt(w, n=None):
        k, m = w.shape
        return np.ascontiguousarray(w.reshape(k // 128, 128, m // 128, 128).transpose(2, 1, 0, 3).reshape(m // 128, 128, k))

    def pad(parts):
        out = np.zeros((1024, 128), np.float32)
        for at, a in parts:
            out[:, at:at + a.shape[1]] = a
        return out

    w = g["w_in"]
    o["w_u"] = wt(w[:, 0:512])
    o["w_qkvo"] = wt(w[:, 512:2560])
    o["w_gates"] = wt(pad([(0, w[:, 2560:2564]), (32, w[:, 2564:2568])]))
    o["w_g"] = wt(w[:, 2568:4616])
    o["w_glu"], o["w_a"], o["w_b"] = wt(g["w_ssm_glu"]), wt(g["w_branch_ssm"]), wt(g["w_branch_mlstm"])
    o["w_out"] = wt(g["w_out"])
    o["f_gate1"], o["f_up1"], o["f_down1"] = wt(g["w_ffn_gate"]), wt(g["w_ffn_up"]), wt(g["w_ffn_down"])
    w = g["w_in_2"]
    o["w2_rkv"] = wt(w[:, 0:1536])
    o["w2_wa"] = wt(pad([(0, w[:, 1536:1600])]))
    o["w2_gd"] = wt(pad([(0, w[:, 1600:1696])]))
    o["w2_attn"] = wt(w[:, 1696:3232])
    o["w2_out"] = wt(g["w_out_2"])
    o["f_gate2"], o["f_up2"] = wt(g["w_ffn_up_2"][:, 0:2816]), wt(g["w_ffn_up_2"][:, 2816:5632])
    o["f_down2"] = wt(g["w_ffn_down_2"])
    o["lora_wa"] = np.concatenate([g["w_lora_up_2"], g["a_lora_up_2"]], axis=0)
    o["lora_g"] = np.ascontiguousarray(g["g_lora_up_2"])
    v = np.zeros((128, NV), np.float32)

    def put(name, a, off=0):
        a = np.asarray(a).reshape(-1)
        n = a.shape[0] // 128
        at = VCOLS[name][0] + off
        v[:, at:at + n] = a.reshape(n, 128).T

    for name, src in (("g_mix_pre", "g_mix_pre"), ("g_mix_post", "g_mix_post"), ("bqk", "b_qk_conv"),
                      ("g_head", "g_head_norm"), ("ssm_d", "ssm_d"), ("g_ffn_pre", "g_ffn_pre"),
                      ("g_ffn_post", "g_ffn_post"), ("fcb", "b_ffn_conv"), ("mix_norm", "mix_norm_gain_2"),
                      ("w0", "w0_2"), ("a0", "a0_2"), ("k_k", "k_k_2"), ("k_a", "k_a_2"), ("r_k", "r_k_2"),
                      ("ln_w", "ln_x_w_2"), ("ln_b", "ln_x_b_2"), ("attn_g", "attn_norm_gain_2"),
                      ("ffn_norm", "ffn_norm_gain_2"), ("fcb2", "ffn_conv_b_2"), ("final", "final_norm_gain_2")):
        put(name, g[src])
    put("wqk", g["w_qk_conv"].reshape(4, 8, 128).transpose(1, 0, 2))
    put("fconv", g["w_ffn_conv"].reshape(3, 22, 128).transpose(1, 0, 2))
    put("fconv2", g["ffn_conv_w_2"].reshape(3, 22, 128).transpose(1, 0, 2))
    at = VCOLS["bgate"][0]
    v[0:4, at], v[32:36, at] = g["b_gates"][0:4], g["b_gates"][4:8]
    sm = g["rwkv_shift_mix_2"]
    put("smix", sm[0:1536])
    at = VCOLS["smix"][0]
    v[0:64, at + 12], v[0:96, at + 13] = sm[1536:1600], sm[1600:1696]
    o["vecs"] = v
    lr, li, ld = g["ssm_lambda_re"], g["ssm_lambda_im"], g["ssm_log_dt"]
    bre, bim, cre, cim = g["ssm_b_re"], g["ssm_b_im"], g["ssm_c_re"], g["ssm_c_im"]
    ldt = np.repeat(ld[:, None], 64, axis=1)
    one = lambda a: a.reshape(16, 2, 64).transpose(1, 2, 0).reshape(128, 16)
    o["ssm_p1"] = np.stack([one(lr), one(li), one(ldt)], axis=1)
    o1 = lambda a: a.reshape(16, 2, 64, 16).transpose(1, 2, 0, 3).reshape(128, 16, 16)
    o["ssm_bc1"] = np.stack([o1(bre), o1(bim), o1(cre.transpose(0, 2, 1)), o1(cim.transpose(0, 2, 1))], axis=1)
    rep = lambda a: np.repeat(a.reshape(4, 8, 1, 64), 16, axis=2).transpose(1, 2, 0, 3).reshape(128, 256)
    o2 = lambda a: a.transpose(0, 2, 1).reshape(4, 8, 16, 64).transpose(1, 2, 0, 3).reshape(128, 256)
    o["ssm_p2"] = np.stack([rep(lr), rep(li), rep(ldt), o2(bre), o2(bim)], axis=1)
    o["cst"], o["a_rot"], o["a_mask"] = constants()
    return {n: np.ascontiguousarray(a) for n, a in o.items()}


def kernel(**inputs):
    import concourse.bacc as _bacc
    from concourse.bass_utils import run_bass_kernel_spmd as _run

    nc = _bacc.Bacc("TRN2", target_bir_lowering=False, num_devices=1)
    arrays = {"in_" + n: a for n, a in layout(inputs).items()}
    I = {n[3:]: nc.dram_tensor(n, a.shape, mybir.dt.from_np(a.dtype), kind="ExternalInput").ap()
         for n, a in arrays.items()}
    out = nc.dram_tensor("out", (128, 8, 1024), F, kind="ExternalOutput").ap()
    build(nc, I, out)
    r = _run(nc, [arrays], core_ids=[0])
    y = r.results[0]["out"]
    return np.ascontiguousarray(y.transpose(2, 1, 0).reshape(1, 1024, 1024))
```

```python
from contextlib import ExitStack

import numpy as np
import concourse.bass as bass
from concourse import mybir

F = mybir.dt.float32
R = mybir.dt.float32r
ALU = mybir.AluOpType
ACT = mybir.ActivationFunctionType
AX_X = mybir.AxisListType.X
MUL, ADD, SUB, MAX, MIN = ALU.mult, ALU.add, ALU.subtract, ALU.max, ALU.min

T1 = 1040
CH1 = [(0, 352), (352, 344), (696, 344)]
T2 = 1024
CH2 = [(0, 512), (512, 512)]
TT1 = [(128 * i, min(128, T1 - 128 * i)) for i in range(9)]
NB = 130
FQ = [(0, 6), (6, 6), (12, 5), (17, 5)]
MAGIC = 12582912.0
TWO_PI_HI = 6.28125
TWO_PI_LO = 0.0019353071795864769

LAG, K0, K1, K2, K3, RS, RM, NG, K4, PN, PA, Q1, Q2, Q3, Q4, Q5, QP = 20, 1, 6, 12, 7, 3, 5, 7, 30, 2, 3, 1, 1, 1, 1, 1, 3
VCOLS = {}


def _vec_layout():
    at = 0
    for name, n in (("g_mix_pre", 8), ("g_mix_post", 8), ("wqk", 32), ("bqk", 8), ("bgate", 1), ("g_head", 4),
                    ("ssm_d", 4), ("g_ffn_pre", 8), ("g_ffn_post", 8), ("fconv", 66), ("fcb", 22),
                    ("mix_norm", 8), ("smix", 14), ("w0", 4), ("a0", 4), ("k_k", 4), ("k_a", 4), ("r_k", 4),
                    ("ln_w", 4), ("ln_b", 4), ("attn_g", 4), ("ffn_norm", 8), ("fconv2", 66), ("fcb2", 22),
                    ("final", 8)):
        VCOLS[name] = (at, n)
        at += n
    return at


NV = _vec_layout()


class Queue:

    def __init__(self, sem):
        self.sem, self.n, self.ops, self.seen, self.last = sem, 0, [], {}, None

    def wait(self, *toks):
        for t in toks:
            if t is None:
                continue
            if isinstance(t, dict):
                t = list(t.values())
            if isinstance(t, list):
                self.wait(*t)
                continue
            key, sem, v = t
            if self.seen.get(key, 0) < v:
                self.seen[key] = v
                self.ops.append((0, sem, v))

    def do(self, fn, *toks, inc=True):
        self.wait(*toks)
        if not inc:
            self.ops.append((1, fn, None))
            return None
        self.n += 1
        self.ops.append((1, fn, self.sem))
        self.last = (self.sem[0], self.sem[1], self.n)
        return self.last

    def play(self, eng):
        for kind, a, b in self.ops:
            if kind == 0:
                eng.wait_ge(a, b)
            elif kind == 2:
                a(eng).then_inc(b, 16)
            elif b is None:
                a(eng)
            else:
                a(eng).then_inc(b[1], 1)


class Buf:

    def __init__(self, t):
        self.t, self.free = t, []


class Ring:
    def __init__(self, bufs):
        self.bufs, self.i = bufs, 0

    def get(self):
        b = self.bufs[self.i % len(self.bufs)]
        self.i += 1
        return b


class Banks:

    def __init__(self, tensors):
        self.idle = [Buf(t) for t in tensors]

    def get(self):
        assert self.idle
        return self.idle.pop(0)

    def put(self, b, *toks):
        b.free = [t for t in toks if t is not None]
        self.idle.append(b)


class Prog:
    pass


def dma(q, out, src, sem, count, *toks):
    q.wait(*toks)
    q.ops.append((2, lambda e: e.dma_start(out, src), sem[1]))
    return (sem[0], sem[1], count)


def mm(P, out, a, b, start, stop, *toks, inc=False, skip=False):
    if skip:
        return P.pe.do(lambda e: e.matmul(out, a, b, start=start, stop=stop, skip_group_check=True), *toks, inc=inc)
    return P.pe.do(lambda e: e.matmul(out, a, b, start=start, stop=stop), *toks, inc=inc)


def tp(P, out, src, ident, *toks, inc=False):
    return P.pe.do(lambda e: e.transpose(out, src, ident), *toks, inc=inc)


def act(P, out, src, func, *toks, bias=None, scale=None, acc=None):
    kw = {}
    if bias is not None:
        kw["bias"] = bias
    if scale is not None:
        kw["scale"] = scale
    if acc is not None:
        kw["accum_out"] = acc
    return P.act.do(lambda e: e.activation(out, src, func, **kw), *toks)


def cp(P, out, src, *toks):
    return act(P, out, src, ACT.Copy, *toks)


def tt(q, out, a, b, op, *toks):
    return q.do(lambda e: e.tensor_tensor(out, a, b, op), *toks)


def ts(q, out, a, s1, s2, op0, op1, *toks):
    if op1 is None:
        return q.do(lambda e: e.tensor_scalar(out, a, s1, None, op0), *toks)
    return q.do(lambda e: e.tensor_scalar(out, a, s1, s2, op0, op1), *toks)


def stt(q, out, a, s, b, op0, op1, *toks):
    return q.do(lambda e: e.scalar_tensor_tensor(out=out, in0=a, scalar=s, in1=b, op0=op0, op1=op1), *toks)


def recip(P, out, src, *toks):
    return P.dve.do(lambda e: e.reciprocal(out, src), *toks)


def vcopy(q, out, src, *toks):
    return q.do(lambda e: e.tensor_copy(out, src), *toks)


def reduce(P, out, src, op, *toks, negate=False):
    return P.dve.do(lambda e: e.tensor_reduce(out, src, AX_X, op, negate=negate), *toks)


def mset(q, out, v, *toks):
    return q.do(lambda e: e.memset(out, v), *toks)


def split(P, src, hi, lo, *toks):
    t = cp(P, hi, src, *toks)
    return tt(P.dve, lo, src, hi.bitcast(F), SUB, t, *toks)


def everyone(P):
    return [q.last for q in (P.pe, P.act, P.dve, P.pool)]


class Weights:

    def __init__(self, P, plan, raws, his, los, sems):
        self.P, self.plan, self.raws, self.his, self.los, self.sems = P, plan, raws, his, los, sems
        self.loads = self.splits = self.used = 0
        self.raw_tok, self.split_tok, self.done_tok = {}, {}, {}

    def load(self):
        i = self.loads
        if i >= len(self.plan):
            return
        self.loads += 1
        name, src, kt = self.plan[i]
        s = i % len(self.raws)
        free = self.split_tok[i - len(self.raws)] if i >= len(self.raws) else None
        self.raw_tok[i] = dma(self.P.sp, self.raws[s][:, 0:kt * 128], src, self.sems[s],
                              16 * (i // len(self.raws) + 1), free)

    def split(self):
        i = self.splits
        if i >= len(self.plan):
            return
        self.splits += 1
        kt = self.plan[i][2]
        raw = self.raws[i % len(self.raws)][:, 0:kt * 128]
        s = i % len(self.his)
        free = self.done_tok[i - len(self.his)] if i >= len(self.his) else None
        self.split_tok[i] = split(self.P, raw, self.his[s][:, 0:kt * 128], self.los[s][:, 0:kt * 128],
                                  self.raw_tok[i], free)
        self.load()

    def use(self, name):
        i = self.used
        assert self.plan[i][0] == name, (self.plan[i][0], name)
        self.used += 1
        while self.splits < min(i + len(self.his), len(self.plan)):
            self.split()
        kt = self.plan[i][2]
        s = i % len(self.his)
        shape = lambda t: t[:, 0:kt * 128].rearrange("p (k n) -> p k n", k=kt)
        return i, shape(self.his[s]), shape(self.los[s]), self.split_tok[i]

    def done(self, i, tok):
        self.done_tok[i] = tok


def tick(P, n=1):
    for _ in range(n):
        if P.bg:
            if next(P.bg[0], "end") == "end":
                P.bg.pop(0)


def drain(P):
    while P.bg:
        tick(P)


def dense(P, name, kt, xh, xl, xtok, chunks, evac):
    i, wh, wl, wt = P.w.use(name)
    for c, (c0, cn) in enumerate(chunks):
        b = P.ps.get()
        t = None
        for k in range(kt):
            xs = (xh[:, k, c0:c0 + cn], xl[:, k, c0:c0 + cn])
            for n, (a, x) in enumerate(((wh, xs[0]), (wh, xs[1]), (wl, xs[0]))):
                last = k == kt - 1 and n == 2
                xt = xtok[k][c] if isinstance(xtok[k], dict) else xtok[k]
                t = mm(P, b.t[:, 0:cn], a[:, k, :], x, k == 0 and n == 0, last, wt, xt, b.free, inc=last)
        if c == len(chunks) - 1:
            P.w.done(i, t)
        P.ps.put(b, *evac(c, c0, cn, b.t[:, 0:cn], t))
        tick(P, P.rate)


class Stats:

    def __init__(self, P, acc, sq, T, chunks, free):
        self.P, self.acc, self.sq, self.T, self.chunks = P, acc[:, 0:T], sq, T, chunks
        self.n, self.tok, self.free = 0, None, free

    def add(self, x, *toks):
        P = self.P
        if self.n == 0:
            self.tok = tt(P.dve, self.acc, x, x, MUL, self.free, *toks)
        else:
            b = self.sq.get()
            t = act(P, b.t[:, 0:self.T], x, ACT.Square, b.free, *toks)
            self.tok = tt(P.dve, self.acc, self.acc, b.t[:, 0:self.T], ADD, t, self.tok)
            b.free = [self.tok]
        self.n += 1

    def finish(self, rstd, count, eps):
        P = self.P
        toks = []
        for c0, cn in self.chunks:
            b = P.ps.get()
            t = mm(P, b.t[:, 0:cn], P.ones, self.acc[:, c0:c0 + cn], True, True, self.tok, P.ctok, b.free, inc=True)
            t = act(P, rstd[:, c0:c0 + cn], b.t[:, 0:cn], ACT.Sqrt, t, bias=eps, scale=1.0 / count)
            P.ps.put(b, t)
            toks.append(recip(P, rstd[:, c0:c0 + cn], rstd[:, c0:c0 + cn], t))
        return toks[-1]


def ffn(P, kind, T, chunks, xtok, H, tag, vconv, vcb, after, rs, res=None):
    htok = [None] * 8
    wname = "ffn" + tag
    with ExitStack() as cx:
        PH = cx.enter_context(P.nc.sbuf_tensor("PH" + tag, [128, 6, T], R))
        PL = cx.enter_context(P.nc.sbuf_tensor("PL" + tag, [128, 6, T], R))
        gs = Ring([Buf(cx.enter_context(P.nc.sbuf_tensor(f"G{tag}{i}", [128, T + 2], F))) for i in range(2)])
        cs = Ring([Buf(cx.enter_context(P.nc.sbuf_tensor(f"C{tag}{i}", [128, T], F))) for i in range(2)])
        for b in gs.bufs:
            b.free = [mset(P.pool, b.t[:, 0:2], 0.0, after)]
        for b in cs.bufs:
            b.free = [after]
        pfree = [after] * 6
        for f0, nf in FQ:
            ptok = [None] * nf
            for f in range(f0, f0 + nf):
                g, cbuf = gs.get(), cs.get()
                gt = []

                def ev_gate(c, c0, cn, ps, t):
                    gt.append(cp(P, g.t[:, 2 + c0:2 + c0 + cn], ps, t, g.free))
                    return [gt[-1]]

                dense(P, wname + "g", 8, P.XH, P.XL, xtok, chunks, ev_gate)
                w = lambda j: P.vec(vconv, 3 * f + j)
                t = ts(P.dve, cbuf.t[:, :], g.t[:, 2:2 + T], w(2), P.vec(vcb, f), MUL, ADD, gt, cbuf.free)
                t = stt(P.dve, cbuf.t[:, :], g.t[:, 1:1 + T], w(1), cbuf.t[:, :], MUL, ADD, t)
                t = stt(P.dve, cbuf.t[:, :], g.t[:, 0:T], w(0), cbuf.t[:, :], MUL, ADD, t)
                g.free = [t]
                ta = act(P, cbuf.t[:, :], cbuf.t[:, :], kind, t)
                ut = []

                def ev_up(c, c0, cn, ps, t):
                    ut.append(tt(P.dve, cbuf.t[:, c0:c0 + cn], cbuf.t[:, c0:c0 + cn], ps, MUL, t, ta))
                    return [ut[-1]]

                dense(P, wname + "u", 8, P.XH, P.XL, xtok, chunks, ev_up)
                k = f - f0
                ptok[k] = split(P, cbuf.t[:, :], PH[:, k, :], PL[:, k, :], ut, pfree[k])
                cbuf.free = [ptok[k]]
            if f0 == FQ[-1][0]:
                st = Stats(P, rs, Ring(gs.bufs), T, chunks, after)
                xr = Ring(cs.bufs)
            for m in range(8):
                def ev_down(c, c0, cn, ps, t):
                    if f0 == 0:
                        htok[m] = cp(P, H[:, m, c0:c0 + cn], ps, t, P.hfree)
                    else:
                        htok[m] = tt(P.dve, H[:, m, c0:c0 + cn], H[:, m, c0:c0 + cn], ps, ADD, t, htok[m])
                    return [htok[m]]

                dense(P, wname + "d", nf, PH, PL, ptok, chunks, ev_down)
                if f0 == FQ[-1][0]:
                    if res is not None:
                        x, lt = reload(P, xr, m, T, *res)
                        htok[m] = tt(P.dve, H[:, m, 0:T], H[:, m, 0:T], x.t[:, 0:T], ADD, htok[m], lt)
                        x.free = [htok[m]]
                    st.add(H[:, m, 0:T], htok[m])
            last = P.pe.last
            pfree = [last] * 6
        P.xfree = P.pe.last
        t = st.finish(rs, 1024, P.eps6)
    return htok, t


def helper(P, m, every):
    return P.pool if m % every == every - 1 else P.dve


def splits(P, srcs, hi, lo, chunks, toks, *free):
    out = [{} for _ in srcs]
    for c, (c0, cn) in enumerate(chunks):
        for k, src in enumerate(srcs):
            h = cp(P, hi[:, k, c0:c0 + cn], src[:, c0:c0 + cn], toks[k], *free)
            l = tt(helper(P, k, 2), lo[:, k, c0:c0 + cn], src[:, c0:c0 + cn], hi[:, k, c0:c0 + cn].bitcast(F), SUB, h,
                   toks[k], *free)
            out[k][c] = [h, l]
    return out


def normalise(P, H, rs, rt, c, c0, cn, gname, tmp, out, free):
    for k in range(8):
        b = tmp.get()
        a = stt(P.dve, b.t[:, 0:cn], H[:, k, c0:c0 + cn], P.vec(gname, k), rs[:, c0:c0 + cn], MUL, MUL, rt, b.free,
                P.vtok)
        hi = P.XH[:, k, c0:c0 + cn]
        h = cp(P, hi, b.t[:, 0:cn], a, free)
        lo = tt(helper(P, k, PN), P.XL[:, k, c0:c0 + cn], b.t[:, 0:cn], hi.bitcast(F), SUB, h, a)
        b.free = [lo]
        out[k][c] = [h, lo]


def renorm(P, H, rs, t, gname, X, T, chunks, gnext, rs2, tmp, free):
    ht, out = [[] for _ in range(8)], [{} for _ in range(8)]
    rt = [None] * len(chunks)

    def add(c, c0, cn):
        bk = P.ps.get()
        for m in range(8):
            x, lt = X[m]
            h = H[:, m, c0:c0 + cn]
            a = stt(P.dve, h, h, P.vec(gname, m), rs[:, c0:c0 + cn], MUL, MUL, t)
            a = tt(helper(P, m, PA), h, h, x[:, c0:c0 + cn], ADD, a, lt)
            ht[m].append(a)
            s = tmp.get()
            a = act(P, s.t[:, 0:cn], h, ACT.Square, a, s.free)
            a = mm(P, bk.t[:, 0:cn], P.ones, s.t[:, 0:cn], m == 0, m == 7, a, P.ctok, bk.free, inc=True)
            s.free = [a]
        a = act(P, rs2[:, c0:c0 + cn], bk.t[:, 0:cn], ACT.Sqrt, a, bias=P.eps6, scale=1.0 / 1024)
        P.ps.put(bk, a)
        rt[c] = recip(P, rs2[:, c0:c0 + cn], rs2[:, c0:c0 + cn], a)

    for c in range(len(chunks)):
        add(c, *chunks[c])
        if c:
            normalise(P, H, rs2, rt[c - 1], c - 1, *chunks[c - 1], gnext, tmp, out, free)
    normalise(P, H, rs2, rt[-1], len(chunks) - 1, *chunks[-1], gnext, tmp, out, free)
    return ht, out


def cmul(q, outr, outi, ar, ai, br, bi, t1, t2, *toks):
    tt(q, outr, ar, br, MUL, *toks)
    a = tt(q, t1, ai, bi, MUL)
    tt(q, outi, ar, bi, MUL)
    b = tt(q, t2, ai, br, MUL)
    tt(q, outr, outr, t1, SUB, a)
    return tt(q, outi, outi, t2, ADD, b)


def pause(n):
    for _ in range(n):
        yield


def discretise(P, lr, li, ldt, s, *toks):
    d = P.dve
    dt, mag, kc, cs, sn, ar, ai, den, zr, zi = s
    t0 = act(P, dt, ldt, ACT.Exp, *toks)
    yield
    t = tt(d, den, lr, dt, MUL, t0)
    tm = act(P, mag, den, ACT.Exp, t)
    t = tt(d, ar, li, dt, MUL, t0)
    for out, shift, back in ((sn, 0.0, 0.0), (cs, 0.25, 1.5707963267948966)):
        k = ts(d, kc, ar, 1.0 / (2.0 * np.pi), shift, MUL, ADD, t)
        k = ts(d, kc, kc, MAGIC, None, ADD, None, k)
        k = ts(d, kc, kc, -MAGIC, None, ADD, None, k)
        k2 = stt(d, out, kc, -TWO_PI_HI, ar, MUL, ADD, k)
        k2 = stt(d, out, kc, -TWO_PI_LO, out, MUL, ADD, k2)
        k2 = ts(d, out, out, back, None, ADD, None, k2)
        k2 = ts(d, out, out, 3.1415925, -3.1415925, MIN, MAX, k2)
        t = act(P, out, out, ACT.Sin, k2)
        yield
    t = tt(d, ar, mag, cs, MUL, t, tm)
    t = tt(d, ai, mag, sn, MUL, t)
    a = tt(d, den, lr, lr, MUL, t)
    b = tt(d, kc, li, li, MUL, t)
    a = tt(d, den, den, kc, ADD, a, b)
    rd = recip(P, den, den, a)
    n = ts(d, dt, ar, -1.0, None, ADD, None, t, t0)
    a = tt(d, zr, dt, lr, MUL, n)
    b = tt(d, kc, ai, li, MUL, n)
    a = tt(d, zr, zr, kc, ADD, a, b)
    a = tt(d, zr, zr, den, MUL, a, rd)
    b = tt(d, zi, ai, lr, MUL, a)
    c = tt(d, kc, dt, li, MUL, b)
    b = tt(d, zi, zi, kc, SUB, b, c)
    b = tt(d, zi, zi, den, MUL, b)
    yield
    return mag, cs, sn, ar, ai, zr, zi, b


def ssm(P, U, free, VX, gate, ytok):
    nc, d = P.nc, P.dve
    after = None
    with ExitStack() as cx:
        sb = lambda name, shape: cx.enter_context(nc.sbuf_tensor(name, shape, F))
        p1 = sb("ssm_p1", [128, 3, 16])
        s1 = sb("ssm_s1", [128, 10, 16])
        bc1 = sb("ssm_bc1", [128, 4, 16, 16])
        bb1 = sb("ssm_bb1", [128, 2, 256])
        q1 = sb("ssm_q1", [128, 2, 256])
        Bn = sb("ssm_Bn", [128, 2, 16, 2, 16])
        a2 = sb("ssm_a2", [128, 2, 256])
        bb2 = sb("ssm_bb2", [128, 2, 256])
        E = free.rearrange("p (r q c) -> p r q c", r=2, q=16)
        e8 = sb("ssm_e8", [128, 4, 16])
        r8 = sb("ssm_r8", [128, 16])
        Bop = sb("ssm_Bop", [128, 16, 2, 64])
        W = sb("ssm_W", [128, 9, 2, 64])
        Cop = sb("ssm_Cop", [128, 72, 2, 16])
        Dop = sb("ssm_Dop", [128, 8, 128])
        bt_ = sb("ssm_BT", [128, 4 * 4 * NB])
        BU = bt_[:, 0:8 * NB].rearrange("p (r c) -> p r c", r=2)
        tq = bt_[:, 8 * NB:16 * NB].rearrange("p (r c) -> p r c", r=2)
        p2 = bt_[:, 0:1280].rearrange("p (a c) -> p a c", a=5)
        q2 = Bop[:, :, :, :].rearrange("p a b c -> p (a b c)").rearrange("p (r c) -> p r c", r=2)
        pw = W[:, 0:8, :, :]
        s2 = Cop[:, :, :, :].rearrange("p a b c -> p (a b c)").rearrange("p (r c) -> p r c", r=9)
        V = VX[:, 0:8 * NB].rearrange("p (r c) -> p r c", r=2)
        Rk = sb("ssm_R", [128, 4 * NB])
        X = VX[:, :].rearrange("p (r q c) -> p r q c", r=2, q=4)
        sem = P.newsem("ssm")
        dz = mset(P.pool, Dop[:, :, :], 0.0)
        dma(P.sp, p1[:, :, :], P.I["ssm_p1"], sem, 16, after)
        dma(P.sp, bc1[:, :, :, :], P.I["ssm_bc1"], sem, 32)
        ld = dma(P.sp, p2, P.I["ssm_p2"], sem, 48)
        yield
        s = [s1[:, i, :] for i in range(10)]
        mag1, c1, n1, ar1, ai1, zr1, zi1, t1 = yield from discretise(P, p1[:, 0, :], p1[:, 1, :], p1[:, 2, :], s, ld, after)
        s = [s2[:, i, :] for i in range(5)] + [a2[:, 0, :], a2[:, 1, :]] + [s2[:, i, :] for i in range(5, 8)]
        _, _, _, ar2, ai2, zr2, zi2, t2 = yield from discretise(P, p2[:, 0, :], p2[:, 1, :], p2[:, 2, :], s, ld, after)
        t2 = cmul(d, bb2[:, 0, :], bb2[:, 1, :], zr2, zi2, p2[:, 3, :], p2[:, 4, :], q1[:, 0, :], q1[:, 1, :], t2)
        b16 = lambda a: a.unsqueeze(2).broadcast_to([128, 16, 16])
        sq = lambda a: a.rearrange("p (q h) -> p q h", h=16)
        t1 = cmul(d, sq(bb1[:, 0, :]), sq(bb1[:, 1, :]), b16(zr1), b16(zi1), bc1[:, 0], bc1[:, 1],
                  sq(q1[:, 0, :]), sq(q1[:, 1, :]), t1, t2)
        for ri in range(2):
            for gg in range(2):
                t1 = ts(d, Bn[:, ri, :, gg, :], sq(bb1[:, ri, :]), P.mask64[:, gg:gg + 1], None, MUL, None, t1, P.ctok)
        yield
        t = t1
        cur = (c1, n1)
        for i in range(3):
            nxt = (e8[:, 2 * (i % 2), :], e8[:, 2 * (i % 2) + 1, :])
            t = cmul(d, nxt[0], nxt[1], cur[0], cur[1], cur[0], cur[1], q2[:, 0, 0:16], q2[:, 1, 0:16], t)
            cur = nxt
        m = tt(d, r8[:, :], mag1, mag1, MUL, t)
        m = tt(d, r8[:, :], r8[:, :], r8[:, :], MUL, m)
        m = tt(d, r8[:, :], r8[:, :], r8[:, :], MUL, m)
        yield
        while gate.free is None:
            yield
        ta = mset(d, E[:, 0, :, 0:1], 1.0, gate.free)
        tb = mset(d, E[:, 1, :, 0:1], 0.0, gate.free)
        t = tb
        n, which = 1, 0
        while n < NB:
            k = min(n, NB - n)
            bc = lambda a: a.unsqueeze(2).broadcast_to([128, 16, k])
            qa = q2[:, 0, 0:16 * k].rearrange("p (q c) -> p q c", c=k)
            qb = q2[:, 1, 0:16 * k].rearrange("p (q c) -> p q c", c=k)
            t = cmul(d, E[:, 0, :, n:n + k], E[:, 1, :, n:n + k], E[:, 0, :, 0:k], E[:, 1, :, 0:k],
                     bc(cur[0]), bc(cur[1]), qa, qb, t, ta, m)
            n += k
            if n < NB:
                i = 1 if which else 0
                nxt = (e8[:, 2 * (1 - i), :], e8[:, 2 * (1 - i) + 1, :])
                t = cmul(d, nxt[0], nxt[1], cur[0], cur[1], cur[0], cur[1], q2[:, 0, 0:16], q2[:, 1, 0:16], t)
                cur, which = nxt, not which
            yield
        setup = t
        peB, peC, peX = setup, setup, after
        for j in range(4):
            a64r, a64i = ar2[:, 64 * j:64 * j + 64], ai2[:, 64 * j:64 * j + 64]
            t = vcopy(d, pw[:, 7, :, :], bb2[:, :, 64 * j:64 * j + 64], t2, setup)
            for tau in range(6, -1, -1):
                t = cmul(d, pw[:, tau, 0, :], pw[:, tau, 1, :], pw[:, tau + 1, 0, :], pw[:, tau + 1, 1, :],
                         a64r, a64i, q1[:, 0, 0:64], q1[:, 1, 0:64], t)
                yield
            pv = pw.rearrange("p a b c -> p (a b) c")
            for gg in range(2):
                bt = ts(P.pool, Bop[:, :, gg, :], pv, P.mask16[:, gg:gg + 1], None, MUL, None, t, peB, P.ctok)
            yield from pause(K1 if j else K4)
            while len(gate.utok) <= j:
                yield
            utok = gate.utok
            but = []
            for k in range(4):
                b = P.ps.get()
                for ri in range(2):
                    for tau in range(8):
                        tk = mm(P, b.t[:, ri * NB:(ri + 1) * NB],
                                Bop[32 * k:32 * k + 32, 2 * tau + ri, :, :].rearrange("p a b -> p (a b)"),
                                U[32 * k:32 * k + 32, j, tau:T1:8], tau == 0, tau == 7, bt, utok[j], b.free,
                                inc=(tau == 7 and ri == 1))
                    yield
                t = cp(P, BU[:, :, NB * k:NB * k + NB], b.t[:, 0:2 * NB].rearrange("p (r c) -> p r c", r=2), tk, peX)
                P.ps.put(b, t)
                but.append(t)
            peB = tk
            fl = lambda a: a.rearrange("p q c -> p (q c)")
            Er, Ei = fl(E[:, 0, 4 * j:4 * j + 4, :]), fl(E[:, 1, 4 * j:4 * j + 4, :])
            br, bi = BU[:, 0, :], BU[:, 1, :]
            a = tt(d, tq[:, 0, :], br, Er, MUL, but, peX, setup)
            b_ = tt(d, tq[:, 1, :], bi, Ei, MUL)
            v1 = tt(d, V[:, 0, :], tq[:, 0, :], tq[:, 1, :], ADD, a, b_)
            a = tt(d, tq[:, 0, :], bi, Er, MUL, v1)
            b_ = tt(d, tq[:, 1, :], br, Ei, MUL, v1)
            v2 = tt(d, V[:, 1, :], tq[:, 0, :], tq[:, 1, :], SUB, a, b_)
            rv = Rk[:, :].rearrange("p (q c) -> p q c", c=NB)
            t = vcopy(d, rv, r8[:, 4 * j:4 * j + 4].unsqueeze(2).broadcast_to([128, 4, NB]), v2, setup)
            t = mset(d, rv[:, :, 0:1], 0.0, t)
            yr, yi = BU[:, 0, :], BU[:, 1, :]

            def scan(o, v):
                return d.do(lambda e: e.tensor_tensor_scan(o, Rk[:, :], v, 0.0, MUL, ADD), t, v2)

            yield
            t = scan(yr, V[:, 0, :])
            t = scan(yi, V[:, 1, :])
            q = lambda a: a.rearrange("p (q c) -> p q c", c=NB)
            xt = cmul(d, X[:, 0, :, 1:NB + 1], X[:, 1, :, 1:NB + 1], q(yr), q(yi), E[:, 0, 4 * j:4 * j + 4, :],
                      E[:, 1, 4 * j:4 * j + 4, :], q(tq[:, 0, :]), q(tq[:, 1, :]), t, peX)
            xz = mset(d, X[:, :, :, 0:1], 0.0, t)
            yield
            w4 = lambda tau, ri: W[:, tau, ri, :].rearrange("p (k h) -> p k h", h=16)
            t = vcopy(d, w4(0, 0), bc1[:, 2, 4 * j:4 * j + 4, :], ld, xt)
            t = ts(d, w4(0, 1), bc1[:, 3, 4 * j:4 * j + 4, :], -1.0, None, MUL, None, ld)
            a4 = lambda a: a[:, 4 * j:4 * j + 4].unsqueeze(2).broadcast_to([128, 4, 16])
            A, AI = a4(ar1), a4(ai1)
            h4 = lambda a: a[:, 0:64].rearrange("p (k h) -> p k h", h=16)
            ua, ub = h4(q1[:, 0, :]), h4(q1[:, 1, :])
            for tau in range(8):
                a = tt(d, ua, w4(tau, 0), A, MUL, t, t1)
                b_ = tt(d, ub, w4(tau, 1), AI, MUL, t)
                c = tt(d, w4(tau + 1, 0), ua, ub, ADD, a, b_)
                a = tt(d, ua, w4(tau, 1), A, MUL, c)
                b_ = tt(d, ub, w4(tau, 0), AI, MUL, c)
                t = tt(d, w4(tau + 1, 1), ua, ub, SUB, a, b_)
                if tau % 2 == 1:
                    yield
            wv = W[:, :, :, :].rearrange("p a b (k h) -> p (a b k) h", h=16)
            for gg in range(2):
                ct = ts(P.pool, Cop[:, :, gg, :], wv, P.mask64[:, gg:gg + 1], None, MUL, None, t, peC)
            cop = Cop[:, :, :, :].rearrange("p (a b k) g h -> p a b k (g h)", a=9, b=2)
            yield from pause(K2)
            b = P.ps.get()
            for k in range(4):
                for ri in range(2):
                    tk = mm(P, b.t[32 * k:32 * k + 32, 0:256], Bn[:, ri, 4 * j + k, :, :].rearrange("p g h -> p (g h)"),
                            cop[:, 0:8, ri, k, :], ri == 0, ri == 1, ct, t1, b.free, inc=(k == 3 and ri == 1))
            dt = []
            for k in range(4):
                dt.append(vcopy(d, Dop[32 * k:32 * k + 32, :, 32 * k:32 * k + 32],
                                b.t[32 * k:32 * k + 32, 0:256].rearrange("p (a c) -> p a c", a=8), tk, dz, peC))
            P.ps.put(b, dt[-1])
            dt = stt(d, Dop[:, 0, :], P.ident, P.vec("ssm_d", j), Dop[:, 0, :], MUL, ADD, dt)
            gt = []
            yield from pause(K3)
            for half in (3, 2, 1, 0):
                b = P.ps.get()
                for tau in (2 * half, 2 * half + 1):
                    o = b.t[:, (tau % 2) * NB:(tau % 2 + 1) * NB]
                    for sg in range(tau + 1):
                        mm(P, o, Dop[:, tau - sg, :], U[:, j, sg:T1:8], sg == 0, False, dt, utok[j], b.free, skip=True)
                    for k in range(4):
                        for ri in range(2):
                            tk = mm(P, b.t[32 * k:32 * k + 32, (tau % 2) * NB:(tau % 2 + 1) * NB],
                                    cop[:, tau + 1, ri, k, :], X[:, ri, k, 0:NB], False, ri == 1, xt, xz, ct,
                                    inc=(tau % 2 == 1 and k == 3 and ri == 1), skip=True)
                    yield
                yv = U[:, j, 0:T1].rearrange("p (c a) -> p a c", a=8)
                t = act(P, yv[:, 2 * half:2 * half + 2, :], b.t[:, 0:2 * NB].rearrange("p (a c) -> p a c", a=2),
                        ACT.Gelu_apprx_tanh, tk, after)
                P.ps.put(b, t)
                gt.append(t)
            peC = peX = tk
            ytok[j] = gt[-1]


def mlstm(P, M, qs, ks, vs):
    def fetch(h):
        q, k = qs.get(), ks.get()
        dma(P.sp, q.t[:, 0:T1], P.mq[3 * h], M.sem[h % 2], 0, q.free, M.stok[3 * h])
        t = dma(P.sp, k.t[:, 0:T1], P.mq[3 * h + 1], M.sem[h % 2], 32 * (h // 2 + 1), k.free, M.stok[3 * h + 1])
        return Tiled(q, t), Tiled(k, t)

    ahead = fetch(0)
    for h in range(4):
        q, k = ahead
        v, V = M.D.get(), vs.get()
        t = dma(P.sp, v.t[:, 0:T1], P.mq[3 * h + 2], M.vsem, 32 * h + 16, v.free, M.stok[3 * h + 2])
        if h < 3:
            ahead = fetch(h + 1)
        yield from pause(3)
        vt = []
        for j0 in (0, 4, 8):
            b = P.ps.get()
            js = range(j0, min(j0 + 4, 9))
            for j in js:
                t0, tn = TT1[j]
                tk = tp(P, b.t[0:tn, 128 * (j - j0):128 * (j - j0) + 128], v.t[:, t0:t0 + tn], P.ident,
                        t, P.ctok, b.free, inc=(j == js[-1]))
            n = len(js)
            tn = TT1[js[-1]][1]
            vt.append(cp(P, V.t[0:tn, j0:j0 + n, 0:128],
                         b.t[0:tn, 0:128 * n].rearrange("p (a c) -> p a c", a=n), tk, V.free))
            P.ps.put(b, vt[-1])
            yield
        v.free = [tk]
        yield from mlstm_head(P, h, q, k, Tiled(V, vt), M)


def mlstm_head(P, h, q, k, V1, M):
    d = P.dve
    sc = float(128 ** -0.5)
    nt = []
    for c0, cn in CH1:
        b = P.ps.get()
        t = mm(P, b.t[:, 0:cn], P.sel4[0:4, h, :], M.negM[0:4, c0:c0 + cn], True, True, M.tok, P.ctok, b.free, inc=True)
        t = cp(P, M.NMB[:, c0:c0 + cn], b.t[:, 0:cn], t, M.nmbfree)
        P.ps.put(b, t)
        nt.append(t)
    offs, off = [], 0
    stoks = []
    for i in range(9):
        s0 = 128 * i
        L = T1 - s0
        dn = min(128, L)
        D = M.D.get()
        u = M.UC[:, i, h:h + 1]
        t = ts(d, D.t[:, 0:dn], M.NMB[:, s0:s0 + dn], u, 0.0, ADD, MIN, nt, M.uctok, D.free)
        t = tt(d, D.t[:, 0:dn], D.t[:, 0:dn], P.triu_neg[:, 0:dn], ADD, t)
        dt = [act(P, D.t[:, 0:dn], D.t[:, 0:dn], ACT.Exp, t)]
        if L > 128:
            dt.append(act(P, D.t[:, 128:L], M.NMB[:, s0 + 128:T1], ACT.Exp, nt, M.uctok, D.free, bias=u))
        for c0 in range(0, L, 512):
            cn = min(512, L - c0)
            b = P.ps.get()
            t = mm(P, b.t[:, 0:cn], k.t[:, s0:s0 + 128], q.t[:, s0 + c0:s0 + c0 + cn], True, True, q.tok, k.tok,
                   b.free, inc=True)
            t = stt(d, M.SS[:, off + c0:off + c0 + cn], b.t[:, 0:cn], sc, D.t[:, c0:c0 + cn], MUL, MUL, t, dt, M.ssfree)
            P.ps.put(b, t)
            yield
        D.free = [t]
        stoks.append(t)
        offs.append(off)
        off += L
    M.nmbfree = P.everyone()
    q.buf.free = [P.pe.last]
    k.buf.free = [P.pe.last]
    ob = M.D.get()
    ot = dma(P.sp, ob.t[:, 0:T1], P.mo[h], M.vsem, 32 * (h + 1), ob.free, M.otok[h])
    ct = []
    for j in range(9):
        t0, tn = TT1[j]
        b = P.ps.get()
        for i in range(j + 1):
            o = offs[i] + t0 - 128 * i
            t = mm(P, b.t[0:tn, 0:129], M.SS[:, o:o + tn], V1.t[:, i, 0:129], i == 0, i == j, stoks[i], V1.tok,
                   b.free, inc=(i == j))
        ct.append(cp(P, M.NUM[0:tn, j, :], b.t[0:tn, 0:129], t, M.numfree))
        P.ps.put(b, ct[-1])
        yield
    M.ssfree = P.pe.last
    V1.buf.free = [P.pe.last]
    g = M.small
    N3 = M.NUM[:, :, 0:128]
    den = g[:, 0, :]
    t = stt(d, den, M.NUM[:, :, 128], -1.0, M.NUM[:, :, 128], MUL, MAX, ct)
    t = tt(d, den, den, M.EC[:, :, h], MAX, t, M.uctok)
    t = recip(P, den, den, t)
    bc = lambda a: a.unsqueeze(2).broadcast_to([128, 9, 128])
    t = tt(d, N3, N3, bc(den), MUL, t)
    D = M.D.get()
    HQ = D.t[:, :].rearrange("p (a c) -> p a c", a=9)
    t = tt(d, HQ, N3, N3, MUL, t, D.free)
    t = P.dve.do(lambda e: e.tensor_reduce(g[:, 1, :], HQ, AX_X, ADD), t)
    D.free = [t]
    t = act(P, g[:, 1, :], g[:, 1, :], ACT.Sqrt, t, bias=P.eps6, scale=1.0 / 128)
    t = recip(P, g[:, 1, :], g[:, 1, :], t)
    t = tt(d, N3, N3, bc(g[:, 1, :]), MUL, t)
    yield
    for j0 in (0, 4, 8):
        b = P.ps.get()
        js = range(j0, min(j0 + 4, 9))
        for j in js:
            t0, tn = TT1[j]
            tk = tp(P, b.t[:, 128 * (j - j0):128 * (j - j0) + tn], M.NUM[0:tn, j, 0:128], P.ident[0:tn, 0:tn], t,
                    b.free, inc=(j == js[-1]))
        w = T1 - 128 * j0 if j0 == 8 else 512
        M.ytok[h] = stt(d, M.Y[:, h, 128 * j0:128 * j0 + w], b.t[:, 0:w], P.vec("g_head", h),
                        ob.t[:, 128 * j0:128 * j0 + w], MUL, MUL, tk, ot)
        P.ps.put(b, M.ytok[h])
        yield
    ob.free = [M.ytok[h]]
    M.numfree = P.pe.last


class Tiled:
    def __init__(self, buf, tok):
        self.buf, self.t, self.tok = buf, buf.t, tok


def project(P, name, G, T, chunks, xtok, pad):
    toks = []

    def ev(c, c0, cn, ps, t):
        toks.append(cp(P, G.t[:, pad + c0:pad + c0 + cn], ps, t, G.free))
        return [toks[-1]]

    dense(P, name, 8, P.XH, P.XL, xtok, chunks, ev)
    return toks


class Spills:

    def __init__(self, P, name, n, shape, cx, free):
        self.P = P
        self.ring = Ring([Buf(cx.enter_context(P.nc.sbuf_tensor(f"{name}{i}", shape, F))) for i in range(n)])
        for i, b in enumerate(self.ring.bufs):
            b.free, b.sem, b.count = [free], P.newsem(f"{name}{i}"), 0
        self.get = self.ring.get

    def store(self, q, b, dst, t):
        b.count += 16
        b.free = [dma(q, dst, b.t[:, :], b.sem, b.count, t)]
        return b.free[0]

    def all(self):
        return [b.free for b in self.ring.bufs]


def block1(P):
    nc, d = P.nc, P.dve
    I = P.I
    HB = P.HB
    toks = []
    for k in range(8):
        toks.append(dma(P.pool, HB[:, k, 0:T1], I["x1"][:, k, :], P.xsem[k], 16))
    outer = ExitStack()
    with outer:
        osb = lambda name, shape: outer.enter_context(nc.sbuf_tensor(name, shape, F))
        M = Prog()
        M.UC, M.EC = osb("UC", [128, 9, 4]), osb("EC", [128, 9, 4])
        gi, gw = HB[0:64, 3, :], HB[0:64, 0:3, :]
        M.negM = gi[0:4, :]
        M.stok = [None] * 12
        ytok = [None] * 4
        with ExitStack() as cx:
            sb = lambda name, shape: cx.enter_context(nc.sbuf_tensor(name, shape, F))
            G = Ring([Buf(sb(f"m_G{i}", [128, T1 + 3])) for i in range(1)])
            VX = sb("ssm_VX", [128, 8 * (NB + 1)])
            S = Spills(P, "m_S", 2, [128, T1], cx, None)
            for b in G.bufs:
                b.free = [mset(P.pool, b.t[:, 0:3], 0.0)]
            gate = Prog()
            gate.free, gate.utok = None, []
            P.bg.append(ssm(P, HB[:, 4:8, :], HB[:, 0:4, :].rearrange("p a t -> p (a t)"), VX, gate, ytok))
            tick(P)
            for _ in range(3):
                P.w.split()
            tmp = Ring([Buf(t[:, o:o + 512]) for t in (VX, S.ring.bufs[1].t, G.bufs[0].t) for o in (3, 515)])
            tmp.bufs[2].t, tmp.bufs[3].t = S.ring.bufs[1].t[:, 0:512], S.ring.bufs[1].t[:, 512:1024]
            xtok = prenorm(P, HB, toks, CH1, "g_mix_pre", S.ring.bufs[0].t, tmp)
            after = P.everyone()
            for b in G.bufs + S.ring.bufs:
                b.free = [b.free, after]
            gate.free = after
            P.rate = RS
            for m in range(4):
                uts = []

                def ev_u(c, c0, cn, ps, t):
                    uts.append(cp(P, HB[:, 4 + m, c0:c0 + cn], ps, t, after))
                    return [uts[-1]]

                dense(P, "u", 8, P.XH, P.XL, xtok, CH1, ev_u)
                gate.utok.append(uts)
            def conv_silu(name, w0):
                g = G.get()
                t = project(P, name, g, T1, CH1, xtok, 3)
                w = lambda j: P.vec("wqk", 4 * w0 + j)
                b = S.get()
                o = b.t[:, 0:T1]
                t = ts(d, o, g.t[:, 3:3 + T1], w(3), P.vec("bqk", w0), MUL, ADD, t, b.free, P.vtok)
                for j in (2, 1, 0):
                    t = stt(d, o, g.t[:, j:j + T1], w(j), o, MUL, ADD, t)
                g.free = [t]
                i = 3 * (w0 % 4) + w0 // 4
                M.stok[i] = S.store(P.act, b, P.mq[i], act(P, o, o, ACT.Silu, t))

            def plain(name, func, dst, S):
                b = S.get()
                e = []

                def ev(c, c0, cn, ps, t):
                    e.append(act(P, b.t[:, c0:c0 + cn], ps, func, t, b.free))
                    return [e[-1]]

                dense(P, name, 8, P.XH, P.XL, xtok, CH1, ev)
                return S.store(P.act, b, dst, e)

            for h in range(4):
                M.stok[3 * h + 2] = plain("v", ACT.Copy, P.mq[3 * h + 2], S)
            M.otok = [plain("o", ACT.Sigmoid, P.mo[m], S) for m in range(4)]
            for h in range(4):
                conv_silu("q", h)
                conv_silu("k", 4 + h)
            gtok = [plain("ga" if m < 8 else "gb", ACT.Sigmoid, P.mo[4 + m], S) for m in range(NG)]
            drain(P)
            after = P.everyone() + S.all()
        P.dbg("ya0", HB[:, 4:8, 0:T1], ytok)
        gt = []

        def ev_g(c, c0, cn, ps, t):
            gt.append(ts(d, gi[0:64, c0:c0 + cn], ps[0:64, :], P.vec("bgate", 0)[0:64, :], None, ADD, None, t, after,
                         P.vtok))
            return [gt[-1]]

        dense(P, "gates", 8, P.XH, P.XL, xtok, CH1, ev_g)

        with ExitStack() as cy:
            AH = cy.enter_context(nc.sbuf_tensor("glu_h", [128, 4, T1], R))
            AL = cy.enter_context(nc.sbuf_tensor("glu_l", [128, 4, T1], R))
            sg = Ring([Buf(cy.enter_context(nc.sbuf_tensor(f"glu_s{i}", [128, 352], F))) for i in range(2)])
            for b in sg.bufs:
                b.free = [after]
            at = splits(P, [HB[:, 4 + m, 0:T1] for m in range(4)], AH, AL, CH1, ytok, after)
            P.bg.append(mlstm_gates(P, gi, gw, M, gt, after))
            P.rate = 1
            for m in range(4):
                def ev_glu(c, c0, cn, ps, t):
                    s = sg.get()
                    t = act(P, s.t[:, 0:cn], ps, ACT.Sigmoid, t, s.free)
                    ytok[m] = tt(d, HB[:, 4 + m, c0:c0 + cn], HB[:, 4 + m, c0:c0 + cn], s.t[:, 0:cn], MUL, t, at)
                    s.free = [ytok[m]]
                    return [t]

                dense(P, "glu", 4, AH, AL, at, CH1, ev_glu)
            drain(P)
        after = P.everyone()
        P.dbg("ya", HB[:, 4:8, 0:T1], ytok)
        with ExitStack() as cy:
            sb = lambda name, shape: cy.enter_context(nc.sbuf_tensor(name, shape, F))
            qs = Ring([Buf(sb(f"m_q{i}", [128, T1])) for i in range(2)])
            ks = Ring([Buf(sb(f"m_k{i}", [128, 1152])) for i in range(2)])
            vs = Ring([Buf(sb("m_V0", [128, 9, 130]))])
            S = Spills(P, "m_g", 2, [128, T1], cy, after)
            M.SS = sb("m_SS", [128, 4752])
            M.D = Ring([Buf(sb(f"m_D{i}", [128, 1152])) for i in range(2)])
            M.NMB = sb("m_NMB", [128, T1])
            M.NUM = sb("m_NUM", [128, 9, 129])
            M.small = sb("m_small", [128, 2, 9])
            M.Y, M.ytok = HB, [None] * 4
            M.ssfree = M.nmbfree = after
            M.sem, M.vsem = [P.newsem("m_l0"), P.newsem("m_l1")], P.newsem("m_lv")
            for b in qs.bufs + M.D.bufs:
                b.free = [after]
            for b in ks.bufs:
                b.free = [mset(P.pool, b.t[:, T1:1152], 0.0, after), after]
            for b in vs.bufs:
                t = mset(P.pool, b.t[:, 8, :], 0.0, after)
                b.free = [mset(P.pool, b.t[:, 0:8, 128:130], 1.0, after), mset(P.pool, b.t[0:16, 8, 128:130], 1.0, t),
                          after]
            M.numfree = mset(P.pool, M.NUM[:, 8, :], 0.0, P.pool.last)
            P.bg.append(mlstm(P, M, qs, ks, vs))
            P.rate = RM
            gtok += [plain("ga" if m < 8 else "gb", ACT.Sigmoid, P.mo[4 + m], S) for m in range(NG, 16)]
            drain(P)
            after = P.everyone() + S.all()
        P.dbg("hb", HB[:, 0:4, 0:T1], M.ytok)
    P.rate = 1
    with ExitStack() as cx:
        sb = lambda name, shape, t=F: cx.enter_context(nc.sbuf_tensor(name, shape, t))
        AH, AL = sb("ya_h", [128, 4, T1], R), sb("ya_l", [128, 4, T1], R)
        BH, BL = sb("yb_h", [128, 4, T1], R), sb("yb_l", [128, 4, T1], R)
        ld = Ring([Buf(sb(f"mg{i}", [128, 352])) for i in range(3)])
        for n, b in enumerate(ld.bufs):
            b.free, b.sem, b.count = [after], P.newsem(f"mg{n}"), 0
        order = [(m, c0, cn) for m in range(8) for c0, cn in CH1]
        gb = []

        def fetch():
            if len(gb) < len(order):
                m, c0, cn = order[len(gb)]
                b = ld.get()
                b.count += 16
                gb.append(Tiled(b, dma(P.pool, b.t[:, 0:cn], P.mo[12 + m][:, c0:c0 + cn], b.sem, b.count, b.free,
                                       gtok[8 + m])))

        for _ in range(3):
            fetch()
        at = splits(P, [HB[:, 4 + m, 0:T1] for m in range(4)], AH, AL, CH1, ytok, after)
        bt = splits(P, [HB[:, m, 0:T1] for m in range(4)], BH, BL, CH1, M.ytok, after)
        asem = [P.newsem(f"mga{m}") for m in range(8)]
        ga = [dma(P.sp, HB[:, m, 0:T1], P.mo[4 + m], asem[m], 16, (bt + at)[m], gtok[m]) for m in range(8)]
        mt, mtok = [None] * 3, []
        for m in range(8):
            def ev_a(c, c0, cn, ps, t):
                mt[c] = tt(d, HB[:, m, c0:c0 + cn], HB[:, m, c0:c0 + cn], ps, MUL, t, ga[m])
                return [mt[c]]

            def ev_b(c, c0, cn, ps, t):
                s = gb[3 * m + c]
                r = tt(d, s.t[:, 0:cn], s.t[:, 0:cn], ps, MUL, t, s.tok)
                mt[c] = tt(d, HB[:, m, c0:c0 + cn], HB[:, m, c0:c0 + cn], s.t[:, 0:cn], ADD, r, mt[c])
                s.buf.free = [mt[c]]
                fetch()
                return [r]

            dense(P, "wa", 4, AH, AL, at, CH1, ev_a)
            dense(P, "wb", 4, BH, BL, bt, CH1, ev_b)
            mtok.append(split(P, HB[:, m, 0:T1], P.XH[:, m, 0:T1], P.XL[:, m, 0:T1], mt[2], after))
        P.dbg("merged", HB[:, :, 0:T1], mt)
        xtok = mtok
    after = P.everyone()
    with ExitStack() as cx:
        sb = lambda name, shape, t=F: cx.enter_context(nc.sbuf_tensor(name, shape, t))
        acc, rs, rs2 = sb("n2_acc", [128, T1]), sb("n2_rs", [128, T1]), sb("n2_rs2", [128, T1])
        sq = Ring([Buf(sb(f"n2_sq{i}", [128, T1])) for i in range(2)])
        tmp = Ring([Buf(sb(f"n2_t{i}", [128, 512])) for i in range(6)])
        for b in sq.bufs + tmp.bufs:
            b.free = [after]
        X = preload(P, "n2", cx, after, T1, lambda m: I["x1"][:, m, :], None)
        st = Stats(P, acc, sq, T1, CH1, after)
        for m in range(8):
            t8 = []

            def ev_w(c, c0, cn, ps, t):
                t8.append(cp(P, HB[:, m, c0:c0 + cn], ps, t, xtok[m]))
                return [t8[-1]]

            dense(P, "wout", 8, P.XH, P.XL, xtok, CH1, ev_w)
            st.add(HB[:, m, 0:T1], t8)
        t = st.finish(rs, 1024, P.eps6)
        ht, xtok = renorm(P, HB, rs, t, "g_mix_post", X, T1, CH1, "g_ffn_pre", rs2, tmp, P.pe.last)
        P.h1store = [dma(P.pool, P.h1[:, k, :], HB[:, k, 0:T1], P.hsem[k], 16, ht[k]) for k in range(8)]
        P.dbg("h1", HB[:, :, 0:T1], ht)
        after = P.everyone()
    P.hfree = [after, P.h1store]
    with ExitStack() as cx:
        rs = cx.enter_context(nc.sbuf_tensor("n3_rs", [128, T1], F))
        htok, t = ffn(P, ACT.Gelu_apprx_tanh, T1, CH1, xtok, HB, "1", "fconv", "fcb", after, rs)
        after = P.everyone()
        sb = lambda name, shape, t=F: cx.enter_context(nc.sbuf_tensor(name, shape, t))
        rs2 = sb("n3_rs2", [128, T2])
        tmp = Ring([Buf(sb(f"n3_t{i}", [128, 512])) for i in range(6)])
        for b in tmp.bufs:
            b.free = [after]
        X = preload(P, "n3", cx, after, T2, lambda m: P.h1[:, m, 16:T1], P.h1store)
        ht, xtok = renorm(P, HB[:, :, 16:T1], rs[:, 16:T1], [t, htok], "g_ffn_post", X, T2, CH2, "mix_norm", rs2, tmp,
                          P.xfree)
        P.h2store = [dma(P.pool, P.h2[:, k, :], HB[:, k, 16:T1], P.hsem[k], 32, ht[k]) for k in range(8)]
    return xtok


def preload(P, name, cx, free, T, src, ready):
    x = cx.enter_context(P.nc.sbuf_tensor(name + "_x", [128, 8, T], F))
    out = []
    for m in range(8):
        sem = P.newsem(f"{name}_x{m}")
        out.append((x[:, m, :], dma(P.sp, x[:, m, :], src(m), sem, 16, free, ready)))
    return out


def prenorm(P, H, toks, chunks, gname, rs, tmp):
    banks = [P.ps.get() for _ in chunks]
    last = []
    for k in range(8):
        for b, (c0, cn) in zip(banks, chunks):
            s = tmp.get()
            a = act(P, s.t[:, 0:cn], H[:, k, c0:c0 + cn], ACT.Square, toks[k], s.free)
            a = mm(P, b.t[:, 0:cn], P.ones, s.t[:, 0:cn], k == 0, k == 7, a, P.ctok, b.free, inc=True)
            s.free = [a]
            last = (last + [a])[-len(chunks):]
        tick(P, K0)
    rt = []
    for b, a, (c0, cn) in zip(banks, last, chunks):
        a = act(P, rs[:, c0:c0 + cn], b.t[:, 0:cn], ACT.Sqrt, a, bias=P.eps6, scale=1.0 / 1024)
        P.ps.put(b, a)
        rt.append(recip(P, rs[:, c0:c0 + cn], rs[:, c0:c0 + cn], a))
    out = [{} for _ in range(8)]
    for c, (c0, cn) in enumerate(chunks):
        normalise(P, H, rs, rt[c], c, c0, cn, gname, tmp, out, None)
    return out


def mlstm_gates(P, gi, gw, M, gt, after):
    d = P.dve
    f = gi[32:36, :]
    a, b = gw[32:36, 0, :], gw[32:36, 1, :]
    yield
    t = act(P, a, f, ACT.Abs, gt, after)
    t = act(P, a, a, ACT.Exp, t, scale=-1.0)
    t = act(P, a, a, ACT.Ln, t, bias=P.one[32:36, :])
    t = stt(d, b, f, 0.0, a, MIN, SUB, t)
    yield
    o = mset(d, gw[32:36, 2, :], 1.0, after)
    t = d.do(lambda e: e.tensor_tensor_scan(a, gw[32:36, 2, :], b, 0.0, MUL, ADD), t, o)
    B, u, m = gw[0:4, 0, :], gw[0:4, 1, :], gw[0:4, 2, :]
    t = vcopy(d, B, a, t)
    t = tt(d, u, gi[0:4, :], B, SUB, t)
    yield
    z = mset(d, M.negM[0:4, :], 0.0, t)
    t = d.do(lambda e: e.tensor_tensor_scan(m, M.negM[0:4, :], u, 0.0, ADD, MAX), t, z)
    n = ts(d, M.negM[0:4, :], m, -1.0, None, MUL, None, t)
    t = tt(d, B, B, m, ADD, t)
    e = act(P, B, B, ACT.Exp, t, scale=-1.0)
    z = mset(P.pool, M.UC[:, 8, :], -1e30, after)
    z2 = mset(P.pool, M.EC[:, 8, :], 1.0, after)
    yield from pause(3)
    bk = P.ps.get()
    for j, (t0, tn) in enumerate(TT1):
        tp(P, bk.t[0:tn, 8 * j:8 * j + 4], gw[0:4, 1, t0:t0 + tn], P.ident[0:4, 0:4], e, n, P.ctok, bk.free)
        tk = tp(P, bk.t[0:tn, 8 * j + 4:8 * j + 8], gw[0:4, 0, t0:t0 + tn], P.ident[0:4, 0:4], inc=(j == 8))
    v = bk.t[:, 0:72].rearrange("p (a c) -> p a c", c=8)
    t1 = cp(P, M.UC[:, 0:8, :], v[:, 0:8, 0:4], tk, after)
    t2 = cp(P, M.EC[:, 0:8, :], v[:, 0:8, 4:8], tk)
    t3 = cp(P, M.UC[0:16, 8, :], v[0:16, 8, 0:4], tk, z)
    t4 = cp(P, M.EC[0:16, 8, :], v[0:16, 8, 4:8], tk, z2)
    P.ps.put(bk, t4)
    M.uctok = [t1, t2, t3, t4, z, z2]
    M.tok = n


def vtrans(P, out, src, *toks):
    t = None
    for h in range(2):
        for a in range(2):
            for b in range(2):
                r, w = 64 * h + 32 * a, 64 * h + 32 * b
                o = out[w:w + 32, :].rearrange("p (c x) -> p c x", x=64)[:, :, 32 * a:32 * a + 32]
                s = src[r:r + 32, :].rearrange("p (c x) -> p c x", x=64)[:, :, 32 * b:32 * b + 32]
                t = P.dve.do(lambda e, o=o, s=s: e.transpose(o, s), *toks)
    return t


def pieces(P, n, outs, emit, evac):
    per = 512 // n
    for c0 in range(0, 8, per):
        b = P.ps.get()
        for c in range(c0, c0 + per):
            for h in range(2):
                last = c == c0 + per - 1 and h == 1
                t = emit(h, c, b.t[64 * h:64 * h + 64, (c - c0) * n:(c - c0 + 1) * n], b.free, last)
        P.ps.put(b, evac(c0, per, b.t[:, 0:512], t))
        yield


def rwkv_half(P, j, hf, D):
    d = P.dve
    g0 = 512 * hf
    r, k, v = D.in3[:, 0, :], D.in3[:, 1, :], D.in3[:, 2, :]
    r_t = k_t = v_t = D.intok
    S = D.S
    inplace = {"Xt": r, "Vt": k}
    full = lambda n: inplace.get(n) if n in inplace else S[n][:, :]
    c3 = lambda a: a.rearrange("p (c x) -> p c x", x=64)
    lw, a_, kk = full("t0"), full("t1"), full("t2")
    tk = []
    for c0, cn in ((0, 512),):
        b = P.ps.get()
        t = mm(P, b.t[:, 0:cn], D.wl[0:32, 128 * j:128 * j + 128], D.WA[0:32, g0:g0 + cn], True, True, D.wat, b.free,
               inc=True)
        t = act(P, lw[:, c0:c0 + cn], b.t[:, 0:cn], ACT.Sigmoid, t, D.free, bias=P.vec("w0", j))
        P.ps.put(b, t)
        b = P.ps.get()
        t = mm(P, b.t[:, 0:cn], D.wl[32:64, 128 * j:128 * j + 128], D.WA[32:64, g0:g0 + cn], True, True, D.wat, b.free,
               inc=True)
        t = act(P, a_[:, c0:c0 + cn], b.t[:, 0:cn], ACT.Sigmoid, t, D.free, bias=P.vec("a0", j))
        P.ps.put(b, t)
        yield
    lt = ts(d, lw, lw, -0.6065306597126334, None, MUL, None, t)
    yield
    t2 = ts(d, kk, k, P.vec("k_k", j), None, MUL, None, k_t, t)
    t3 = tt(d, full("t3"), kk, kk, MUL, t2)
    yield from pause(Q1)
    for c0, cn in ((0, 512),):
        b = P.ps.get()
        t = mm(P, b.t[:, 0:cn], P.ones64, full("t3")[:, c0:c0 + cn], True, True, t3, P.ctok, b.free, inc=True)
        t = act(P, full("t4")[:, c0:c0 + cn], b.t[:, 0:cn], ACT.Sqrt, t, D.free)
        P.ps.put(b, t)
    yield
    t = ts(d, full("t4"), full("t4"), 1e-12, None, MAX, None, t)
    t = recip(P, full("t4"), full("t4"), t)
    yield
    t = tt(d, kk, kk, full("t4"), MUL, t)
    tb = stt(d, full("t3"), kk, -1.0, a_, MUL, MUL, t)
    yield
    t = ts(d, a_, a_, -1.0, P.vec("k_a", j), ADD, MUL, tb)
    tk2 = stt(d, a_, a_, 1.0, k, ADD, MUL, t, k_t)
    k2, bn = a_, full("t3")
    t = stt(d, full("bon"), r, P.vec("r_k", j), k2, MUL, MUL, tk2, r_t, D.free)
    bt = []
    yield from pause(Q2)
    for c0, cn in ((0, 512),):
        b = P.ps.get()
        t1 = mm(P, b.t[:, 0:cn], P.ones64, full("bon")[:, c0:c0 + cn], True, True, t, b.free, inc=True)
        t1 = tt(d, full("bon")[:, c0:c0 + cn], b.t[:, 0:cn], v[:, c0:c0 + cn], MUL, t1, v_t)
        P.ps.put(b, t1)
        bt.append(t1)
    yield
    cum = full("t4")
    t = d.do(lambda e: e.tensor_tensor_scan(cum, D.reset[:, :], lw, 0.0, MUL, ADD), lt, tk2, D.rtok)
    AR = S["AR"][:, :].rearrange("p (c a x) -> p c a x", a=2, x=64)
    e1 = act(P, AR[:, :, 1, :], c3(cum), ACT.Exp, t, D.free)
    trho = tt(d, AR[:, :, 1, :], AR[:, :, 1, :], c3(r), MUL, e1, r_t)
    tl = tt(d, lw, cum, lw, SUB, t)
    e2 = act(P, AR[:, :, 0, :], c3(lw), ACT.Exp, tl)
    yield
    tal = tt(d, AR[:, :, 0, :], AR[:, :, 0, :], c3(kk), MUL, e2)
    e3 = act(P, lw, cum, ACT.Exp, tl, e2, scale=-1.0)
    be, ka = S["BK"][:, 0:512], S["BK"][:, 512:1024]
    tbe = tt(d, be, bn, lw, MUL, e3, D.free)
    tka = tt(P.pool if QP & 1 else d, ka, k2, lw, MUL, e3)
    yield
    last = c3(cum)[:, :, 63:64].broadcast_to([128, 8, 64])
    t = tt(d, c3(kk), last, c3(cum), SUB, tal)
    e4 = act(P, kk, kk, ACT.Exp, t)
    e5 = act(P, D.pc[:, :], c3(cum)[:, :, 63], ACT.Exp, t, D.free)
    yield
    tb2 = tt(d, bn, bn, kk, MUL, e4, tbe)
    tk2b = tt(P.pool if QP & 2 else d, k2, k2, kk, MUL, e4, tka)
    yield
    AM = S["AM"][:, :].rearrange("p (c a x) -> p c a x", a=2, x=64)
    tcp = vcopy(d, c3(lw), AR[:, :, 0, :], tal, tbe, tka)
    Vt, Bt, Kt, At = full("Vt"), kk, full("t4"), full("Xa")
    x1 = vtrans(P, Vt, v, v_t, tk2)
    yield
    x2 = vtrans(P, Bt, bn, tb2, tk2b)
    yield
    x3 = vtrans(P, Kt, k2, tk2b, e5)
    yield
    x4 = vtrans(P, At, lw, tcp, D.free)
    x5 = vcopy(d, AM[:, :, 0, :], c3(At), x4)
    yield
    yield from pause(Q3)
    GB = S["GB"][:, :].rearrange("p (c a x) -> p c a x", a=2, x=64)
    GK = S["GK"][:, :].rearrange("p (c a x) -> p c a x", a=2, x=64)
    hs = lambda h: slice(64 * h, 64 * h + 64)
    cs = lambda c: slice(64 * c, 64 * c + 64)
    st = {}

    def keep(key, t):
        st.setdefault(key, []).append(t)
        return t

    for key, out, lhs in (("GB", GB, be), ("GK", GK, ka)):
        def emit(h, c, o, fr, lastone):
            return mm(P, o, lhs[hs(h), cs(c)], AR[hs(h), c, :, :].rearrange("p a x -> p (a x)"), True, True, tbe, tka,
                      trho, tal, fr, inc=lastone)

        def evac(c0, n, ps, t):
            return keep(key, tt(d, out[:, c0:c0 + n, :, :].rearrange("p c a x -> p c (a x)"),
                                ps.rearrange("p (c x) -> p c x", x=128),
                                P.mtri[:, :].unsqueeze(1).broadcast_to([128, n, 128]), MUL, t, P.ctok, D.free))

        yield from pieces(P, 128, out, emit, evac)
    X, Xt, Y = full("Xa"), full("Xt"), full("t0")
    Ln = full("t1")

    def emit(h, c, o, fr, lastone):
        return mm(P, o, AR[hs(h), c, 0, :], be[hs(h), cs(c)], True, True, fr, inc=lastone)

    def evac(c0, n, ps, t):
        return keep("L", tt(d, c3(Ln)[:, c0:c0 + n, :], ps.rearrange("p (c x) -> p c x", x=64),
                            P.levels[:, 0, :].unsqueeze(1).broadcast_to([128, n, 64]), MUL, t, x3, P.ctok))

    yield from pieces(P, 64, Ln, emit, evac)
    id3 = P.ident2[:, :].unsqueeze(1).broadcast_to([128, 8, 64])
    t = tt(d, c3(X), c3(Ln), id3, ADD, st["L"], x5)
    tx = t
    t = tt(d, c3(Xt), GB[:, :, 0, :], P.levels[:, 1, :].unsqueeze(1).broadcast_to([128, 8, 64]), MUL, st["GB"], D.free)
    txt = tt(d, c3(Xt), c3(Xt), id3, ADD, t)
    ty = [tcp]
    for lv in range(5):
        st["Y"] = []

        def emit(h, c, o, fr, lastone):
            return mm(P, o, GB[hs(h), c, 0, :], X[hs(h), cs(c)], True, True, tx, txt, st["GB"], fr, inc=lastone)

        def evac(c0, n, ps, t):
            return keep("Y", tt(d, c3(Y)[:, c0:c0 + n, :], ps.rearrange("p (c x) -> p c x", x=64),
                                P.levels[:, 2 + lv, :].unsqueeze(1).broadcast_to([128, n, 64]), MUL, t, ty))

        yield from pieces(P, 64, Y, emit, evac)
        st["X"], st["Xt"] = [], []
        outs = []
        for c0 in (0,):
            bx, by = P.ps.get(), P.ps.get()
            for c in range(c0, c0 + 8):
                for h in range(2):
                    end = c == c0 + 7 and h == 1
                    o = slice(64 * (c - c0), 64 * (c - c0) + 64)
                    if lv < 4:
                        tz = mm(P, bx.t[hs(h), o], Xt[hs(h), cs(c)], Y[hs(h), cs(c)], True, True, st["Y"], txt, bx.free,
                                inc=end)
                    tzt = mm(P, by.t[hs(h), o], Y[hs(h), cs(c)], Xt[hs(h), cs(c)], True, True, st["Y"], txt, by.free,
                             inc=end)
            outs.append((bx, by, tz if lv < 4 else None, tzt))
            yield
        for c0, (bx, by, tz, tzt) in zip((0,), outs):
            w = slice(64 * c0, 64 * c0 + 512)
            if lv < 4:
                tx = tt(d, X[:, w], X[:, w], bx.t[:, 0:512], ADD, tz)
                P.ps.put(bx, tx)
            else:
                P.ps.put(bx, bx.free)
            txt = tt(d, Xt[:, w], Xt[:, w], by.t[:, 0:512], ADD, outs[0][3])
            P.ps.put(by, txt)
        ty = [outs[0][3]]
        yield

    def emit(h, c, o, fr, lastone):
        return mm(P, o, GK[hs(h), c, 0, :], Vt[hs(h), cs(c)], True, True, st["GK"], x1, fr, inc=lastone)

    def evac(c0, n, ps, t):
        return keep("MV", cp(P, AM[:, c0:c0 + n, 1, :], ps.rearrange("p (c x) -> p c x", x=64), t, D.free))

    yield from pieces(P, 64, None, emit, evac)
    WU = S["BK"][:, :].rearrange("p (c a x) -> p c a x", a=2, x=64)

    def emit(h, c, o, fr, lastone):
        return mm(P, o, Xt[hs(h), cs(c)], AM[hs(h), c, :, :].rearrange("p a x -> p (a x)"), True, True, st["MV"], x5,
                  txt, fr, inc=lastone)

    def evac(c0, n, ps, t):
        return keep("WU", cp(P, WU[:, c0:c0 + n, :, :].rearrange("p c a x -> p c (a x)"),
                             ps.rearrange("p (c x) -> p c x", x=128), t, st["L"]))

    yield from pieces(P, 128, None, emit, evac)
    FT, O, Rh, S0 = full("Xa"), full("t1"), full("t0"), full("S0")
    tdp = tt(P.pool if QP & 4 else d, c3(FT), id3, D.pc[:, :].unsqueeze(2).broadcast_to([128, 8, 64]), MUL, e5, tx, ty)

    def emit(h, c, o, fr, lastone):
        return mm(P, o, WU[hs(h), c, 0, :], Bt[hs(h), cs(c)], True, True, st["WU"], x2, fr, inc=lastone)

    def evac(c0, n, ps, t):
        w = slice(64 * c0, 64 * (c0 + n))
        return keep("F", tt(d, FT[:, w], FT[:, w], ps, ADD, t, tdp))

    yield from pieces(P, 64, None, emit, evac)

    def emit(h, c, o, fr, lastone):
        mm(P, o, Kt[hs(h), cs(c)], Vt[hs(h), cs(c)], True, False, st["WU"], x3, x1, fr)
        return mm(P, o, Bt[hs(h), cs(c)], WU[hs(h), c, 1, :], False, True, inc=lastone)

    def evac(c0, n, ps, t):
        return keep("O", cp(P, O[:, 64 * c0:64 * (c0 + n)], ps, t, tx))

    yield from pieces(P, 64, None, emit, evac)

    def emit(h, c, o, fr, lastone):
        return mm(P, o, WU[hs(h), c, 0, :], GB[hs(h), c, 1, :], True, True, fr, inc=lastone)

    def evac(c0, n, ps, t):
        return keep("R", tt(d, c3(Rh)[:, c0:c0 + n, :], ps.rearrange("p (c x) -> p c x", x=64), AR[:, c0:c0 + n, 1, :],
                            ADD, t))

    yield from pieces(P, 64, None, emit, evac)
    if hf == 0:
        t = mset(d, S0[:, 0:64], 0.0, D.free)
    else:
        t = vcopy(d, S0[:, 0:64], S0[:, 512:576], D.free)
    sk = [t]
    for c in range(8 if hf == 0 else 7):
        b = P.ps.get()
        for h in range(2):
            t = mm(P, b.t[hs(h), 0:64], FT[hs(h), cs(c)], S0[hs(h), cs(c)], True, True, sk[-1], st["F"], b.free,
                   inc=h == 1)
        t = tt(d, S0[:, 64 * (c + 1):64 * (c + 2)], b.t[:, 0:64], O[:, cs(c)], ADD, t, st["O"])
        P.ps.put(b, t)
        sk.append(t)
        yield

    def emit(h, c, o, fr, lastone):
        mm(P, o, Vt[hs(h), cs(c)], GK[hs(h), c, 1, :], True, False, fr)
        mm(P, o, WU[hs(h), c, 1, :], GB[hs(h), c, 1, :], False, False)
        return mm(P, o, S0[hs(h), cs(c)], Rh[hs(h), cs(c)], False, True, sk, st["R"], inc=lastone)

    yc = full("t2")

    def evac(c0, n, ps, t):
        return keep("YY", cp(P, yc[:, 64 * c0:64 * (c0 + n)], ps, t))

    yield from pieces(P, 64, None, emit, evac)
    yield from pause(Q4)
    sq, rs = full("t3"), full("t4")
    yt = []
    for c0, cn in ((0, 512),):
        b = P.ps.get()
        t = mm(P, b.t[:, 0:cn], P.ones64, yc[:, c0:c0 + cn], True, True, st["YY"], b.free, inc=True)
        t = stt(d, yc[:, c0:c0 + cn], b.t[:, 0:cn], -1.0 / 64, yc[:, c0:c0 + cn], MUL, ADD, t)
        P.ps.put(b, t)
    t = tt(d, sq, yc, yc, MUL, t)
    yield from pause(1 + Q4)
    for c0, cn in ((0, 512),):
        b = P.ps.get()
        tq = mm(P, b.t[:, 0:cn], P.ones64, sq[:, c0:c0 + cn], True, True, t, b.free, inc=True)
        tq = act(P, rs[:, c0:c0 + cn], b.t[:, 0:cn], ACT.Sqrt, tq, t, bias=P.eps64, scale=1.0 / 64)
        P.ps.put(b, tq)
    t = recip(P, rs, rs, tq)
    yield
    t = tt(d, yc, yc, rs, MUL, t)
    t = ts(d, yc, yc, P.vec("ln_w", j), P.vec("ln_b", j), MUL, ADD, t)
    t = tt(d, yc, yc, full("bon"), ADD, t, bt)
    yield from pause(1 + Q4)
    for c0, cn in ((0, 512),):
        b = P.ps.get()
        tg = mm(P, b.t[:, 0:cn], D.gl[0:96, 128 * j:128 * j + 128], D.GD[0:96, g0:g0 + cn], True, True, D.gdt, b.free,
                inc=True)
        tg = tt(d, P.HB[:, j, g0:g0 + cn], yc[:, c0:c0 + cn], b.t[:, 0:cn], MUL, tg, t, D.hfree)
        P.ps.put(b, tg)
        yt.append(tg)
    P.ytok[j] = yt[-1]
    D.free = P.everyone()
    D.fetch()


def rwkv_pairs(P, pairs, D):
    order = [(j, hf) for j in pairs for hf in range(2)]
    count = [0]

    def fetch():
        if count[0] == len(order):
            return
        j, hf = order[count[0]]
        count[0] += 1
        for n in range(3):
            D.intok = dma(P.sp, D.in3[:, n, :], P.rkv[4 * n + j][:, 512 * hf:512 * hf + 512], D.sem,
                          48 * count[0], D.free, P.rkvtok[4 * n + j])

    D.fetch = fetch
    fetch()
    for j, hf in order:
        yield from rwkv_half(P, j, hf, D)


def attention(P, D):
    d = P.dve
    for j in range(4):
        at = P.attn
        toks = [P.atok[4 * n + j] for n in range(3)]
        dma(P.sp, D.qz[0:64, 0, :], at[j][0:64, :], D.sem, 0, D.qfree, toks)
        dma(P.sp, D.qz[64:128, 1, :], at[j][64:128, :], D.sem, 0)
        dma(P.sp, D.k[:, :], at[4 + j], D.sem, 0)
        V = D.A.get()
        ld = dma(P.sp, V.t[:, :], at[8 + j], D.sem, 64 * (j + 1), V.free)
        yield
        vt = []
        for c in range(0, 8, 4):
            b = P.ps.get()
            for n in range(4):
                t = tp(P, b.t[:, 128 * n:128 * n + 128], V.t[:, 128 * (c + n):128 * (c + n) + 128], P.ident, ld,
                       P.ctok, b.free, inc=n == 3)
            vt.append(cp(P, D.VT[:, 128 * c:128 * c + 512], b.t[:, :], t, D.qfree))
            P.ps.put(b, vt[-1])
        V.free = [P.pe.last]
        yield
        HO = P.HB[:, 4 + j, 0:1024].rearrange("p (a h x) -> p a h x", a=8, h=2)
        units = [(i, h) for i in range(8) for h in range(2)]
        st, ot = {}, []

        def scores(u):
            i, h = units[u]
            n = 128 * (i + 1)
            A = D.A.get()
            at = []
            for c0 in range(0, n, 512):
                cn = min(512, n - c0)
                b = P.ps.get()
                t = mm(P, b.t[:, 0:cn], D.qz[:, h, 128 * i:128 * i + 128], D.k[:, c0:c0 + cn], True, True, ld, D.ztok,
                       b.free, inc=True)
                t = tt(d, A.t[:, c0:c0 + cn], b.t[:, 0:cn], D.mask[:, (7 - i) * 128 + c0:(7 - i) * 128 + c0 + cn], ADD,
                       t, A.free, D.mtok)
                P.ps.put(b, t)
                at.append(t)
            mx = D.mx[:, 2 * i + h:2 * i + h + 1]
            t = reduce(P, mx, A.t[:, 0:n], MAX, at, D.ofree, negate=True)
            st[u] = A, act(P, A.t[:, 0:n], A.t[:, 0:n], ACT.Exp, t, bias=mx, acc=D.den[:, 2 * i + h:2 * i + h + 1])

        def turn(u):
            i, h = units[u]
            A, ta = st[u]
            PT = D.PT.get()
            ptt = []
            for c0 in range(0, i + 1, 4):
                cn = min(4, i + 1 - c0)
                b = P.ps.get()
                for c in range(cn):
                    tk = tp(P, b.t[:, 128 * c:128 * c + 128], A.t[:, 128 * (c0 + c):128 * (c0 + c) + 128], P.ident, ta,
                            b.free, inc=c == cn - 1)
                ptt.append(cp(P, PT.t[:, 128 * c0:128 * (c0 + cn)], b.t[:, 0:128 * cn], tk, PT.free))
                P.ps.put(b, ptt[-1])
            A.free = [tk]
            st[u] = PT, ptt

        def weigh(u):
            i, h = units[u]
            PT, ptt = st.pop(u)
            b = P.ps.get()
            for c in range(i + 1):
                tk = mm(P, b.t[:, 0:128], PT.t[:, 128 * c:128 * c + 128], D.VT[:, 128 * c:128 * c + 128],
                        c == 0, c == i, ptt, vt, b.free, inc=c == i)
            PT.free = [tk]
            ot.append(cp(P, HO[:, i, h, :], b.t[:, 64 * h:64 * h + 64], tk, D.hfree))
            P.ps.put(b, ot[-1])

        for u in range(len(units) + 2):
            if u < len(units):
                scores(u)
                yield
            if 0 <= u - 1 < len(units):
                turn(u - 1)
            if u >= 2:
                weigh(u - 2)
            yield
        D.qfree = [P.pe.last]
        O = HO.rearrange("p a h x -> p (a h) x")
        A = D.A.get()
        OQ = A.t[:, :].rearrange("p (a x) -> p a x", x=64)
        bc = lambda a: a.unsqueeze(2).broadcast_to([128, 16, 64])
        t = recip(P, D.den[:, :], D.den[:, :], ot)
        t = tt(d, O, O, bc(D.den[:, :]), MUL, t)
        t = tt(d, OQ, O, O, MUL, t, A.free)
        t = reduce(P, D.mx[:, :], OQ, ADD, t)
        A.free = [t]
        t = act(P, D.mx[:, :], D.mx[:, :], ACT.Sqrt, t, bias=P.eps6, scale=1.0 / 64)
        t = recip(P, D.mx[:, :], D.mx[:, :], t)
        t = tt(d, O, O, bc(D.mx[:, :]), MUL, t)
        yield from pause(2 + Q5)
        for c in range(0, 8, 4):
            b = P.ps.get()
            for n in range(4):
                tk = tp(P, b.t[:, 128 * n:128 * n + 128], P.HB[:, 4 + j, 128 * (c + n):128 * (c + n) + 128], P.ident, t,
                        b.free, inc=n == 3)
            P.ytok[4 + j] = ts(d, P.HB[:, 4 + j, 128 * c:128 * c + 512], b.t[:, :], P.vec("attn_g", j), None, MUL, None,
                               tk)
            P.ps.put(b, P.ytok[4 + j])
        D.ofree = [P.pe.last, P.dve.last]
        yield


def shift_mix(P, dst, G, rows, mix, *toks):
    t = tt(P.dve, dst, G.t[0:rows, 0:1024], G.t[0:rows, 1:1025], SUB, *toks)
    return stt(P.dve, dst, dst, mix, G.t[0:rows, 1:1025], MUL, ADD, t)


def block2(P, xtok, free_x, alloc_x):
    nc, d = P.nc, P.dve
    I, HB = P.I, P.HB
    P.ytok, P.rkvtok, P.atok = [None] * 8, [], []
    after = P.everyone()
    WA, GD = HB[0:64, 4, 0:1024], HB[0:96, 5, 0:1024]
    with ExitStack() as cx:
        sb = lambda name, shape, t=F: cx.enter_context(nc.sbuf_tensor(name, shape, t))
        G = Ring([Buf(sb(f"p_G{i}", [128, 1025])) for i in range(2)])
        S = Ring([Buf(sb(f"p_S{i}", [128, 1024])) for i in range(4)])
        rt = Buf(sb("p_rt", [128, 1024]))
        rot = sb("p_rot", [128, 2, 1024])
        rl = dma(P.sp, rot[:, :, :], I["a_rot"], P.newsem("p_rot"), 16, after)
        for b in G.bufs:
            b.free = [mset(P.pool, b.t[:, 0:1], 0.0, after), after]
        for n, b in enumerate(S.bufs):
            b.free, b.sem, b.count = [after], P.newsem(f"p_S{n}"), 0
        rt.free = [after]

        def spill(b, dst, t):
            b.count += 16
            b.free = [dma(P.pool, dst, b.t[:, :], b.sem, b.count, t)]
            return b.free[0]

        g = G.get()
        t = project(P, "wa", g, T2, CH2, xtok, 1)
        t = shift_mix(P, WA, g, 64, P.vec("smix", 12)[0:64, :], t, after, P.h2store)
        g.free = [t]
        wat = [act(P, WA[0:32, :], WA[0:32, :], ACT.Tanh, t), t]
        g = G.get()
        t = project(P, "gd", g, T2, CH2, xtok, 1)
        t = shift_mix(P, GD, g, 96, P.vec("smix", 13)[0:96, :], t, after, P.h2store)
        g.free = [t]
        gdt = act(P, GD, GD, ACT.Sigmoid, t)
        toks = {}
        for j in range(4):
            for n in range(3):
                g, b = G.get(), S.get()
                t = project(P, "rkv", g, T2, CH2, xtok, 1)
                t = shift_mix(P, b.t[:, :], g, 128, P.vec("smix", 4 * n + j), t, b.free)
                g.free = [t]
                toks[4 * n + j] = spill(b, P.rkv[4 * n + j], t)
        P.rkvtok = [toks[i] for i in range(12)]
        for j in range(4):
            for n in range(3):
                b = S.get()
                pt = []

                def ev(c, c0, cn, ps, t):
                    if n == 0:
                        pt.append(act(P, b.t[:, c0:c0 + cn], ps, ACT.Copy, t, b.free, scale=0.125))
                    else:
                        pt.append(cp(P, b.t[:, c0:c0 + cn], ps, t, b.free))
                    return [pt[-1]]

                dense(P, "aqkv", 8, P.XH, P.XL, xtok, CH2, ev)
                t = pt[-1]
                if n < 2:
                    for c0, cn in CH2:
                        bk = P.ps.get()
                        t = mm(P, bk.t[:, 0:cn], P.perm, b.t[:, c0:c0 + cn], True, True, pt, P.ctok, bk.free, inc=True)
                        a = tt(d, rt.t[:, c0:c0 + cn], bk.t[:, 0:cn], rot[:, 1, c0:c0 + cn], MUL, t, rl, rt.free)
                        P.ps.put(bk, a)
                        t = tt(d, b.t[:, c0:c0 + cn], b.t[:, c0:c0 + cn], rot[:, 0, c0:c0 + cn], MUL, a)
                        t = tt(d, b.t[:, c0:c0 + cn], b.t[:, c0:c0 + cn], rt.t[:, c0:c0 + cn], ADD, t)
                    rt.free = [t]
                toks[4 * n + j] = spill(b, P.attn[4 * n + j], t)
        P.atok = [toks[i] for i in range(12)]
        after = P.everyone() + [b.free for b in S.bufs]
    free_x()
    with ExitStack() as cx:
        sb = lambda name, shape, t=F: cx.enter_context(nc.sbuf_tensor(name, shape, t))
        WA2, GD2 = sb("r_WA", [64, 1024]), sb("r_GD", [96, 1024])
        c1 = cp(P, WA2[:, :], WA, wat, after)
        c2 = cp(P, GD2[:, :], GD, gdt, after)
        wl, gl = sb("r_wl", [64, 512]), sb("r_gl", [96, 512])
        reset = sb("r_reset", [128, 512])
        sem = P.newsem("r_ld")
        dma(P.sp, wl[:, :], I["lora_wa"], sem, 0, after)
        lt = dma(P.sp, gl[:, :], I["lora_g"], sem, 32, after)
        t = mset(P.pool, reset[:, :], 1.0, after)
        rtok = mset(P.pool, reset[:, :].rearrange("p (c x) -> p c x", x=64)[:, :, 0:1], 0.0, t)
        gens = []
        for gi in range(2):
            D = Prog()
            D.WA, D.GD, D.wl, D.gl, D.reset, D.rtok = WA2, GD2, wl, gl, reset, rtok
            D.wat, D.gdt = [c1, lt], [c2, lt]
            D.S = {}
            for n, w in (("t0", 1), ("t1", 1), ("t2", 1), ("t3", 1), ("t4", 1), ("bon", 1), ("AR", 2), ("BK", 2),
                         ("GB", 2), ("GK", 2), ("AM", 2), ("Xa", 1)):
                D.S[n] = sb(f"r{gi}_{n}", [128, 512 * w])
            D.S["S0"] = sb(f"r{gi}_S0", [128, 576])
            D.pc, D.in3 = sb(f"r{gi}_pc", [128, 8]), sb(f"r{gi}_in", [128, 3, 512])
            D.sem = P.newsem(f"r{gi}_ld")
            D.free, D.hfree = after, [after, P.h2store]
            gens.append(rwkv_pairs(P, (2 * gi, 2 * gi + 1), D))
        D = Prog()
        D.mask, D.mx, D.den = sb("a_mask", [128, 1024]), sb("a_mx", [128, 16]), sb("a_den", [128, 16])
        D.qz, D.k, D.VT = sb("a_qz", [128, 2, 1024]), sb("a_k", [128, 1024]), sb("a_VT", [128, 1024])
        D.A = Ring([Buf(sb(f"a_A{i}", [128, 1024])) for i in range(2)])
        D.PT = Ring([Buf(sb(f"a_PT{i}", [128, 1024])) for i in range(2)])
        for b in D.A.bufs + D.PT.bufs:
            b.free = [after]
        D.ofree = D.qfree = after
        D.hfree = [after, P.h2store, c1, c2]
        D.sem = P.newsem("a_ld")
        D.mtok = dma(P.sp, D.mask[:, :], I["a_mask"], P.newsem("a_mask"), 16, after)
        z = mset(P.pool, D.qz[64:128, 0, :], 0.0, after, rtok)
        D.ztok = mset(P.pool, D.qz[0:64, 1, :], 0.0, z)
        gens.append(attention(P, D))
        late = gens[1]
        step = 0
        while gens:
            step += 1
            for g in list(gens):
                if g is late and step < LAG:
                    continue
                if next(g, "end") == "end":
                    gens.remove(g)
        P.dbg("rwkv", HB[:, 0:4, 0:1024], P.ytok[0:4])
        P.dbg("attn", HB[:, 4:8, 0:1024], P.ytok[4:8])
        after = P.everyone()
    alloc_x()
    xtok = splits(P, [HB[:, m, 0:T2] for m in range(8)], P.XH, P.XL, CH2, P.ytok, after)
    with ExitStack() as cx:
        sb = lambda name, shape, t=F: cx.enter_context(nc.sbuf_tensor(name, shape, t))
        acc, rs = sb("n4_acc", [128, T2]), sb("n4_rs", [128, T2])
        sq = Ring([Buf(sb(f"n4_sq{i}", [128, T2])) for i in range(2)])
        xr = Ring([Buf(sb(f"n4_x{i}", [128, T2])) for i in range(3)])
        tmp = Ring([Buf(sb(f"n4_t{i}", [128, 512])) for i in range(6)])
        for b in sq.bufs + xr.bufs + tmp.bufs:
            b.free = [after]
        st = Stats(P, acc, sq, T2, CH2, after)
        ht = []
        for m in range(8):
            t2 = []
            x, lt = reload(P, xr, m, T2, P.h2, P.h2store)

            def ev(c, c0, cn, ps, t):
                t2.append(tt(d, HB[:, m, c0:c0 + cn], x.t[:, c0:c0 + cn], ps, ADD, t, lt, xtok[m]))
                return [t2[-1]]

            dense(P, "wout2", 8, P.XH, P.XL, xtok, CH2, ev)
            x.free = [t2[-1]]
            ht.append(t2[-1])
            st.add(HB[:, m, 0:T2], ht[m])
        P.h3store = [dma(P.pool, P.h3[:, k, :], HB[:, k, 0:T2], P.hsem[k], 48, ht[k]) for k in range(8)]
        P.dbg("h3", HB[:, :, 0:T2], ht)
        xfree = P.pe.last
        t = st.finish(rs, 1024, P.eps6)
        out = [{} for _ in range(8)]
        for c, (c0, cn) in enumerate(CH2):
            normalise(P, HB, rs, t, c, c0, cn, "ffn_norm", tmp, out, xfree)
        xtok = out
        after = P.everyone()
    P.hfree = [after, P.h3store]
    with ExitStack() as cx:
        rs = cx.enter_context(nc.sbuf_tensor("n5_rs", [128, T2], F))
        htok, t = ffn(P, ACT.Silu, T2, CH2, xtok, HB, "2", "fconv2", "fcb2", after, rs, (P.h3, P.h3store))
        for m in range(8):
            t = stt(d, HB[:, m, 0:T2], HB[:, m, 0:T2], P.vec("final", m), rs[:, 0:T2], MUL, MUL, t, htok)
            P.outs.append(dma(P.sp, P.out[:, m, :], HB[:, m, 0:T2], P.osem, 16 * (m + 1), t))


def reload(P, xr, m, T, src, ready):
    x = xr.get()
    P.xrcount[m % 3] += 16
    return x, dma(P.pool, x.t[:, 0:T], src[:, m, :], P.xrsem[m % 3], P.xrcount[m % 3], x.free, ready)


def build(nc, I, out, dbg=None):
    with ExitStack() as cx:
        sem_count = [0]

        def newsem(name):
            sem_count[0] += 1
            return (name, cx.enter_context(nc.semaphore(name)))

        sb = lambda name, shape, t=F: cx.enter_context(nc.sbuf_tensor(name, shape, t))
        P = Prog()
        P.nc, P.I, P.out, P.newsem = nc, I, out, newsem
        P.pe, P.act, P.dve, P.pool, P.sp = [Queue(newsem(n)) for n in ("s_pe", "s_act", "s_dve", "s_pool", "s_sp")]
        P.everyone = lambda: everyone(P)
        P.bg, P.rate, P.xfree = [], 1, None
        P.xsem = [newsem(f"s_x{i}") for i in range(8)]
        P.hsem = [newsem(f"s_h{i}") for i in range(8)]
        P.xrsem, P.xrcount = [newsem(f"s_xr{i}") for i in range(3)], [0, 0, 0]
        P.osem, P.outs = newsem("s_out"), []
        P.h1 = nc.dram_tensor("h1", [128, 8, T1], F).ap()
        P.h2 = nc.dram_tensor("h2", [128, 8, T2], F).ap()
        P.h3 = nc.dram_tensor("h3", [128, 8, T2], F).ap()
        P.HB = sb("HB", [128, 8, T1])
        vecs = sb("vecs", [128, NV])
        cst = sb("cst", [128, 1224])
        small = sb("small", [128, 4])
        P.ps = Banks([cx.enter_context(nc.psum_tensor(f"ps{i}", [128, 512], F)) for i in range(8)])
        P.vec = lambda name, i: vecs[:, VCOLS[name][0] + i:VCOLS[name][0] + i + 1]
        csem, vsem = newsem("s_c"), newsem("s_v")
        ct = dma(P.act, cst[:, :], I["cst"], csem, 16)
        P.vtok = dma(P.act, vecs[:, :], I["vecs"], vsem, 16)
        P.ident, P.ones, P.ones64 = cst[:, 0:128], cst[:, 128:256], cst[:, 256:384]
        P.triu_neg, P.perm, P.mtri = cst[:, 384:512], cst[:, 512:640], cst[:, 640:768]
        P.levels = cst[:, 768:1216].rearrange("p (a x) -> p a x", x=64)
        P.mask64, P.mask16 = cst[:, 1216:1218], cst[:, 1218:1220]
        P.sel4 = cst[:, 1220:1224]
        id2 = sb("ident2", [128, 64])
        s4 = sb("sel4", [4, 4, 128])
        P.ident2 = id2
        t = mset(P.pool, small[:, 0:1], 1e-6)
        t2 = mset(P.pool, small[:, 1:2], 64e-5)
        t3 = mset(P.pool, small[:, 2:3], 1.0)
        P.eps6, P.eps64, P.one = small[:, 0:1], small[:, 1:2], small[:, 2:3]
        t4 = vcopy(P.dve, s4[:, :, :], cst[0:4, 1220:1224].unsqueeze(2).broadcast_to([4, 4, 128]), ct)
        P.sel4 = s4
        t5 = tt(P.dve, id2[:, :], P.ident[:, 0:64], P.ident[:, 64:128], ADD, ct)
        P.ctok = [ct, t3, t5]
        plan = []
        for name, src, kt in weight_plan(I):
            if dbg is not None and dbg["_stop"] == 1 and plan and plan[-1][0] == "ffn1d" and name == "wa":
                break
            plan.append((name, src, kt))
        raws = [sb(f"w_raw{i}", [128, 1024]) for i in range(2)]
        his = [sb(f"w_hi{i}", [128, 1024], R) for i in range(3)]
        los = [sb(f"w_lo{i}", [128, 1024], R) for i in range(3)]
        P.w = Weights(P, plan, raws, his, los, [newsem(f"s_w{i}") for i in range(2)])
        for _ in range(2):
            P.w.load()
        P.xscope, xn = None, [0]

        def alloc_x():
            P.xscope = ExitStack()
            xn[0] += 1
            P.XH, P.XL = [P.xscope.enter_context(nc.sbuf_tensor(f"X{part}{xn[0]}", [128, 8, T1], R)) for part in "HL"]

        def free_x():
            P.xscope.close()

        P.mq = [nc.dram_tensor(f"mq{i}", [128, T1], F).ap() for i in range(12)]
        P.mo = [nc.dram_tensor(f"mo{i}", [128, T1], F).ap() for i in range(20)]
        P.rkv = [nc.dram_tensor(f"rkv{i}", [128, T2], F).ap() for i in range(12)]
        P.attn = [nc.dram_tensor(f"attn{i}", [128, T2], F).ap() for i in range(12)]
        alloc_x()

        def dbg_store(name, ap, toks):
            if dbg is not None and name in dbg:
                s = newsem("s_dbg_" + name)
                dma(P.pool, dbg[name], ap, s, 16, *[t for t in toks])
                for q in (P.pool, P.act, P.dve, P.pe):
                    q.wait((s[0], s[1], 16))
                P.pool.do(lambda e: e.memset(small[:, 3:4], 0.0), P.pool.last)

        P.dbg = dbg_store
        stop = dbg.get("_stop") if dbg is not None else None
        xtok = block1(P)
        if stop != 1:
            block2(P, xtok, free_x, alloc_x)
        for t in P.outs + P.h1store + P.h2store + (P.h3store if stop != 1 else []):
            P.sp.wait(t)
        free_x()
        block = cx.enter_context(nc.Block())

        @block.sync
        def _(eng):
            P.sp.play(eng)

        @block.gpsimd
        def _(eng):
            P.pool.play(eng)

        @block.scalar
        def _(eng):
            P.act.play(eng)

        @block.vector
        def _(eng):
            P.dve.play(eng)

        @block.tensor
        def _(eng):
            P.pe.play(eng)


def weight_plan(I):
    for m in range(4):
        yield "u", I["w_u"][m], 8
    for h in range(4):
        yield "v", I["w_qkvo"][8 + h], 8
    for h in range(4):
        yield "o", I["w_qkvo"][12 + h], 8
    for h in range(4):
        yield "q", I["w_qkvo"][h], 8
        yield "k", I["w_qkvo"][4 + h], 8
    gates = [("ga" if m < 8 else "gb", I["w_g"][m], 8) for m in range(16)]
    yield from gates[:NG]
    yield "gates", I["w_gates"][0], 8
    for m in range(4):
        yield "glu", I["w_glu"][m], 4
    yield from gates[NG:]
    for m in range(8):
        yield "wa", I["w_a"][m], 4
        yield "wb", I["w_b"][m], 4
    for m in range(8):
        yield "wout", I["w_out"][m], 8
    yield from ffn_plan(I, "1")
    yield "wa", I["w2_wa"][0], 8
    yield "gd", I["w2_gd"][0], 8
    for j in range(4):
        for n in range(3):
            yield "rkv", I["w2_rkv"][4 * n + j], 8
    for j in range(4):
        for n in range(3):
            yield "aqkv", I["w2_attn"][4 * n + j], 8
    for m in range(8):
        yield "wout2", I["w2_out"][m], 8
    yield from ffn_plan(I, "2")


def ffn_plan(I, tag):
    for f0, nf in FQ:
        for f in range(f0, f0 + nf):
            yield "ffn" + tag + "g", I["f_gate" + tag][f], 8
            yield "ffn" + tag + "u", I["f_up" + tag][f], 8
        for m in range(8):
            yield "ffn" + tag + "d", I["f_down" + tag][m][:, f0 * 128:(f0 + nf) * 128], nf


def constants():
    p = np.arange(128)
    c = np.zeros((128, 1224), np.float32)
    c[:, 0:128] = np.eye(128)
    c[:, 128:256] = 1.0
    c[:, 256:384] = (p[:, None] // 64) == (p[None, :] // 64)
    c[:, 384:512] = np.where(p[:, None] <= p[None, :], 0.0, -1e30)
    perm = np.zeros((128, 128), np.float32)
    for i in range(128):
        r = i % 64
        if r < 8:
            perm[i + 8, i] = -1.0
        elif r < 16:
            perm[i - 8, i] = 1.0
    c[:, 512:640] = perm
    s, t = (p % 64)[:, None], np.arange(64)[None, :]
    c[:, 640:704] = s < t
    c[:, 704:768] = s <= t
    level = lambda b, r, q: ((r // b) % 2 == 1) & ((q // b) == (r // b) - 1)
    c[:, 768:832] = level(1, s, t)
    c[:, 832:896] = level(1, t, s)
    for n, b in enumerate((2, 4, 8, 16, 32)):
        c[:, 896 + 64 * n:960 + 64 * n] = level(b, s, t)
    c[:, 1216], c[:, 1217] = p < 64, p >= 64
    c[:, 1218], c[:, 1219] = (p // 16) % 2 == 0, (p // 16) % 2 == 1
    c[0:4, 1220:1224] = np.eye(4)
    half = 8
    inv = (np.float32(500000.0) ** (-np.arange(half, dtype=np.float32) * np.float32(2.0) / np.float32(16))).astype(np.float32)
    ang = np.arange(1024, dtype=np.float32)[:, None] * inv[None, :]
    rot = np.zeros((128, 2, 1024), np.float32)
    rot[:, 0, :] = 1.0
    for i in range(128):
        if i % 64 < 16:
            rot[i, 0], rot[i, 1] = np.cos(ang[:, i % 8]), np.sin(ang[:, i % 8])
    mask = np.zeros((128, 8, 128), np.float32)
    for b in range(8):
        dist = 128 * (7 - b) + p[:, None] - p[None, :]
        n = ((dist >= 0) & (dist <= 128)).astype(int) + ((dist >= 0) & (dist <= 512) & (dist % 4 == 0)) \
            + ((dist >= 0) & (dist % 16 == 0))
        mask[:, b] = np.where(n > 0, np.log(np.maximum(n, 1)), -1e30)
    return c, rot, mask.reshape(128, 1024)


def layout(i):
    g = {n: np.asarray(a)[0] if np.asarray(a).ndim > 1 and n not in ("meta_tokens",) else np.asarray(a)
         for n, a in i.items()}
    o = {}
    x = np.concatenate([g["meta_tokens"], g["x"]], axis=0)
    cm = lambda a: np.ascontiguousarray(a.T.reshape(8, 128, -1).transpose(1, 0, 2))
    o["x1"] = cm(x)

    def wt(w, n=None):
        k, m = w.shape
        return np.ascontiguousarray(w.reshape(k // 128, 128, m // 128, 128).transpose(2, 1, 0, 3).reshape(m // 128, 128, k))

    def pad(parts):
        out = np.zeros((1024, 128), np.float32)
        for at, a in parts:
            out[:, at:at + a.shape[1]] = a
        return out

    w = g["w_in"]
    o["w_u"] = wt(w[:, 0:512])
    o["w_qkvo"] = wt(w[:, 512:2560])
    o["w_gates"] = wt(pad([(0, w[:, 2560:2564]), (32, w[:, 2564:2568])]))
    o["w_g"] = wt(w[:, 2568:4616])
    o["w_glu"], o["w_a"], o["w_b"] = wt(g["w_ssm_glu"]), wt(g["w_branch_ssm"]), wt(g["w_branch_mlstm"])
    o["w_out"] = wt(g["w_out"])
    o["f_gate1"], o["f_up1"], o["f_down1"] = wt(g["w_ffn_gate"]), wt(g["w_ffn_up"]), wt(g["w_ffn_down"])
    w = g["w_in_2"]
    o["w2_rkv"] = wt(w[:, 0:1536])
    o["w2_wa"] = wt(pad([(0, w[:, 1536:1600])]))
    o["w2_gd"] = wt(pad([(0, w[:, 1600:1696])]))
    o["w2_attn"] = wt(w[:, 1696:3232])
    o["w2_out"] = wt(g["w_out_2"])
    o["f_gate2"], o["f_up2"] = wt(g["w_ffn_up_2"][:, 0:2816]), wt(g["w_ffn_up_2"][:, 2816:5632])
    o["f_down2"] = wt(g["w_ffn_down_2"])
    o["lora_wa"] = np.concatenate([g["w_lora_up_2"], g["a_lora_up_2"]], axis=0)
    o["lora_g"] = np.ascontiguousarray(g["g_lora_up_2"])
    v = np.zeros((128, NV), np.float32)

    def put(name, a, off=0):
        a = np.asarray(a).reshape(-1)
        n = a.shape[0] // 128
        at = VCOLS[name][0] + off
        v[:, at:at + n] = a.reshape(n, 128).T

    for name, src in (("g_mix_pre", "g_mix_pre"), ("g_mix_post", "g_mix_post"), ("bqk", "b_qk_conv"),
                      ("g_head", "g_head_norm"), ("ssm_d", "ssm_d"), ("g_ffn_pre", "g_ffn_pre"),
                      ("g_ffn_post", "g_ffn_post"), ("fcb", "b_ffn_conv"), ("mix_norm", "mix_norm_gain_2"),
                      ("w0", "w0_2"), ("a0", "a0_2"), ("k_k", "k_k_2"), ("k_a", "k_a_2"), ("r_k", "r_k_2"),
                      ("ln_w", "ln_x_w_2"), ("ln_b", "ln_x_b_2"), ("attn_g", "attn_norm_gain_2"),
                      ("ffn_norm", "ffn_norm_gain_2"), ("fcb2", "ffn_conv_b_2"), ("final", "final_norm_gain_2")):
        put(name, g[src])
    put("wqk", g["w_qk_conv"].reshape(4, 8, 128).transpose(1, 0, 2))
    put("fconv", g["w_ffn_conv"].reshape(3, 22, 128).transpose(1, 0, 2))
    put("fconv2", g["ffn_conv_w_2"].reshape(3, 22, 128).transpose(1, 0, 2))
    at = VCOLS["bgate"][0]
    v[0:4, at], v[32:36, at] = g["b_gates"][0:4], g["b_gates"][4:8]
    sm = g["rwkv_shift_mix_2"]
    put("smix", sm[0:1536])
    at = VCOLS["smix"][0]
    v[0:64, at + 12], v[0:96, at + 13] = sm[1536:1600], sm[1600:1696]
    o["vecs"] = v
    lr, li, ld = g["ssm_lambda_re"], g["ssm_lambda_im"], g["ssm_log_dt"]
    bre, bim, cre, cim = g["ssm_b_re"], g["ssm_b_im"], g["ssm_c_re"], g["ssm_c_im"]
    ldt = np.repeat(ld[:, None], 64, axis=1)
    one = lambda a: a.reshape(16, 2, 64).transpose(1, 2, 0).reshape(128, 16)
    o["ssm_p1"] = np.stack([one(lr), one(li), one(ldt)], axis=1)
    o1 = lambda a: a.reshape(16, 2, 64, 16).transpose(1, 2, 0, 3).reshape(128, 16, 16)
    o["ssm_bc1"] = np.stack([o1(bre), o1(bim), o1(cre.transpose(0, 2, 1)), o1(cim.transpose(0, 2, 1))], axis=1)
    rep = lambda a: np.repeat(a.reshape(4, 8, 1, 64), 16, axis=2).transpose(1, 2, 0, 3).reshape(128, 256)
    o2 = lambda a: a.transpose(0, 2, 1).reshape(4, 8, 16, 64).transpose(1, 2, 0, 3).reshape(128, 256)
    o["ssm_p2"] = np.stack([rep(lr), rep(li), rep(ldt), o2(bre), o2(bim)], axis=1)
    o["cst"], o["a_rot"], o["a_mask"] = constants()
    return {n: np.ascontiguousarray(a) for n, a in o.items()}


def kernel(**inputs):
    import concourse.bacc as _bacc
    from concourse.bass_utils import run_bass_kernel_spmd as _run

    nc = _bacc.Bacc("TRN2", target_bir_lowering=False, num_devices=1)
    arrays = {"in_" + n: a for n, a in layout(inputs).items()}
    I = {n[3:]: nc.dram_tensor(n, a.shape, mybir.dt.from_np(a.dtype), kind="ExternalInput").ap()
         for n, a in arrays.items()}
    out = nc.dram_tensor("out", (128, 8, 1024), F, kind="ExternalOutput").ap()
    build(nc, I, out)
    r = _run(nc, [arrays], core_ids=[0])
    y = r.results[0]["out"]
    return np.ascontiguousarray(y.transpose(2, 1, 0).reshape(1, 1024, 1024))
```
